# Optimizing a Trainium2 kernel written in Bass

```python
import math
import jax, jax.numpy as jnp
from jax import lax
import numpy as np

'''One inference step (prompt group + sample group, shared weights) of a 2-layer
hybrid decoder: layer 0 = native sparse attention (compressed / selected / sliding
window branches, gated), layer 1 = S5-style grouped complex-diagonal SSM + GLU.
Every layer: sandwich RMSNorm around the mixer and around a squared-ReLU MLP.

Inputs: x_prompt (BATCH, SEQ, D_MODEL), x_sample (DEC_BATCH, DEC_SEQ, D_MODEL),
 cache_kv_cmp, cache_kv_sel (N_NSA_LAYERS, N_POOL, PAGE_SIZE, 2, N_KV_HEADS, HEAD_DIM) paged raw K/V rows,
 cache_kv_win (N_NSA_LAYERS, DEC_BATCH, WINDOW, 2, N_KV_HEADS, HEAD_DIM) window buffer,
 state_ssm (N_SSM_LAYERS, DEC_BATCH, 2, SSM_GROUPS, SSM_STATE) [re, im] of the S5 state,
 page_table (DEC_BATCH, PAST_LEN // PAGE_SIZE) int32, then weights.
Output tuple:
 y_prompt (BATCH, SEQ, D_MODEL), y_sample (DEC_BATCH, DEC_SEQ, D_MODEL),
 kv_cmp_prompt (N_NSA_LAYERS, BATCH, SEQ, 2, N_KV_HEADS, HEAD_DIM),
 kv_cmp_sample (N_NSA_LAYERS, DEC_BATCH, DEC_SEQ, 2, N_KV_HEADS, HEAD_DIM),
 kv_sel_prompt (N_NSA_LAYERS, BATCH, SEQ, 2, N_KV_HEADS, HEAD_DIM),
 kv_sel_sample (N_NSA_LAYERS, DEC_BATCH, DEC_SEQ, 2, N_KV_HEADS, HEAD_DIM),
 kv_win_prompt (N_NSA_LAYERS, BATCH, WINDOW, 2, N_KV_HEADS, HEAD_DIM),
 kv_win_sample (N_NSA_LAYERS, DEC_BATCH, WINDOW, 2, N_KV_HEADS, HEAD_DIM),
 ssm_prompt (N_SSM_LAYERS, BATCH, 2, SSM_GROUPS, SSM_STATE),
 ssm_sample (N_SSM_LAYERS, DEC_BATCH, 2, SSM_GROUPS, SSM_STATE).
'''

D_MODEL = 1024
BATCH = 1
SEQ = 512
DEPTH = 2
DEC_BATCH = 8
DEC_SEQ = 1
PAST_LEN = 1024
PAGE_SIZE = 128

N_MIXERS = 2
N_NSA_LAYERS = (DEPTH + 1) // 2
N_SSM_LAYERS = DEPTH // 2
N_HEADS = 16
HEAD_DIM = 64
N_KV_HEADS = 4
GROUP = N_HEADS // N_KV_HEADS
CMP_BLOCK = 32
CMP_STRIDE = 16
CMP_RATIO = CMP_BLOCK // CMP_STRIDE
SEL_BLOCK = 64
TOP_N = 16
WINDOW = 512
Q_CHUNK = 64
ROPE_THETA = 10000.0
Q_W = N_HEADS * HEAD_DIM
KV_W = N_KV_HEADS * HEAD_DIM
IN_W = Q_W + 6 * KV_W + 3 * N_HEADS
SSM_GROUP = 16
SSM_GROUPS = D_MODEL // SSM_GROUP
SSM_STATE = 64
D_FF = 4 * D_MODEL
EPS = 1e-6
NEG = -1e30
FORCE = 1e9

kernel_name = 'nsa_s5_hybrid_decoder_step'

def rms_norm(x, g):
    xf = x.astype(jnp.float32)
    y = xf * lax.rsqrt(jnp.mean(xf * xf, axis=-1, keepdims=True) + EPS)
    return (y * g.astype(jnp.float32)).astype(x.dtype)

def rope(x, pos):
    half = HEAD_DIM // 2
    inv = ROPE_THETA ** (-jnp.arange(half, dtype=jnp.float32) / half)
    ang = pos.astype(jnp.float32)[:, None] * inv[None, :]
    cos = jnp.cos(ang)[None, :, None, :]
    sin = jnp.sin(ang)[None, :, None, :]
    xf = x.astype(jnp.float32)
    x1, x2 = xf[..., :half], xf[..., half:]
    return jnp.concatenate([x1 * cos - x2 * sin, x2 * cos + x1 * sin], axis=-1).astype(x.dtype)

def masked_softmax(s, mask):
    s = jnp.where(mask, s.astype(jnp.float32), NEG)
    m = jnp.max(s, axis=-1, keepdims=True)
    e = jnp.where(mask, jnp.exp(s - m), 0.0)
    return e / jnp.maximum(jnp.sum(e, axis=-1, keepdims=True), 1e-20)

def compress(raw, w1, w2, pe):
    b, l = raw.shape[0], raw.shape[1]
    n_sb = l // CMP_STRIDE
    nc = n_sb - CMP_RATIO + 1
    sb = raw[:, :n_sb * CMP_STRIDE].reshape(b, n_sb, CMP_STRIDE, N_KV_HEADS, HEAD_DIM)
    w1r = w1.reshape(CMP_RATIO, CMP_STRIDE, HEAD_DIM, HEAD_DIM)
    per = pe.reshape(CMP_RATIO, CMP_STRIDE, HEAD_DIM)
    parts = []
    for r in range(CMP_RATIO):
        pr = jnp.einsum('bnskd,sde->bnke', sb + per[r][None, None, :, None, :], w1r[r])
        parts.append(pr[:, r:r + nc])
    h = sum(parts[1:], parts[0])
    return jnp.einsum('bnke,ef->bnkf', jax.nn.gelu(h), w2)

def nsa_attend(q, q_rot, gates, q_pos, kc, vc, kblk, vblk, kw, vw, kw_pos):
    b, tq = q.shape[0], q.shape[1]
    scale = HEAD_DIM ** -0.5
    qg = q.reshape(b, tq, N_KV_HEADS, GROUP, HEAD_DIM)
    qrg = q_rot.reshape(b, tq, N_KV_HEADS, GROUP, HEAD_DIM)
    nc = kc.shape[1]
    c_start = jnp.arange(nc, dtype=jnp.int32) * CMP_STRIDE
    mask_c = (c_start + CMP_BLOCK - 1)[None, :] <= q_pos[:, None]
    s_c = jnp.einsum('bqkgd,bckd->bkgqc', qg, kc) * scale
    p_c = masked_softmax(s_c, mask_c)
    o_c = jnp.einsum('bkgqc,bckd->bqkgd', p_c.astype(vc.dtype), vc)
    nsel = kblk.shape[1]
    blk = jnp.arange(nsel, dtype=jnp.int32)
    s_start = blk * SEL_BLOCK
    overlap = ((c_start[:, None] < s_start[None, :] + SEL_BLOCK)
               & (c_start[:, None] + CMP_BLOCK > s_start[None, :])).astype(jnp.float32)
    imp = jnp.einsum('bkgqc,cs->bkqs', p_c, overlap)
    cur = q_pos // SEL_BLOCK
    forced = (blk[None, :] == 0) | (blk[None, :] == cur[:, None]) | (blk[None, :] == cur[:, None] - 1)
    causal = s_start[None, :] <= q_pos[:, None]
    imp = jnp.where(forced, FORCE, jnp.where(causal, imp, NEG))
    n_top = min(TOP_N, nsel)
    _, top = lax.top_k(imp, n_top)
    gather = jax.vmap(jax.vmap(lambda blocks, idx: blocks[idx]))
    k_sel = gather(jnp.moveaxis(kblk, 3, 1), top)
    v_sel = gather(jnp.moveaxis(vblk, 3, 1), top)
    k_pos = top[..., None] * SEL_BLOCK + jnp.arange(SEL_BLOCK, dtype=jnp.int32)
    mask_s = (k_pos <= q_pos[None, None, :, None, None]).reshape(b, N_KV_HEADS, 1, tq, n_top * SEL_BLOCK)
    s_s = jnp.einsum('bqkgd,bkqnpd->bkgqnp', qrg, k_sel) * scale
    p_s = masked_softmax(s_s.reshape(b, N_KV_HEADS, GROUP, tq, n_top * SEL_BLOCK), mask_s)
    o_s = jnp.einsum('bkgqm,bkqmd->bqkgd', p_s.astype(vblk.dtype),
                     v_sel.reshape(b, N_KV_HEADS, tq, n_top * SEL_BLOCK, HEAD_DIM))
    dist = q_pos[:, None] - kw_pos[None, :]
    mask_w = (dist >= 0) & (dist <= WINDOW) & (kw_pos[None, :] >= 0)
    s_w = jnp.einsum('bqkgd,blkd->bkgql', qrg, kw) * scale
    p_w = masked_softmax(s_w, mask_w)
    o_w = jnp.einsum('bkgql,blkd->bqkgd', p_w.astype(vw.dtype), vw)
    gk = gates.reshape(b, tq, N_KV_HEADS, GROUP, 3)[..., None]
    o = gk[..., 0, :] * o_c + gk[..., 1, :] * o_s + gk[..., 2, :] * o_w
    return o.reshape(b, tq, N_HEADS, HEAD_DIM)

def nsa_project(xn, w_in, pos):
    b, t = xn.shape[0], xn.shape[1]
    proj = jnp.einsum('btd,de->bte', xn, w_in)
    q = proj[..., :Q_W].reshape(b, t, N_HEADS, HEAD_DIM)
    kv = proj[..., Q_W:Q_W + 6 * KV_W].reshape(b, t, 6, N_KV_HEADS, HEAD_DIM)
    gates = jax.nn.sigmoid(proj[..., Q_W + 6 * KV_W:].astype(jnp.float32)).astype(xn.dtype)
    gates = gates.reshape(b, t, N_HEADS, 3)
    return (q, rope(q, pos), gates, kv[:, :, 0], kv[:, :, 1], rope(kv[:, :, 2], pos), kv[:, :, 3],
            rope(kv[:, :, 4], pos), kv[:, :, 5])

def nsa_prompt(xn, w_in, w_o, cmp_w1, cmp_w2, cmp_pe):
    b, t = xn.shape[0], xn.shape[1]
    pos = jnp.arange(t, dtype=jnp.int32)
    q, q_rot, gates, k_c, v_c, k_s, v_s, k_w, v_w = nsa_project(xn, w_in, pos)
    kc = compress(k_c, cmp_w1[0], cmp_w2[0], cmp_pe[0])
    vc = compress(v_c, cmp_w1[1], cmp_w2[1], cmp_pe[1])
    nsel = t // SEL_BLOCK
    kblk = k_s.reshape(b, nsel, SEL_BLOCK, N_KV_HEADS, HEAD_DIM)
    vblk = v_s.reshape(b, nsel, SEL_BLOCK, N_KV_HEADS, HEAD_DIM)
    pad = ((0, 0), (WINDOW, 0), (0, 0), (0, 0))
    kwp = jnp.pad(k_w, pad)
    vwp = jnp.pad(v_w, pad)
    n_chunks = t // Q_CHUNK

    def to_chunks(a):
        return jnp.moveaxis(a.reshape((b, n_chunks, Q_CHUNK) + a.shape[2:]), 1, 0)

    starts = jnp.arange(n_chunks, dtype=jnp.int32) * Q_CHUNK

    def chunk_fn(args):
        qc, qrc, gc, start = args
        q_pos = start + jnp.arange(Q_CHUNK, dtype=jnp.int32)
        kw = lax.dynamic_slice_in_dim(kwp, start, Q_CHUNK + WINDOW, axis=1)
        vw = lax.dynamic_slice_in_dim(vwp, start, Q_CHUNK + WINDOW, axis=1)
        kw_pos = start - WINDOW + jnp.arange(Q_CHUNK + WINDOW, dtype=jnp.int32)
        return nsa_attend(qc, qrc, gc, q_pos, kc, vc, kblk, vblk, kw, vw, kw_pos)

    o = lax.map(chunk_fn, (to_chunks(q), to_chunks(q_rot), to_chunks(gates), starts))
    o = jnp.moveaxis(o, 0, 1).reshape(b, t, Q_W)
    y = jnp.einsum('bte,ed->btd', o, w_o)
    kv_cmp = jnp.stack([k_c, v_c], axis=2)
    kv_sel = jnp.stack([k_s, v_s], axis=2)
    kv_win = jnp.stack([kwp[:, -WINDOW:], vwp[:, -WINDOW:]], axis=2)
    return y, kv_cmp, kv_sel, kv_win

def nsa_sample(xn, kv_cmp_pages, kv_sel_pages, kv_win_buf, page_table, w_in, w_o, cmp_w1, cmp_w2, cmp_pe):
    b, t = xn.shape[0], xn.shape[1]
    past = page_table.shape[1] * PAGE_SIZE
    pos = past + jnp.arange(t, dtype=jnp.int32)
    q, q_rot, gates, k_c, v_c, k_s, v_s, k_w, v_w = nsa_project(xn, w_in, pos)

    def gather_past(pages):
        return pages[page_table].reshape(b, past, 2, N_KV_HEADS, HEAD_DIM)

    cmp_new = jnp.stack([k_c, v_c], axis=2)
    cmp_all = jnp.concatenate([gather_past(kv_cmp_pages), cmp_new], axis=1)
    kc = compress(cmp_all[:, :, 0], cmp_w1[0], cmp_w2[0], cmp_pe[0])
    vc = compress(cmp_all[:, :, 1], cmp_w1[1], cmp_w2[1], cmp_pe[1])
    sel_new = jnp.stack([k_s, v_s], axis=2)
    sel_all = jnp.concatenate([gather_past(kv_sel_pages), sel_new], axis=1)
    l = past + t
    nsel = -(-l // SEL_BLOCK)
    sel_all = jnp.pad(sel_all, ((0, 0), (0, nsel * SEL_BLOCK - l), (0, 0), (0, 0), (0, 0)))
    sel_blk = sel_all.reshape(b, nsel, SEL_BLOCK, 2, N_KV_HEADS, HEAD_DIM)
    win_all = jnp.concatenate([kv_win_buf, jnp.stack([k_w, v_w], axis=2)], axis=1)
    kw_pos = past - WINDOW + jnp.arange(WINDOW + t, dtype=jnp.int32)
    o = nsa_attend(q, q_rot, gates, pos, kc, vc, sel_blk[:, :, :, 0], sel_blk[:, :, :, 1],
                   win_all[:, :, 0], win_all[:, :, 1], kw_pos)
    y = jnp.einsum('bte,ed->btd', o.reshape(b, t, Q_W), w_o)
    return y, cmp_new, sel_new, win_all[:, -WINDOW:]

def s5_mix(xn, h0, a_re, a_im, log_dt, b_re, b_im, c_re, c_im, d_skip, w_glu, b_glu):
    b, t = xn.shape[0], xn.shape[1]
    f32 = jnp.float32
    u = xn.astype(f32).reshape(b, t, SSM_GROUPS, SSM_GROUP)
    a = lax.complex(a_re.astype(f32), a_im.astype(f32))
    dt = jnp.exp(log_dt.astype(f32))[:, None]
    a_bar = jnp.exp(a * dt)
    b_bar = ((a_bar - 1.0) / a)[:, :, None] * lax.complex(b_re.astype(f32), b_im.astype(f32))
    c = lax.complex(c_re.astype(f32), c_im.astype(f32))
    bu = jnp.einsum('gnc,btgc->btgn', b_bar, u.astype(jnp.complex64))
    h_init = lax.complex(h0[:, 0].astype(f32), h0[:, 1].astype(f32))
    bu = bu.at[:, 0].add(a_bar[None] * h_init)
    a_seq = jnp.broadcast_to(a_bar, (1, t) + a_bar.shape)

    def combine(left, right):
        a_l, b_l = left
        a_r, b_r = right
        return a_r * a_l, a_r * b_l + b_r

    _, h = lax.associative_scan(combine, (a_seq, bu), axis=1)
    y = jnp.real(jnp.einsum('gcn,btgn->btgc', c, h)) + d_skip.astype(f32).reshape(SSM_GROUPS, SSM_GROUP) * u
    y = jax.nn.gelu(y.reshape(b, t, D_MODEL))
    out = y * jax.nn.sigmoid(y @ w_glu.astype(f32) + b_glu.astype(f32))
    h_last = h[:, -1]
    state = jnp.stack([jnp.real(h_last), jnp.imag(h_last)], axis=1)
    return out.astype(xn.dtype), state

def sq_relu_mlp(x, w1, w2):
    h = jax.nn.relu(x @ w1)
    return (h * h) @ w2

def setup_inputs(seed: int = 0) -> dict:
    key = jax.random.key(seed)
    ks = jax.random.split(key, 32)
    f32 = jnp.float32
    n_pages = PAST_LEN // PAGE_SIZE
    n_used = DEC_BATCH * n_pages
    n_pool = (5 * n_used + 3) // 4

    def nrm(k, shape, s):
        return jax.random.normal(k, shape, f32) * s

    kv_page_shape = (N_NSA_LAYERS, n_pool, PAGE_SIZE, 2, N_KV_HEADS, HEAD_DIM)
    ssm_shape = (N_SSM_LAYERS, SSM_GROUPS, SSM_STATE)
    return {
        'x_prompt': nrm(ks[0], (BATCH, SEQ, D_MODEL), 1.0),
        'x_sample': nrm(ks[1], (DEC_BATCH, DEC_SEQ, D_MODEL), 1.0),
        'cache_kv_cmp': nrm(ks[2], kv_page_shape, 1.0),
        'cache_kv_sel': nrm(ks[3], kv_page_shape, 1.0),
        'cache_kv_win': nrm(ks[4], (N_NSA_LAYERS, DEC_BATCH, WINDOW, 2, N_KV_HEADS, HEAD_DIM), 1.0),
        'state_ssm': nrm(ks[5], (N_SSM_LAYERS, DEC_BATCH, 2, SSM_GROUPS, SSM_STATE), 0.1),
        'page_table': jax.random.permutation(ks[6], n_pool)[:n_used].reshape(DEC_BATCH, n_pages).astype(jnp.int32),
        'norm_g': 1.0 + nrm(ks[7], (DEPTH, 4, D_MODEL), 0.02),
        'mlp_w1': nrm(ks[8], (DEPTH, D_MODEL, D_FF), D_MODEL ** -0.5),
        'mlp_w2': nrm(ks[9], (DEPTH, D_FF, D_MODEL), D_FF ** -0.5),
        'nsa_w_in': nrm(ks[10], (N_NSA_LAYERS, D_MODEL, IN_W), D_MODEL ** -0.5),
        'nsa_w_o': nrm(ks[11], (N_NSA_LAYERS, Q_W, D_MODEL), Q_W ** -0.5),
        'nsa_cmp_w1': nrm(ks[12], (N_NSA_LAYERS, 2, CMP_BLOCK * HEAD_DIM, HEAD_DIM), (CMP_BLOCK * HEAD_DIM) ** -0.5),
        'nsa_cmp_w2': nrm(ks[13], (N_NSA_LAYERS, 2, HEAD_DIM, HEAD_DIM), HEAD_DIM ** -0.5),
        'nsa_cmp_pe': nrm(ks[14], (N_NSA_LAYERS, 2, CMP_BLOCK, HEAD_DIM), 0.1),
        's5_a_re': -0.5 + nrm(ks[15], ssm_shape, 0.01),
        's5_a_im': math.pi * jnp.arange(SSM_STATE, dtype=f32) + nrm(ks[16], ssm_shape, 0.01),
        's5_log_dt': jax.random.uniform(ks[17], (N_SSM_LAYERS, SSM_GROUPS), f32, math.log(1e-3), math.log(1e-1)),
        's5_b_re': nrm(ks[18], (N_SSM_LAYERS, SSM_GROUPS, SSM_STATE, SSM_GROUP), (2 * SSM_GROUP) ** -0.5),
        's5_b_im': nrm(ks[19], (N_SSM_LAYERS, SSM_GROUPS, SSM_STATE, SSM_GROUP), (2 * SSM_GROUP) ** -0.5),
        's5_c_re': nrm(ks[20], (N_SSM_LAYERS, SSM_GROUPS, SSM_GROUP, SSM_STATE), 0.5),
        's5_c_im': nrm(ks[21], (N_SSM_LAYERS, SSM_GROUPS, SSM_GROUP, SSM_STATE), 0.5),
        's5_d': nrm(ks[22], (N_SSM_LAYERS, D_MODEL), 1.0),
        's5_w_glu': nrm(ks[23], (N_SSM_LAYERS, D_MODEL, D_MODEL), D_MODEL ** -0.5),
        's5_b_glu': nrm(ks[24], (N_SSM_LAYERS, D_MODEL), 0.01),
    }

def reference(x_prompt, x_sample, cache_kv_cmp, cache_kv_sel, cache_kv_win, state_ssm, page_table,
              norm_g, mlp_w1, mlp_w2, nsa_w_in, nsa_w_o, nsa_cmp_w1, nsa_cmp_w2, nsa_cmp_pe,
              s5_a_re, s5_a_im, s5_log_dt, s5_b_re, s5_b_im, s5_c_re, s5_c_im, s5_d, s5_w_glu, s5_b_glu):
    hp, hs = x_prompt, x_sample
    cmp_p, cmp_s, sel_p, sel_s, win_p, win_s, ssm_p, ssm_s = [], [], [], [], [], [], [], []
    for i in range(DEPTH):
        li = i // N_MIXERS
        g = norm_g[i]
        xp, xs = rms_norm(hp, g[0]), rms_norm(hs, g[0])
        if i % N_MIXERS == 0:
            yp, kc_p, ks_p, kw_p = nsa_prompt(xp, nsa_w_in[li], nsa_w_o[li], nsa_cmp_w1[li], nsa_cmp_w2[li], nsa_cmp_pe[li])
            ys, kc_s, ks_s, kw_s = nsa_sample(xs, cache_kv_cmp[li], cache_kv_sel[li], cache_kv_win[li], page_table,
                                              nsa_w_in[li], nsa_w_o[li], nsa_cmp_w1[li], nsa_cmp_w2[li], nsa_cmp_pe[li])
            cmp_p.append(kc_p)
            cmp_s.append(kc_s)
            sel_p.append(ks_p)
            sel_s.append(ks_s)
            win_p.append(kw_p)
            win_s.append(kw_s)
        else:
            h0p = jnp.zeros((hp.shape[0], 2, SSM_GROUPS, SSM_STATE), jnp.float32)
            yp, st_p = s5_mix(xp, h0p, s5_a_re[li], s5_a_im[li], s5_log_dt[li], s5_b_re[li], s5_b_im[li],
                              s5_c_re[li], s5_c_im[li], s5_d[li], s5_w_glu[li], s5_b_glu[li])
            ys, st_s = s5_mix(xs, state_ssm[li], s5_a_re[li], s5_a_im[li], s5_log_dt[li], s5_b_re[li], s5_b_im[li],
                              s5_c_re[li], s5_c_im[li], s5_d[li], s5_w_glu[li], s5_b_glu[li])
            ssm_p.append(st_p)
            ssm_s.append(st_s)
        hp = hp + rms_norm(yp, g[1])
        hs = hs + rms_norm(ys, g[1])
        hp = hp + rms_norm(sq_relu_mlp(rms_norm(hp, g[2]), mlp_w1[i], mlp_w2[i]), g[3])
        hs = hs + rms_norm(sq_relu_mlp(rms_norm(hs, g[2]), mlp_w1[i], mlp_w2[i]), g[3])
    return (hp, hs, jnp.stack(cmp_p), jnp.stack(cmp_s), jnp.stack(sel_p), jnp.stack(sel_s),
            jnp.stack(win_p), jnp.stack(win_s), jnp.stack(ssm_p), jnp.stack(ssm_s))


_drawn_inputs = setup_inputs


def setup_inputs(seed=0):
    import zlib

    import numpy as np

    out = dict(_drawn_inputs(seed))
    spreads = {}
    factors = {'s5_a_re': 11.87, 's5_b_glu': 26.266}
    for name, (base, spread) in spreads.items():
        noise = np.random.default_rng([zlib.crc32(name.encode()), seed]).standard_normal(out[name].shape)
        drawn = base * np.exp(spread * noise) if base else spread * noise
        out[name] = __import__('jax').numpy.asarray(drawn.astype(out[name].dtype))
    for name, factor in factors.items():
        out[name] = (out[name] * factor).astype(out[name].dtype)
    return out
```

```python
from contextlib import ExitStack, contextmanager

import numpy as np

import concourse.bass as bass
from concourse import mybir

F32 = mybir.dt.float32
I32 = mybir.dt.int32
ACT = mybir.ActivationFunctionType
ALU = mybir.AluOpType
AX = mybir.AxisListType

P = 128
D = 1024
SEQ = 512
NB = 8
T = SEQ + NB
HALF = T // 2
KD = D // P
QT = SEQ // P
DFF = 4 * D
KF = DFF // P
NH, HD, NKV, GRP = 16, 64, 4, 4
KVW = NKV * HD
ROW = 2 * KVW
PAST, PAGE = 1024, 128
NPAGE = PAST // PAGE
POOL_PAGES = (5 * NB * NPAGE + 3) // 4
WIN = 512
STRIDE = 16
NSUB = PAST // STRIDE
NCS = NSUB - 1
NSUBP = SEQ // STRIDE
NCP = NSUBP - 1
SELB = 64
NSEL = PAST // SELB + 1
SPAIR = STRIDE // 2
SCALE = HD ** -0.5
EPS = 1e-6
BIG = 1e30
G, CH, NS = 64, 16, 64
GP = G // 2
L = 8
NCH = SEQ // L
SUP = 8


def constants():
    half = HD // 2
    inv = (np.float32(10000.0) ** (-np.arange(half, dtype=np.float32) / np.float32(half))).astype(np.float32)
    pos = np.concatenate([np.arange(SEQ), np.full(NB, PAST)]).astype(np.float32)
    ang = pos[:, None] * inv[None, :]
    cos, sin = np.cos(ang).astype(np.float32), np.sin(ang).astype(np.float32)
    rows = np.zeros((P, QT + 1, 2, half), np.float32)
    for t in range(QT + 1):
        n = P if t < QT else NB
        rows[:n, t, 0], rows[:n, t, 1] = cos[t * P:t * P + n], sin[t * P:t * P + n]
    cos_t = np.tile(cos.T, (4, 1))
    sin_t = np.tile(np.concatenate([-sin.T, sin.T]), (2, 1))
    swap = np.zeros((P, P), np.float32)
    for m in range(P):
        swap[m // HD * HD + (m % HD + half) % HD, m] = 1.0
    q = np.arange(P)
    causal = np.where(np.arange(SEQ)[None, :] - (SEQ - P) > q[:, None], BIG, 0.0).astype(np.float32)
    qpos = (np.arange(QT)[None, :] * P + q[:, None])[:, None, :, None]
    cend = (np.arange(NCP) * STRIDE + 2 * STRIDE - 1)[None, None, None, :]
    seen = np.broadcast_to(cend <= qpos, (P, GRP, QT, NCP))
    cmask = np.stack([np.where(seen, 0.0, BIG), seen.astype(np.float32)], 1).astype(np.float32)
    row_b = np.arange(P) // NH
    own = np.where(row_b[:, None] == np.arange(NB)[None, :], 0.0, BIG).astype(np.float32)
    group = (np.arange(P)[:, None] // GRP == np.arange(P)[None, :] // GRP).astype(np.float32)
    c0, s0 = np.arange(NCS) * STRIDE, np.arange(NSEL) * SELB
    over = np.zeros((P, NSEL), np.float32)
    over[:NCS] = (c0[:, None] < s0[None] + SELB) & (c0[:, None] + 2 * STRIDE > s0[None])
    blk = np.broadcast_to(np.arange(NSEL, dtype=np.float32), (P, NSEL))
    sign = np.where(np.arange(P) < NS, 1.0, -1.0).astype(np.float32)[:, None]
    return {
        "c_ident": np.eye(P, dtype=np.float32), "c_swap": swap, "c_ropeT": np.stack([cos_t, sin_t], 1),
        "c_rope": rows, "c_causal": causal, "c_cmask": cmask.reshape(P, -1), "c_own": own,
        "c_group": group, "c_over": over, "c_blk": np.ascontiguousarray(blk), "c_sign": sign,
    }


class Core:

    def __init__(self, nc, ctx, dram):
        self.nc, self.ctx, self.dram = nc, ctx, dram
        self.psum = ctx.enter_context(nc.psum_tensor("psum", [P, 8, 512], F32))

    def buf(self, name, shape, dt=F32, ctx=None):
        return (ctx or self.ctx).enter_context(self.nc.sbuf_tensor(name, shape, dt))

    def sem(self, name):
        self.sems.append(self.nc.alloc_semaphore(name=name))
        return self.sems[-1]

    @contextmanager
    def part(self):
        self.sems = []
        yield
        self.nc.clear_and_free_semaphores(self.sems)
        self.nc.all_engine_barrier()


def rows_of(t):
    return P if t < QT else NB


def stage_inputs(c):
    nc, ps = c.nc, c.psum
    loaded, x_in = c.sem("const_loaded"), [c.sem(f"x_in{t}") for t in range(QT + 1)]
    turned, kept = c.sem("x_turned"), c.sem("x_kept")
    preset = c.sem("x_preset")
    with ExitStack() as mine:
        xr = c.buf("x_rows", [P, QT + 1, D], ctx=mine)
        with nc.Block() as block:
            @block.sync
            def _(sp):
                sp.dma_start(c.ident[:], c.dram["c_ident"]).then_inc(loaded, 16)
                for t in range(QT):
                    sp.dma_start(xr[:, t, :], c.dram["x_prompt"][0, t * P:(t + 1) * P, :]).then_inc(x_in[t], 16)
                sp.dma_start(xr[0:NB, QT, :], c.dram["x_sample"][:, 0, :]).then_inc(x_in[QT], 16)
                for b, name in ((c.causal[:], "c_causal"), (c.cmask[:], "c_cmask"), (c.own[:], "c_own"),
                                (c.group[:], "c_group"), (c.over[:], "c_over"), (c.blk[:], "c_blk"),
                                (c.sign[:], "c_sign")):
                    sp.dma_start(b, c.dram[name]).then_inc(loaded, 16)
                sp.dma_start(c.pages[:], c.dram["page_table"].rearrange("b p -> (b p)")[None, :]).then_inc(loaded, 16)
                sp.dma_start(c.g_rows[:], c.dram["norm_g"].rearrange("l w (k p) -> (l w k) p", p=P)).then_inc(loaded, 16)
                sp.wait_ge(loaded, 16 * 10)

            @block.tensor
            def _(pe):
                pe.wait_ge(loaded, 16 * 10)
                for i in range(2 * (QT + 1)):
                    t, kk = i // 2, i % 2
                    n = rows_of(t)
                    if kk == 0:
                        pe.wait_ge(x_in[t], 16)
                    if i >= 4:
                        pe.wait_ge(kept, i - 3)
                    for k in range(4):
                        last = nc.tensor.transpose(ps[:, i % 4, k * P:k * P + n],
                                                   xr[0:n, t, (kk * 4 + k) * P:(kk * 4 + k + 1) * P],
                                                   c.ident[0:n, 0:n])
                    last.then_inc(turned, 1)
                nc.tensor.transpose(ps[:, 4, 0:8 * KD], c.g_rows[:], c.ident[0:8 * KD, 0:8 * KD]).then_inc(turned, 1)

            @block.vector
            def _(dve):
                nc.vector.memset(c.ones[:], 1.0).then_inc(preset, 1)
                nc.vector.memset(c.eps[:], EPS).then_inc(preset, 1)
                for i in range(2 * (QT + 1)):
                    t, kk = i // 2, i % 2
                    n = rows_of(t)
                    dve.wait_ge(turned, i + 1)
                    nc.vector.tensor_copy(c.hT[:, kk * 4:kk * 4 + 4, t * P:t * P + n],
                                          ps[:, i % 4, :].rearrange("p (k t) -> p k t", k=4)[:, :, 0:n]).then_inc(kept, 1)
                dve.wait_ge(turned, 2 * (QT + 1) + 1)
                nc.vector.tensor_copy(c.g_cols[:], ps[:, 4, 0:8 * KD]).then_inc(kept, 1)


def norm_parts(c, name, src, sq, rs):
    nc, ps = c.nc, c.psum
    squared, summed, rooted, ready = (c.sem(f"{name}_{x}") for x in ("squared", "summed", "rooted", "ready"))
    free = c.sem(f"{name}_sq_free")

    def act_part(act):
        for k in range(KD):
            if k >= 4:
                act.wait_ge(free, k - 3)
            nc.scalar.activation(sq[:, k % 4, :], src[:, k, :], ACT.Square).then_inc(squared, 1)
        act.wait_ge(summed, 1)
        for h in range(2):
            nc.scalar.activation(rs[:, h * HALF:(h + 1) * HALF], ps[:, h, 0:HALF], ACT.Sqrt,
                                 bias=c.eps[:], scale=1.0 / D).then_inc(rooted, 1)

    def pe_part(pe):
        for k in range(KD):
            pe.wait_ge(squared, k + 1)
            for h in range(2):
                mm = nc.tensor.matmul(ps[:, h, 0:HALF], c.ones[:], sq[:, k % 4, h * HALF:(h + 1) * HALF],
                                      start=(k == 0), stop=(k == KD - 1))
            mm.then_inc(free if k < KD - 1 else summed, 1)

    def dve_part(dve):
        dve.wait_ge(rooted, 2)
        nc.vector.reciprocal(rs[:], rs[:]).then_inc(ready, 1)
        dve.wait_ge(ready, 1)
    return act_part, pe_part, dve_part


def stage_norm(c, name, src, dst, layer, which):
    nc = c.nc
    mine = ExitStack()
    sq, rs = c.buf(f"{name}_sq", [P, 4, T], ctx=mine), c.buf(f"{name}_rs", [P, T], ctx=mine)
    act_part, pe_part, dve_part = norm_parts(c, name, src, sq, rs)
    done = c.sem(f"{name}_done")
    with mine, nc.Block() as block:
        @block.scalar
        def _(act):
            act_part(act)

        @block.tensor
        def _(pe):
            pe_part(pe)

        @block.vector
        def _(dve):
            dve_part(dve)
            for k in range(KD):
                col = (layer * 4 + which) * KD + k
                nc.vector.scalar_tensor_tensor(dst[:, k, :], src[:, k, :], c.g_cols[:, col:col + 1], rs[:],
                                               ALU.mult, ALU.mult).then_inc(done, 1)


def stage_residual(c, name, y, layer, which):
    nc = c.nc
    mine = ExitStack()
    sq, rs = c.buf(f"{name}_sq", [P, 4, T], ctx=mine), c.buf(f"{name}_rs", [P, T], ctx=mine)
    act_part, pe_part, dve_part = norm_parts(c, name, y, sq, rs)
    scaled, done = c.sem(f"{name}_scaled"), c.sem(f"{name}_done")
    with mine, nc.Block() as block:
        @block.scalar
        def _(act):
            act_part(act)

        @block.tensor
        def _(pe):
            pe_part(pe)

        @block.vector
        def _(dve):
            dve_part(dve)
            for k in range(KD):
                col = (layer * 4 + which) * KD + k
                nc.vector.scalar_tensor_tensor(y[:, k, :], y[:, k, :], c.g_cols[:, col:col + 1], rs[:],
                                               ALU.mult, ALU.mult).then_inc(scaled, 1)
            for k in range(KD):
                dve.wait_ge(scaled, k + 1)
                nc.vector.tensor_add(c.hT[:, k, :], c.hT[:, k, :], y[:, k, :]).then_inc(done, 1)


CK = 8
NG = 512


def stage_linear(c, name, weights, kt, groups, x, evac, per=1):
    nc, ps = c.nc, c.psum
    nchunk = kt // CK
    slots = 2
    landed = [c.sem(f"{name}_w_landed{s}") for s in range(slots)]
    read, filled = c.sem(f"{name}_w_read"), c.sem(f"{name}_bank_filled")
    freed = [c.sem(f"{name}_even_bank_freed"), c.sem(f"{name}_odd_bank_freed")]
    body = per * nchunk
    assert body % slots == 0 and groups % per == 0
    with ExitStack() as mine:
        w = c.buf(f"{name}_w", [P, slots, CK, NG], ctx=mine)
        act_evac, dve_evac = evac(c, name, filled, freed, per, groups // per, mine)
        with nc.Block() as block:
            @block.sync
            def _(sp):
                for j in range(groups * nchunk):
                    if j >= slots:
                        g, chunk = divmod(j - slots, nchunk)
                        if chunk == nchunk - 1:
                            sp.wait_ge(filled, 8 * (g + 1))
                        else:
                            sp.wait_ge(read, g * (nchunk - 1) + chunk + 1)
                    sp.dma_start(w[:, j % slots], weights(j // nchunk, j % nchunk)).then_inc(landed[j % slots], 16)

            @block.tensor
            def _(pe):
                pe.sem_inc(freed[0], 4)
                pe.sem_inc(freed[1], 4)
                with pe.Fori(0, groups // per) as it:
                    for j in range(body):
                        s, chunk = j % slots, j % nchunk
                        pe.wait_ge(landed[s], it * (16 * body // slots) + 16 * (j // slots + 1))
                        for k in range(CK):
                            kk = chunk * CK + k
                            for m in range(NG // P):
                                for h in range(2):
                                    bank = m * 2 + h
                                    if kk == 0:
                                        pe.wait_ge(freed[h], it * (4 * per) + (j // nchunk) * 4 + m + 1)
                                    mm = nc.tensor.matmul(ps[:, bank, 0:HALF], w[:, s, k, m * P:(m + 1) * P],
                                                          x[:, kk, h * HALF:(h + 1) * HALF],
                                                          start=(kk == 0), stop=(kk == kt - 1))
                                    if kk == kt - 1:
                                        mm.then_inc(filled, 1)
                        if chunk < nchunk - 1:
                            mm.then_inc(read, 1)

            @block.scalar
            def _(act):
                act_evac(act)

            @block.vector
            def _(dve):
                dve_evac(dve)


def evac_copy(dst):
    def make(c, name, filled, freed, per, iters, mine):
        nc, ps = c.nc, c.psum

        def program(eng, copy, h):
            with eng.Fori(0, iters) as it:
                for m in range(4 * per):
                    bank = (m % 4) * 2 + h
                    eng.wait_ge(filled, it * (8 * per) + 2 * m + h + 1)
                    copy(dst[:, bass.ds(it * (4 * per) + m, 1), h * HALF:(h + 1) * HALF],
                         ps[:, bank:bank + 1, 0:HALF]).then_inc(freed[h], 1)
        return (lambda act: program(act, nc.scalar.copy, 0)), (lambda dve: program(dve, nc.vector.tensor_copy, 1))
    return make


def evac_sq_relu(dst):
    def make(c, name, filled, freed, per, iters, mine):
        nc, ps = c.nc, c.psum
        squared = c.sem(f"{name}_squared")
        tmp = c.buf(f"{name}_relu", [P, 4, HALF], ctx=mine)

        def act_prog(act):
            act.sem_inc(squared, 4)
            with act.Fori(0, iters) as it:
                for b in range(8 * per):
                    act.wait_ge(filled, it * (8 * per) + b + 1)
                    act.wait_ge(squared, it * (8 * per) + b + 1)
                    nc.scalar.activation(tmp[:, b % 4, :], ps[:, b % 8, 0:HALF], ACT.Relu).then_inc(freed[b % 2], 1)

        def dve_prog(dve):
            with dve.Fori(0, iters) as it:
                for b in range(8 * per):
                    m, h = b // 2, b % 2
                    dve.wait_ge(freed[h], it * (4 * per) + m + 5)
                    nc.vector.tensor_mul(dst[:, bass.ds(it * (4 * per) + m, 1), h * HALF:(h + 1) * HALF],
                                         tmp[:, b % 4:b % 4 + 1, :], tmp[:, b % 4:b % 4 + 1, :]).then_inc(squared, 1)
        return act_prog, dve_prog
    return make


def stage_outputs(c):
    nc, ps = c.nc, c.psum
    turned, kept, out = c.sem("y_turned"), c.sem("y_kept"), c.sem("y_written")
    with ExitStack() as mine:
        yr = c.buf("y_rows", [P, QT + 1, D], ctx=mine)
        with nc.Block() as block:
            @block.tensor
            def _(pe):
                for i in range(2 * (QT + 1)):
                    t, kk = i // 2, i % 2
                    n = rows_of(t)
                    if i >= 4:
                        pe.wait_ge(kept, i - 3)
                    for k in range(4):
                        mm = nc.tensor.transpose(ps[0:n, i % 4, k * P:(k + 1) * P],
                                                 c.hT[:, kk * 4 + k, t * P:t * P + n], c.ident[:])
                    mm.then_inc(turned, 1)

            @block.vector
            def _(dve):
                for i in range(2 * (QT + 1)):
                    t, kk = i // 2, i % 2
                    n = rows_of(t)
                    dve.wait_ge(turned, i + 1)
                    nc.vector.tensor_copy(yr[0:n, t, kk * 512:kk * 512 + 512], ps[0:n, i % 4, :]).then_inc(kept, 1)

            @block.sync
            def _(sp):
                for t in range(QT + 1):
                    sp.wait_ge(kept, 2 * t + 2)
                    dst = c.dram["y_prompt"][0, t * P:(t + 1) * P, :] if t < QT else c.dram["y_sample"][:, 0, :]
                    sp.dma_start(dst, yr[0:rows_of(t), t, :]).then_inc(out, 16)
                sp.wait_ge(out, 16 * (QT + 1))


def stage_mlp(c, layer):
    with ExitStack() as mine:
        hid = c.buf(f"hidden{layer}", [P, KF, T], ctx=mine)
        w1, w2 = c.dram["mlp_w1"][layer], c.dram["mlp_w2"][layer]
        stage_norm(c, f"mlp_in{layer}", c.hT, c.xT, layer, 2)
        stage_linear(c, f"mlp_up{layer}", lambda g, ch: w1.rearrange("(k p) n -> p k n", p=P)[:, :, bass.ts(g, NG)],
                     KD, DFF // NG, c.xT, evac_sq_relu(hid), per=2)
        stage_linear(c, f"mlp_down{layer}",
                     lambda g, ch: w2.rearrange("(k p) n -> p k n", p=P)[:, ch * CK:(ch + 1) * CK, bass.ts(g, NG)],
                     KF, D // NG, hid, evac_copy(c.xT), per=1)
        stage_residual(c, f"mlp_out{layer}", c.xT, layer, 3)


def stage_project(c):
    nc, ps = c.nc, c.psum
    w_in = c.dram["nsa_w_in"][0].rearrange("(k p) n -> p k n", p=P)
    nblk = 5
    landed = [c.sem(f"proj_w_landed{s}") for s in range(2)]
    gate_landed, table_landed = c.sem("proj_gate_w_landed"), c.sem("proj_table_landed")
    block_read, filled, freed = c.sem("proj_block_read"), c.sem("proj_bank_filled"), c.sem("proj_bank_freed")
    q_kept, swapped, swap_freed, roped = (c.sem(f"proj_{x}") for x in ("q_kept", "q_swapped", "swap_freed", "q_roped"))
    t1_sem, link, gated, written = c.sem("proj_t1"), c.sem("proj_link"), c.sem("proj_gate_exp"), c.sem("proj_written")
    with ExitStack() as mine:
        w = c.buf("proj_w", [P, 2, KD, NG], ctx=mine)
        wg = c.buf("proj_gate_w", [P, KD, 3 * NH], ctx=mine)
        tmp = c.buf("proj_tmp", [P, T], ctx=mine)
        swap = c.buf("swap", [P, P], ctx=mine)
        rope_t, rope = c.buf("rope_t", [P, 2, T], ctx=mine), c.buf("rope", [P, QT + 1, 2, HD // 2], ctx=mine)
        nq, nrow = 2 * KD, 3 * (QT + 1)
        with nc.Block() as block:
            @block.sync
            def _(sp):
                for b, name in ((swap, "c_swap"), (rope_t, "c_ropeT"), (rope, "c_rope")):
                    sp.dma_start(b[:], c.dram[name]).then_inc(table_landed, 16)
                for j in range(nblk):
                    if j >= 2:
                        sp.wait_ge(block_read, j - 1)
                    sp.dma_start(w[:, j % 2], w_in[:, :, bass.ts(j, NG)]).then_inc(landed[j % 2], 16)
                sp.dma_start(wg[:], w_in[:, :, nblk * NG:]).then_inc(gate_landed, 16)
                names = ("kv_cmp", "kv_sel", "kv_win")
                for b in range(3):
                    for t in range(QT + 1):
                        sp.wait_ge(roped, 8 + b * (QT + 1) + t + 1)
                        if t < QT:
                            dst = c.dram[f"{names[b]}_prompt"][0, 0, t * P:(t + 1) * P].rearrange("t s h d -> t (s h d)")
                        elif b < 2:
                            dst = c.dram[f"{names[b]}_sample"][0, :, 0].rearrange("t s h d -> t (s h d)")
                        else:
                            dst = c.dram["kv_win_sample"][0, :, WIN - 1].rearrange("t s h d -> t (s h d)")
                        sp.dma_start(dst, c.kv[0:rows_of(t), t, b, :]).then_inc(written, 16)
                sp.wait_ge(written, 16 * nrow)

            @block.tensor
            def _(pe):
                step = 0

                def start_bank(k):
                    if k == 0 and step >= 6:
                        pe.wait_ge(freed, step - 5)

                def swap_q(m):
                    pe.wait_ge(q_kept, 2 * (m + 1))
                    if m >= 1:
                        pe.wait_ge(swap_freed, m)
                    for h in range(2):
                        mm = nc.tensor.matmul(ps[:, 6 + h, 0:HALF], swap[:], c.qT[:, m, h * HALF:(h + 1) * HALF],
                                              start=True, stop=True)
                    mm.then_inc(swapped, 1)

                pe.wait_ge(table_landed, 48)
                for j in range(2):
                    pe.wait_ge(landed[j], 16)
                    for m in range(4):
                        for h in range(2):
                            for k in range(KD):
                                start_bank(k)
                                mm = nc.tensor.matmul(ps[:, step % 6, 0:HALF], w[:, j, k, m * P:(m + 1) * P],
                                                      c.xT[:, k, h * HALF:(h + 1) * HALF],
                                                      start=(k == 0), stop=(k == KD - 1))
                            mm.then_inc(filled, 1)
                            step += 1
                        if j * 4 + m >= 1:
                            swap_q(j * 4 + m - 1)
                    pe.drain().then_inc(block_read, 1)
                swap_q(KD - 1)
                for b in range(3):
                    pe.wait_ge(landed[b % 2], 16 * (b // 2 + 2))
                    for t in range(QT + 1):
                        n = rows_of(t)
                        for k in range(KD):
                            start_bank(k)
                            mm = nc.tensor.matmul(ps[0:n, step % 6, :], c.xT[:, k, t * P:t * P + n], w[:, b % 2, k, :],
                                                  start=(k == 0), stop=(k == KD - 1))
                        mm.then_inc(filled, 1)
                        step += 1
                    pe.drain().then_inc(block_read, 1)
                pe.wait_ge(gate_landed, 16)
                for t in range(QT + 1):
                    n = rows_of(t)
                    for k in range(KD):
                        start_bank(k)
                        mm = nc.tensor.matmul(ps[0:n, step % 6, 0:3 * NH], c.xT[:, k, t * P:t * P + n], wg[:, k, :],
                                              start=(k == 0), stop=(k == KD - 1))
                    mm.then_inc(filled, 1)
                    step += 1

            @block.scalar
            def _(act):
                step = 0
                for m in range(KD):
                    for h in range(2):
                        act.wait_ge(filled, step + 1)
                        nc.scalar.mul(c.qT[:, m, h * HALF:(h + 1) * HALF], ps[:, step % 6, 0:HALF], -SCALE)\
                            .then_inc(q_kept, 1)
                        act.wait_ge(q_kept, step + 1)
                        act.sem_inc(freed, 1)
                        step += 1
                for b in range(3):
                    for t in range(QT + 1):
                        n = rows_of(t)
                        act.wait_ge(filled, step + 1)
                        nc.scalar.copy(c.kv[0:n, t, b, :], ps[0:n, step % 6, :]).then_inc(freed, 1)
                        step += 1
                for t in range(QT + 1):
                    n = rows_of(t)
                    act.wait_ge(filled, step + 1)
                    nc.scalar.activation(c.gates[0:n, t, :], ps[0:n, step % 6, 0:3 * NH], ACT.Exp, scale=-1.0)\
                        .then_inc(freed, 1)
                    step += 1

            @block.vector
            def _(dve):
                links = 0

                def linked(ins):
                    nonlocal links
                    links += 1
                    ins.then_inc(link, 1)
                    dve.wait_ge(link, links)

                dve.wait_ge(table_landed, 48)
                for m in range(KD):
                    dve.wait_ge(swapped, m + 1)
                    if m >= 1:
                        dve.wait_ge(roped, m)
                    for h in range(2):
                        cols = slice(h * HALF, (h + 1) * HALF)
                        linked(nc.vector.tensor_mul(tmp[:, cols], ps[:, 6 + h, 0:HALF], rope_t[:, 1, cols]))
                    dve.sem_inc(swap_freed, 1)
                    linked(nc.vector.tensor_mul(c.qrT[:, m, :], c.qT[:, m, :], rope_t[:, 0, :]))
                    nc.vector.tensor_add(c.qrT[:, m, :], c.qrT[:, m, :], tmp[:]).then_inc(roped, 1)
                dve.wait_ge(roped, KD)
                for b in range(3):
                    for t in range(QT + 1):
                        n = rows_of(t)
                        dve.wait_ge(freed, nq + b * (QT + 1) + t + 1)
                        if b == 0:
                            dve.sem_inc(roped, 1)
                            continue
                        k = c.kv[0:n, t, b, 0:KVW].rearrange("p (h s d) -> p h s d", s=2, d=HD // 2)
                        tv = tmp[0:n, 0:KVW].rearrange("p (h s d) -> p h s d", s=2, d=HD // 2)

                        def table(i, heads):
                            return rope[0:n, t, i, :].unsqueeze(1).to_broadcast([n, heads, HD // 2])
                        linked(nc.vector.tensor_mul(tv[:, :, 0, :], k[:, :, 1, :], table(1, NKV)))
                        linked(nc.vector.tensor_mul(tv[:, :, 1, :], k[:, :, 0, :], table(1, NKV)))
                        for s in range(2):
                            linked(nc.vector.tensor_mul(k[:, :, s, :], k[:, :, s, :], table(0, NKV)))
                        linked(nc.vector.tensor_sub(k[:, :, 0, :], k[:, :, 0, :], tv[:, :, 0, :]))
                        nc.vector.tensor_add(k[:, :, 1, :], k[:, :, 1, :], tv[:, :, 1, :]).then_inc(roped, 1)
                        dve.wait_ge(roped, 8 + b * (QT + 1) + t + 1)
                for t in range(QT + 1):
                    n = rows_of(t)
                    dve.wait_ge(freed, nq + nrow + t + 1)
                    linked(nc.vector.tensor_scalar_add(c.gates[0:n, t, :], c.gates[0:n, t, :], 1.0))
                    linked(nc.vector.reciprocal(c.gates[0:n, t, :], c.gates[0:n, t, :]))


def stage_compress(c):
    nc, ps = c.nc, c.psum
    cmp_pages = c.dram["cache_kv_cmp"][0].rearrange("g (b t) s h d -> g s b h t d", t=STRIDE)
    prompt = c.dram["kv_cmp_prompt"][0, 0].rearrange("(b t) s h d -> s b h t d", t=STRIDE)
    units = NB // 2 + 1
    pages_ready, w_ready, pe_turned = c.sem("cmp_pages_ready"), c.sem("cmp_w_ready"), c.sem("cmp_pe_turned")
    landed = [c.sem(f"cmp_landed{s}") for s in range(2)]
    turned, turn_kept, summed = c.sem("cmp_turned"), c.sem("cmp_turn_kept"), c.sem("cmp_summed")
    shifted, added, gelued = c.sem("cmp_shifted"), c.sem("cmp_added"), c.sem("cmp_gelued")
    out_filled, out_kept, bias_done, pe_kept = (c.sem(f"cmp_{x}") for x in ("out_filled", "out_kept", "bias_done", "pe_kept"))
    used, xt_read, bias_kept, dup_done = c.sem("cmp_raw_used"), c.sem("cmp_xt_read"), c.sem("cmp_bias_kept"), c.sem("cmp_dup")
    with ExitStack() as mine:
        raw = c.buf("cmp_raw", [P, 2, NKV, STRIDE, HD], ctx=mine)
        xt = c.buf("cmp_xt", [P, 4, 512], ctx=mine)
        w1 = c.buf("cmp_w1", [P, 2, SPAIR, 2, HD], ctx=mine)
        w2 = c.buf("cmp_w2", [HD, 2, 2, HD], ctx=mine)
        pe_rows = c.buf("cmp_pe_rows", [2 * 2 * SPAIR, P], ctx=mine)
        pe_cols = c.buf("cmp_pe_cols", [P, 2 * 2 * SPAIR], ctx=mine)
        bias = c.buf("cmp_bias", [P, 2], ctx=mine)
        tmp = c.buf("cmp_tmp", [HD, 2, 512], ctx=mine)
        gel = c.buf("cmp_gelu", [HD, 2, 512], ctx=mine)

        def shape_of(u):
            return (P, 2, NSUB, NCS) if u < units - 1 else (NSUBP, 1, NSUBP, NCP)

        def view(bank, u):
            nsb, nb, per, nk = shape_of(u)
            return bank[:, 0:NKV * nsb].rearrange("p (h b n) -> p h b n", h=NKV, b=nb)

        with nc.Block() as block:
            @block.sync
            def _(sp):
                for kv in range(2):
                    for r in range(2):
                        sp.dma_start(w1[:, kv, :, r], c.dram["nsa_cmp_w1"][0, kv].rearrange("(r s p) e -> r p s e", r=2, p=P)[r])\
                            .then_inc(w_ready, 16)
                    for d in range(2):
                        sp.dma_start(w2[:, kv, d], c.dram["nsa_cmp_w2"][0, kv]).then_inc(w_ready, 16)
                sp.dma_start(pe_rows[:], c.dram["nsa_cmp_pe"][0].rearrange("v (a t) d -> (v a) (t d)", t=2)).then_inc(w_ready, 16)
                for i in range(2 * units):
                    u, kv = divmod(i, 2)
                    if i >= 2:
                        sp.wait_ge(turned, SPAIR * (i - 1))
                    if u == units - 1:
                        for h in range(NKV):
                            sp.dma_start(raw[0:NSUBP, i % 2, h], prompt[kv, :, h]).then_inc(landed[i % 2], 16)
                        continue
                    for b in range(2):
                        for j in range(NPAGE):
                            n = (2 * u + b) * NPAGE + j
                            page = sp.value_load(c.pages[0:1, n:n + 1], min_val=0, max_val=POOL_PAGES - 1)
                            at = b * NSUB + j * (PAGE // STRIDE)
                            rows = cmp_pages[bass.ds(page, 1), kv].rearrange("g b h t d -> (g b) h t d")
                            for h in range(NKV):
                                sp.dma_start(raw[at:at + PAGE // STRIDE, i % 2, h], rows[:, h]).then_inc(landed[i % 2], 16)

            @block.tensor
            def _(pe):
                pe.wait_ge(w_ready, 16 * 9)
                nc.tensor.transpose(ps[:, 7, 0:4 * SPAIR], pe_rows[:], c.ident[0:4 * SPAIR, 0:4 * SPAIR]).then_inc(pe_turned, 1)
                pe.wait_ge(pe_kept, 1)
                for kv in range(2):
                    for a in range(2 * SPAIR):
                        mm = nc.tensor.matmul(ps[0:HD, 7, 64 + kv:65 + kv], w1[:, kv, a % SPAIR, a // SPAIR, :],
                                              pe_cols[:, kv * 2 * SPAIR + a:kv * 2 * SPAIR + a + 1],
                                              start=(a == 0), stop=(a == 2 * SPAIR - 1))
                    mm.then_inc(bias_done, 1)

                def tail(i):
                    u, kv = divmod(i, 2)
                    nsb, nb, per, nk = shape_of(u)
                    pe.wait_ge(gelued, i + 1)
                    if i >= 2:
                        pe.wait_ge(out_kept, i - 1)
                    g = gel[:, i % 2, :]
                    if kv == 0:
                        cols = NKV * nb * nk
                        nc.tensor.matmul(ps[:, 5 + i % 2, 0:cols], w2[:, 0].rearrange("e a f -> e (a f)"), g[:, 0:cols],
                                         start=True, stop=True).then_inc(out_filled, 1)
                    else:
                        for b in range(nb):
                            for h in range(NKV):
                                at = (h * nb + b) * nk
                                mm = nc.tensor.matmul(ps[0:nk, 5 + i % 2, (b * NKV + h) * HD:(b * NKV + h + 1) * HD],
                                                      g[:, at:at + nk], w2[:, 1, 0, :], start=True, stop=True)
                        mm.then_inc(out_filled, 1)

                step = 0
                for i in range(2 * units):
                    u, kv = divmod(i, 2)
                    nsb = shape_of(u)[0]
                    pe.wait_ge(landed[i % 2], 16 * NKV * (2 * NPAGE * (i // 2) + (2 * NPAGE if u < units - 1 else 1)))

                    def turn(sp_):
                        n = i * SPAIR + sp_
                        if n >= 3:
                            pe.wait_ge(turn_kept, n - 2)
                        for h in range(NKV):
                            mm = nc.tensor.transpose(ps[:, n % 3, h * nsb:(h + 1) * nsb],
                                                     raw[0:nsb, i % 2, h, 2 * sp_:2 * sp_ + 2, :].rearrange("p t d -> p (t d)"),
                                                     c.ident[0:nsb, 0:nsb])
                        mm.then_inc(turned, 1)

                    def product(sp_):
                        n = i * SPAIR + sp_
                        pe.wait_ge(turn_kept, n + 1)
                        if sp_ == 0 and i >= 2:
                            pe.wait_ge(added, i - 1)
                        mm = nc.tensor.matmul(ps[:, 3 + i % 2, 0:NKV * nsb], w1[:, kv, sp_].rearrange("p r e -> p (r e)"),
                                              xt[:, n % 4, 0:NKV * nsb], start=(sp_ == 0), stop=(sp_ == SPAIR - 1))
                        mm.then_inc(summed, 1)

                    turn(0)
                    turn(1)
                    for sp_ in range(SPAIR):
                        product(sp_)
                        if sp_ + 2 < SPAIR:
                            turn(sp_ + 2)
                    if i >= 1:
                        tail(i - 1)
                tail(2 * units - 1)

            @block.scalar
            def _(act):
                for i in range(2 * units):
                    u, kv = divmod(i, 2)
                    nsb, nb, per, nk = shape_of(u)
                    cols = NKV * nb * nk
                    act.wait_ge(bias_kept, 1)
                    act.wait_ge(summed, SPAIR * (i + 1))
                    if i >= 2:
                        act.wait_ge(gelued, i - 1)
                        act.wait_ge(added, i - 1)
                    t = tmp[:, i % 2, 0:cols].rearrange("p (h b n) -> p h b n", h=NKV, b=nb)
                    for b in range(nb):
                        ins = nc.scalar.activation(t[:, :, b], view(ps[HD:P, 3 + i % 2, :], u)[:, :, b, 1:1 + nk], ACT.Identity,
                                                   bias=bias[HD:P, kv:kv + 1])
                    ins.then_inc(shifted, 1)
                    act.wait_ge(added, i + 1)
                    if i >= 2:
                        act.wait_ge(out_filled, i - 1)
                    nc.scalar.activation(gel[:, i % 2, 0:cols], tmp[:, i % 2, 0:cols], ACT.Gelu_apprx_tanh).then_inc(gelued, 1)

            @block.vector
            def _(dve):
                dve.wait_ge(pe_turned, 1)
                nc.vector.tensor_copy(pe_cols[:], ps[:, 7, 0:4 * SPAIR]).then_inc(pe_kept, 1)
                dve.wait_ge(bias_done, 2)
                nc.vector.tensor_copy(bias[HD:P, :], ps[0:HD, 7, 64:66]).then_inc(bias_kept, 1)

                def copy_out(i):
                    u, kv = divmod(i, 2)
                    nsb, nb, per, nk = shape_of(u)
                    dve.wait_ge(out_filled, i + 1)
                    bank = ps[:, 5 + i % 2, :]
                    if kv == 0:
                        v = bank[:, 0:NKV * nb * nk].rearrange("p (h b n) -> p h b n", h=NKV, b=nb)
                        if u == units - 1:
                            nc.vector.tensor_copy(c.kcp[:], v[:, :, 0, :]).then_inc(out_kept, 1)
                        else:
                            for half in range(2):
                                for a in range(2):
                                    ins = nc.vector.tensor_copy(c.kcs[half * HD:(half + 1) * HD, a, 2 * u:2 * u + 2, :],
                                                                v[half * HD:(half + 1) * HD, 2 * a + half])
                            ins.then_inc(out_kept, 1)
                    elif u == units - 1:
                        nc.vector.tensor_copy(c.vcp[0:nk, :], bank[0:nk, 0:KVW]).then_inc(out_kept, 1)
                    else:
                        nc.vector.tensor_copy(c.vcs[0:nk, 2 * u:2 * u + 2, :],
                                              bank[0:nk, :].rearrange("p (b x) -> p b x", b=2)).then_inc(out_kept, 1)

                for i in range(2 * units):
                    u, kv = divmod(i, 2)
                    nsb, nb, per, nk = shape_of(u)
                    cols = NKV * nb * nk
                    for sp_ in range(SPAIR):
                        n = i * SPAIR + sp_
                        dve.wait_ge(turned, n + 1)
                        if n >= 4:
                            dve.wait_ge(summed, n - 3)
                        nc.vector.tensor_copy(xt[:, n % 4, 0:NKV * nsb], ps[:, n % 3, 0:NKV * nsb]).then_inc(turn_kept, 1)
                    dve.wait_ge(shifted, i + 1)
                    t = tmp[:, i % 2, 0:cols].rearrange("p (h b n) -> p h b n", h=NKV, b=nb)
                    for b in range(nb):
                        ins = nc.vector.tensor_add(t[:, :, b], view(ps[0:HD, 3 + i % 2, :], u)[:, :, b, 0:nk], t[:, :, b])
                    ins.then_inc(added, 1)
                    if i >= 1:
                        copy_out(i - 1)
                copy_out(2 * units - 1)


def stage_prompt_attention(c):
    nc, ps = c.nc, c.psum
    turned, kept = c.sem("att_k_turned"), c.sem("att_k_kept")
    with ExitStack() as mine:
        kT = c.buf("att_kT", [P, 2, NKV, SEQ], ctx=mine)
        pcT = c.buf("att_pcT", [NCP, NH, SEQ], ctx=mine)
        with nc.Block() as block:
            @block.tensor
            def _(pe):
                for n in range(4):
                    kind, a = divmod(n, 2)
                    for t in range(QT):
                        mm = nc.tensor.transpose(ps[:, n, t * P:(t + 1) * P], c.kv[:, t, 1 + kind, a * P:(a + 1) * P], c.ident[:])
                    mm.then_inc(turned, 1)

            @block.vector
            def _(dve):
                for n in range(4):
                    kind, a = divmod(n, 2)
                    dve.wait_ge(turned, n + 1)
                    for to in range(2):
                        nc.vector.tensor_copy(kT[to * HD:(to + 1) * HD, kind, 2 * a, :], ps[0:HD, n, :]).then_inc(kept, 1)

            @block.scalar
            def _(act):
                for n in range(4):
                    kind, a = divmod(n, 2)
                    act.wait_ge(kept, 2 * (n + 1))
                    for to in range(2):
                        nc.scalar.copy(kT[to * HD:(to + 1) * HD, kind, 2 * a + 1, :], ps[HD:P, n, :])

        scored, masked, least_d, subbed, exped, scaled = (c.sem(f"attc_{x}") for x in ("scored", "masked", "least", "sub", "exp", "scaled"))
        turned_p, kept_p, summed, rec, gated, pmasked = (c.sem(f"attc_{x}") for x in ("turned", "kept", "summed", "rec", "gated", "pmasked"))
        with ExitStack() as here:
            sc = c.buf("attc_s", [P, 2, GRP, QT, NCP], ctx=here)
            low = c.buf("attc_low", [P, 2, GRP * QT], ctx=here)
            tot = c.buf("attc_tot", [P, 2, GRP * QT], ctx=here)
            cm = c.cmask[:].rearrange("p (w g t k) -> p w (g t) k", w=2, g=GRP, t=QT)

            def wide(x):
                return x.unsqueeze(2).to_broadcast([P, GRP * QT, NCP])

            with nc.Block() as block:
                @block.tensor
                def _(pe):
                    def turn(h):
                        pe.wait_ge(scaled, h + 1)
                        for g in range(GRP):
                            n = h * GRP + g
                            if n >= 3:
                                pe.wait_ge(kept_p, n - 2)
                            for t in range(QT):
                                mm = nc.tensor.transpose(ps[0:NCP, 4 + n % 3, t * P:(t + 1) * P], sc[:, h % 2, g, t, :], c.ident[:])
                            mm.then_inc(turned_p, 1)
                    for h in range(NKV):
                        if h >= 2:
                            pe.wait_ge(masked, h - 1)
                        for g in range(GRP):
                            head = h * GRP + g
                            rows = slice(head % 2 * HD, head % 2 * HD + HD)
                            for t in range(QT):
                                at = (g // 2 * QT + t) * NCP
                                mm = nc.tensor.matmul(ps[:, h % 2 * 2 + g % 2, at:at + NCP], c.qT[rows, head // 2, t * P:(t + 1) * P],
                                                      c.kcp[rows, h, :], start=True, stop=True)
                        mm.then_inc(scored, 1)
                        if h >= 1:
                            turn(h - 1)
                    turn(NKV - 1)

                @block.vector
                def _(dve):
                    def finish(h):
                        s = sc[:, h % 2].rearrange("p g t k -> p (g t) k")
                        dve.wait_ge(exped, h + 1)
                        nc.vector.tensor_mul(s, s, cm[:, 1]).then_inc(pmasked, 1)
                        dve.wait_ge(pmasked, h + 1)
                        nc.vector.tensor_reduce(tot[:, h % 2, :], s, AX.X, ALU.add).then_inc(summed, 1)
                        dve.wait_ge(summed, h + 1)
                        nc.vector.tensor_scalar_max(tot[:, h % 2, :], tot[:, h % 2, :], 1e-20).then_inc(rec, 1)
                        dve.wait_ge(rec, 3 * h + 1)
                        nc.vector.reciprocal(tot[:, h % 2, :], tot[:, h % 2, :]).then_inc(rec, 1)
                        dve.wait_ge(rec, 3 * h + 2)
                        gate = c.gates[:, 0:QT, :].rearrange("p t (h w) -> p h t w", w=3)[:, h * GRP:(h + 1) * GRP, :, 0]
                        nc.vector.tensor_mul(tot[:, h % 2, :].rearrange("p (g t) -> p g t", g=GRP),
                                             tot[:, h % 2, :].rearrange("p (g t) -> p g t", g=GRP), gate).then_inc(rec, 1)
                        dve.wait_ge(rec, 3 * h + 3)
                        nc.vector.tensor_mul(s, s, wide(tot[:, h % 2, :])).then_inc(scaled, 1)

                    for h in range(NKV):
                        s = sc[:, h % 2].rearrange("p g t k -> p (g t) k")
                        dve.wait_ge(scored, h + 1)
                        if h >= 2:
                            dve.wait_ge(turned_p, GRP * (h - 1))
                        for par in range(2):
                            ins = nc.vector.tensor_add(
                                sc[:, h % 2, par::2], ps[:, h % 2 * 2 + par, 0:GRP // 2 * QT * NCP].rearrange("p (g t k) -> p g t k", g=GRP // 2, t=QT),
                                c.cmask[:].rearrange("p (w g t k) -> p w g t k", w=2, g=GRP, t=QT)[:, 0, par::2])
                        ins.then_inc(masked, 1)
                        dve.wait_ge(masked, h + 1)
                        nc.vector.tensor_reduce(low[:, h % 2, :], s, AX.X, ALU.min).then_inc(least_d, 1)
                        dve.wait_ge(least_d, h + 1)
                        nc.vector.tensor_sub(s, s, wide(low[:, h % 2, :])).then_inc(subbed, 1)
                        if h >= 1:
                            finish(h - 1)
                    finish(NKV - 1)

                @block.scalar
                def _(act):
                    n = 0
                    for h in range(NKV + 1):
                        if h < NKV:
                            act.wait_ge(subbed, h + 1)
                            s = sc[:, h % 2].rearrange("p g t k -> p (g t k)")
                            nc.scalar.activation(s, s, ACT.Exp, scale=-1.0).then_inc(exped, 1)
                        if h >= 1:
                            for g in range(GRP):
                                act.wait_ge(turned_p, n + 1)
                                nc.scalar.copy(pcT[:, n, :], ps[0:NCP, 4 + n % 3, :]).then_inc(kept_p, 1)
                                n += 1

        scored, lowered, exped, recip, scaled, turned_u, kept_u, unit_mul = (
            c.sem(f"att_{x}") for x in ("scored", "lowered", "exped", "recip", "scaled", "turned", "kept", "read"))
        o_filled, o_kept = c.sem("att_o_filled"), c.sem("att_o_kept")
        NU = NH * 2 * QT
        LAG, LAG_PV = 3, 5
        with ExitStack() as here:
            pr = c.buf("att_p", [P, 4, SEQ], ctx=here)
            pT = c.buf("att_pT", [P, 2, QT, SEQ], ctx=here)
            low = c.buf("att_low", [P, 4], ctx=here)
            tot = c.buf("att_tot", [P, 4], ctx=here)

            def unit(n):
                return n // (2 * QT), (n // QT) % 2, n % QT

            with nc.Block() as block:
                @block.tensor
                def _(pe):
                    def scores(n):
                        head, kind, i = unit(n)
                        rows = slice(head % 2 * HD, head % 2 * HD + HD)
                        if n >= 3:
                            pe.wait_ge(lowered, n - 2)
                        nc.tensor.matmul(ps[:, n % 3, 0:(i + 1) * P], c.qrT[rows, head // 2, i * P:(i + 1) * P],
                                         kT[rows, kind, head // GRP, 0:(i + 1) * P], start=True, stop=True).then_inc(scored, 1)

                    def turn(n):
                        head, kind, i = unit(n)
                        pe.wait_ge(scaled, n + 1)
                        if n >= 3:
                            pe.wait_ge(kept_u, n - 2)
                        for j in range(i + 1):
                            mm = nc.tensor.transpose(ps[:, 3 + n % 3, j * P:(j + 1) * P], pr[:, n % 4, j * P:(j + 1) * P], c.ident[:])
                        mm.then_inc(turned_u, 1)

                    def values(n):
                        head, kind, i = unit(n)
                        hp, par = head // 2, head % 2
                        out = ps[par * HD:(par + 1) * HD, 6 + hp % 2, :]
                        if kind == 0:
                            if hp >= 2 and par == 0:
                                pe.wait_ge(o_kept, hp - 1)
                            nc.tensor.matmul(out, c.vcp[0:NCP, head // GRP * HD:(head // GRP + 1) * HD], pcT[:, head, :],
                                             start=True, stop=False)
                        pe.wait_ge(kept_u, n + 1)
                        for j in range(QT):
                            mm = nc.tensor.matmul(out[:, j * P:SEQ],
                                                  c.kv[:, j, 1 + kind, KVW + head // GRP * HD:KVW + (head // GRP + 1) * HD],
                                                  pT[:, kind, j, j * P:SEQ], start=False, stop=(kind == 1 and j == QT - 1))
                        mm.then_inc(o_filled, 1)

                    for n in range(NU + LAG_PV):
                        if n < NU:
                            scores(n)
                        if LAG <= n < NU + LAG:
                            turn(n - LAG)
                        if n >= LAG_PV and (n - LAG_PV) % QT == QT - 1:
                            values(n - LAG_PV)

                @block.vector
                def _(dve):
                    for n in range(NU + 1):
                        if n < NU:
                            head, kind, i = unit(n)
                            w = (i + 1) * P
                            dve.wait_ge(scored, n + 1)
                            if n >= 4:
                                dve.wait_ge(turned_u, n - 3)
                            nc.vector.tensor_tensor_reduce(pr[:, n % 4, 0:w], ps[:, n % 3, 0:w], c.causal[:, SEQ - w:SEQ], 1.0,
                                                           3e38, ALU.add, ALU.min, low[:, n % 4:n % 4 + 1]).then_inc(lowered, 1)
                        if n >= 1:
                            m = n - 1
                            head, kind, i = unit(m)
                            w = (i + 1) * P
                            dve.wait_ge(exped, m + 1)
                            nc.vector.reciprocal(tot[:, m % 4:m % 4 + 1], tot[:, m % 4:m % 4 + 1]).then_inc(recip, 1)
                            dve.wait_ge(recip, m + 1)
                            gate = c.gates[:, i, head * 3 + 1 + kind:head * 3 + 2 + kind]
                            nc.vector.tensor_scalar(pr[:, m % 4, 0:w], pr[:, m % 4, 0:w], tot[:, m % 4:m % 4 + 1], gate,
                                                    ALU.mult, ALU.mult).then_inc(scaled, 1)

                @block.scalar
                def _(act):
                    def keep(n):
                        head, kind, i = unit(n)
                        act.wait_ge(turned_u, n + 1)
                        hk = n // QT
                        if hk >= 2:
                            act.wait_ge(o_filled, hk - 1)
                        nc.scalar.copy(pT[:, kind, 0:i + 1, i * P:(i + 1) * P],
                                       ps[:, 3 + n % 3, 0:(i + 1) * P].rearrange("p (j q) -> p j q", q=P)).then_inc(kept_u, 1)

                    def keep_o(hp):
                        act.wait_ge(o_filled, 4 * (hp + 1))
                        nc.scalar.copy(c.oT[:, hp, 0:SEQ], ps[:, 6 + hp % 2, :]).then_inc(o_kept, 1)

                    for n in range(NU + LAG + 3):
                        if n < NU:
                            head, kind, i = unit(n)
                            w = (i + 1) * P
                            act.wait_ge(lowered, n + 1)
                            nc.scalar.activation(pr[:, n % 4, 0:w], pr[:, n % 4, 0:w], ACT.Exp, scale=-1.0,
                                                 bias=low[:, n % 4:n % 4 + 1], accum_out=tot[:, n % 4:n % 4 + 1]).then_inc(exped, 1)
                        if LAG <= n < NU + LAG:
                            keep(n - LAG)
                        if n >= LAG_PV and (n - LAG_PV) % (4 * QT) == 4 * QT - 1:
                            keep_o((n - LAG_PV) // (4 * QT))


NKC = PAST // P
NWC = WIN // P
NC_S = NKC + NWC


def stage_sample_queries(c):
    nc, ps = c.nc, c.psum
    cleared, put, gates_out, k_turned = c.sem("sq_cleared"), c.sem("sq_put"), c.sem("sq_gates"), c.sem("sq_k_turned")
    k_kept = c.sem("sq_k_kept")
    with nc.Block() as block:
        @block.vector
        def _(dve):
            nc.vector.memset(c.qz[:], 0.0).then_inc(cleared, 1)
            dve.wait_ge(cleared, 1)
            for which, src in enumerate((c.qT, c.qrT)):
                flat = c.qz[:, which].rearrange("p a b x -> p a (b x)")
                for t in range(KD):
                    a, kv2 = t // 4, t // 2 % 2
                    for par in range(2):
                        h = 2 * t + par
                        base = flat[kv2 * HD:(kv2 + 1) * HD, a, :]
                        dst = bass.AP(base.tensor, base.offset + h, [list(base.ap[0]), [P + NH, NB]])
                        nc.vector.tensor_copy(dst, src[par * HD:(par + 1) * HD, t, SEQ:T]).then_inc(put, 1)
            dve.wait_ge(k_turned, 1)
            nc.vector.tensor_copy(c.knT[:], ps[:, 0, 0:4 * NB].rearrange("p (w a b) -> p w a b", w=2, a=2)).then_inc(k_kept, 1)

        @block.tensor
        def _(pe):
            for which in range(2):
                for a in range(2):
                    mm = nc.tensor.transpose(ps[:, 0, (which * 2 + a) * NB:(which * 2 + a + 1) * NB],
                                             c.kv[0:NB, QT, 1 + which, a * P:(a + 1) * P], c.ident[0:NB, 0:NB])
            mm.then_inc(k_turned, 1)

        @block.sync
        def _(sp):
            for b in range(NB):
                sp.dma_start(c.gates_s[b * NH:(b + 1) * NH, :],
                             c.gates[b:b + 1, QT, :].rearrange("o (h w) -> o h w", w=3)).then_inc(gates_out, 16)
            sp.wait_ge(gates_out, 16 * NB)


def stage_sample_attention(c):
    nc, ps = c.nc, c.psum
    sel_pages = c.dram["cache_kv_sel"][0].rearrange("g t s h d -> g t (s h d)")
    win = c.dram["cache_kv_win"][0].rearrange("b (c t) s h d -> b t c (s h d)", t=P)
    win_out = c.dram["kv_win_sample"][0].rearrange("b t s h d -> b t (s h d)")
    KS, VS = 2, 3
    k_landed = [c.sem(f"sa_k_landed{s}") for s in range(KS)]
    v_landed, written = [c.sem(f"sa_v_landed{s}") for s in range(VS)], [c.sem(f"sa_k_written{s}") for s in range(KS)]
    v_written, v_read = [c.sem(f"sa_v_written{s}") for s in range(VS)], c.sem("sa_v_read")
    turned, kept, scored, s_done = c.sem("sa_turned"), c.sem("sa_kept"), c.sem("sa_scored"), c.sem("sa_scores_done")
    link, exped, a_ready = c.sem("sa_link"), c.sem("sa_exp"), c.sem("sa_exp_ready")
    imp_in, imp_out, p_turn, p_kept, o_done, o_kept = (c.sem(f"sa_{x}") for x in ("imp_in", "imp_out", "p_turned", "p_kept", "o_done", "o_kept"))
    with ExitStack() as mine:
        kraw = c.buf("sa_kraw", [P, KS, NC_S, KVW], ctx=mine)
        vraw = c.buf("sa_v", [P, VS, NC_S, KVW], ctx=mine)
        kT = c.buf("sa_kT", [P, 4, 512], ctx=mine)
        s_sel = c.buf("sa_s_sel", [P, PAST + NB], ctx=mine)
        s_win = c.buf("sa_s_win", [P, WIN + NB], ctx=mine)
        s_cmp = c.buf("sa_s_cmp", [P, NCS], ctx=mine)
        low = c.buf("sa_low", [P, 3], ctx=mine)
        tot = c.buf("sa_tot", [P, 3], ctx=mine)
        drop = c.buf("sa_drop", [P, 4, NSEL], ctx=mine)
        one = c.buf("sa_one", [P, 4], ctx=mine)
        pc = c.buf("sa_pcT", [P, 2, P], ctx=mine)
        pT = c.buf("sa_pT", [P, NC_S, P], ctx=mine)
        pn = c.buf("sa_pnT", [NB, 2, P], ctx=mine)
        ngroup = NB * 3 * 2
        with nc.Block() as block:
            @block.sync
            def _(sp):
                def shift(src, b, cols, done):
                    sp.dma_start(win_out[b, 0:P - 1, cols], src[1:P, NKC, :]).then_inc(done, 16)
                    sp.dma_start(win_out[b, P - 1:WIN - 1, cols].rearrange("(c t) x -> t c x", t=P),
                                 src[:, NKC + 1:, :]).then_inc(done, 16)

                def load(dst, b, cols, done):
                    for j in range(NPAGE):
                        n = b * NPAGE + j
                        page = sp.value_load(c.pages[0:1, n:n + 1], min_val=0, max_val=POOL_PAGES - 1)
                        rows = sel_pages[bass.ds(page, 1), :, :].rearrange("g t x -> (g t) x")
                        sp.dma_start(dst[:, j, :], rows[:, cols]).then_inc(done, 16)
                    sp.dma_start(dst[:, NKC:, :], win[b, :, :, cols]).then_inc(done, 16)

                for b in range(NB):
                    s = b % KS
                    if b >= KS:
                        sp.wait_ge(turned, 6 * (b - KS + 1))
                        sp.wait_ge(written[s], b // KS * 32)
                    load(kraw[:, s], b, slice(0, KVW), k_landed[s])
                    sp.wait_ge(k_landed[s], 16 * 9 * (b // KS + 1))
                    shift(kraw[:, s], b, slice(0, KVW), written[s])
                for b in range(NB):
                    s = b % VS
                    if b >= VS:
                        sp.wait_ge(v_read, b - VS + 1)
                        sp.wait_ge(v_written[s], b // VS * 32)
                    load(vraw[:, s], b, slice(KVW, ROW), v_landed[s])
                    sp.wait_ge(v_landed[s], 16 * 9 * (b // VS + 1))
                    shift(vraw[:, s], b, slice(KVW, ROW), v_written[s])
                for s in range(KS):
                    sp.wait_ge(written[s], 32 * len(range(s, NB, KS)))
                for s in range(VS):
                    sp.wait_ge(v_written[s], 32 * len(range(s, NB, VS)))

            @block.tensor
            def _(pe):
                for a in range(2):
                    for b in range(NB):
                        nc.tensor.matmul(ps[:, 6, 0:NCS], c.qz[:, 0, a, b, :], c.kcs[:, a, b, :],
                                         start=(a == 0 and b == 0), stop=(a == 1 and b == NB - 1))
                for w in range(2):
                    for a in range(2):
                        for b in range(NB):
                            mm = nc.tensor.matmul(ps[:, 7, w * NB:(w + 1) * NB], c.qz[:, 1, a, b, :], c.knT[:, w, a, :],
                                                  start=(a == 0 and b == 0), stop=(a == 1 and b == NB - 1))
                mm.then_inc(s_done, 1)

                def product(n):
                    b, r = divmod(n, 6)
                    part, a = divmod(r, 2)
                    pe.wait_ge(kept, n + 1)
                    nc.tensor.matmul(ps[:, part, :], c.qz[:, 1, a, b, :], kT[:, n % 4, :],
                                     start=(b == 0 and a == 0), stop=(b == NB - 1 and a == 1)).then_inc(scored, 1)

                for n in range(ngroup + 2):
                    if n < ngroup:
                        b, r = divmod(n, 6)
                        part, a = divmod(r, 2)
                        if r == 0:
                            pe.wait_ge(k_landed[b % KS], 16 * 9 * (b // KS + 1))
                        if n >= 3:
                            pe.wait_ge(kept, n - 2)
                        for j in range(4):
                            mm = nc.tensor.transpose(ps[:, 3 + n % 3, j * P:(j + 1) * P],
                                                     kraw[:, b % KS, part * 4 + j, a * P:(a + 1) * P], c.ident[:])
                        mm.then_inc(turned, 1)
                    if n >= 2:
                        product(n - 2)
                pe.wait_ge(imp_in, 1)
                nc.tensor.transpose(ps[0:NCS, 3, 0:P], s_cmp[:], c.ident[:]).then_inc(imp_out, 1)
                pe.wait_ge(imp_in, 2)
                nc.tensor.matmul(ps[:, 3, P:P + NSEL], pc[0:NCS, 0, :], c.over[0:NCS, :], start=True, stop=True).then_inc(imp_out, 1)
                pe.wait_ge(imp_in, 3)
                nc.tensor.matmul(ps[:, 4, 0:NSEL], c.group[:], drop[:, 0, :], start=True, stop=True).then_inc(imp_out, 1)
                pe.wait_ge(a_ready, 4)
                nc.tensor.transpose(ps[0:NCS, 5, 0:P], s_cmp[:], c.ident[:]).then_inc(p_turn, 1)
                pe.wait_ge(a_ready, 6)
                for q in range(3):
                    if q == 1:
                        pe.wait_ge(p_kept, 1)
                    for j in range(4):
                        src = s_sel[:, (q * 4 + j) * P:(q * 4 + j + 1) * P] if q < 2 else s_win[:, j * P:(j + 1) * P]
                        mm = nc.tensor.transpose(ps[:, (3, 4, 2)[q], j * P:(j + 1) * P], src, c.ident[:])
                    mm.then_inc(p_turn, 1)
                for w in range(2):
                    src = s_win[:, WIN:] if w else s_sel[:, PAST:]
                    mm = nc.tensor.transpose(ps[0:NB, 6, w * P:(w + 1) * P], src, c.ident[:])
                mm.then_inc(p_turn, 1)
                pe.wait_ge(p_kept, 5)
                for b in range(NB):
                    pe.wait_ge(v_landed[b % VS], 16 * 9 * (b // VS + 1))
                    for a in range(2):
                        out = ps[:, 0, (b * 2 + a) * 8:(b * 2 + a + 1) * 8]
                        cols, heads = slice(a * P, (a + 1) * P), slice(b * NH + a * 8, b * NH + a * 8 + 8)
                        nc.tensor.matmul(out, c.vcs[0:NCS, b, cols], pc[0:NCS, 1, heads], start=True, stop=False)
                        for w in range(2):
                            nc.tensor.matmul(out, c.kv[0:NB, QT, 1 + w, KVW + a * P:KVW + (a + 1) * P], pn[:, w, heads],
                                             start=False, stop=False)
                        for j in range(NC_S):
                            mm = nc.tensor.matmul(out, vraw[:, b % VS, j, cols], pT[:, j, heads], start=False, stop=(j == NC_S - 1))
                    mm.then_inc(v_read, 1)

            @block.scalar
            def _(act):
                for n in range(0, ngroup, 2):
                    act.wait_ge(turned, n + 1)
                    if n >= 4:
                        act.wait_ge(scored, n - 3)
                    nc.scalar.copy(kT[:, n % 4, :], ps[:, 3 + n % 3, :]).then_inc(kept, 1)
                    if n + 1 < ngroup:
                        act.wait_ge(turned, n + 2)
                        if n + 1 >= 4:
                            act.wait_ge(scored, n - 2)
                        nc.scalar.copy(kT[:, (n + 1) % 4, :], ps[:, 3 + (n + 1) % 3, :]).then_inc(kept, 1)
                for w, s in enumerate((s_cmp, s_win, s_sel)):
                    act.wait_ge(a_ready, w + 1)
                    nc.scalar.activation(s[:], s[:], ACT.Exp, scale=-1.0, bias=low[:, w:w + 1],
                                         accum_out=tot[:, w:w + 1]).then_inc(exped, 1)

            @block.vector
            def _(dve):
                links = 0

                def linked(ins):
                    nonlocal links
                    links += 1
                    ins.then_inc(link, 1)
                    dve.wait_ge(link, links)

                def weigh(w, s, signal=None):
                    gate = c.gates_s[:, (0, 2, 1)[w]:(0, 2, 1)[w] + 1]
                    return nc.vector.tensor_scalar(s[:], s[:], tot[:, w:w + 1], gate, ALU.mult, ALU.mult)

                dve.wait_ge(s_done, 1)
                linked(nc.vector.tensor_copy(s_cmp[:], ps[:, 6, 0:NCS]))
                linked(nc.vector.tensor_copy(one[:, 0:1], ps[:, 7, 0:1]))
                linked(nc.vector.tensor_add(s_sel[:, PAST:], ps[:, 7, 0:NB], c.own[:]))
                linked(nc.vector.tensor_add(s_win[:, WIN:], ps[:, 7, NB:2 * NB], c.own[:]))
                nc.vector.tensor_reduce(low[:, 0:1], s_cmp[:], AX.X, ALU.min).then_inc(a_ready, 1)
                dve.wait_ge(exped, 1)
                linked(nc.vector.reciprocal(tot[:, 0:1], tot[:, 0:1]))
                nc.vector.tensor_scalar(s_cmp[:], s_cmp[:], tot[:, 0:1], None, ALU.mult).then_inc(imp_in, 1)
                dve.wait_ge(scored, ngroup)
                linked(nc.vector.tensor_copy(s_win[:, 0:WIN], ps[:, 2, :]))
                nc.vector.tensor_reduce(low[:, 1:2], s_win[:], AX.X, ALU.min).then_inc(a_ready, 1)
                dve.wait_ge(imp_out, 1)
                nc.vector.tensor_copy(pc[0:NCS, 0, :], ps[0:NCS, 3, 0:P]).then_inc(imp_in, 1)
                dve.wait_ge(imp_out, 2)
                nc.vector.tensor_copy(drop[:, 0, :], ps[:, 3, P:P + NSEL]).then_inc(imp_in, 1)
                dve.wait_ge(imp_out, 3)
                imp, eq, at = drop[:, 1, :], drop[:, 2, :], drop[:, 3, :]
                linked(nc.vector.tensor_copy(imp, ps[:, 4, 0:NSEL]))
                linked(nc.vector.tensor_reduce(one[:, 1:2], imp[:, 1:NSEL - 2], AX.X, ALU.min))
                linked(nc.vector.tensor_scalar(eq[:, 1:NSEL - 2], imp[:, 1:NSEL - 2], one[:, 1:2], None, ALU.is_equal))
                linked(nc.vector.tensor_mul(at[:, 1:NSEL - 2], eq[:, 1:NSEL - 2], c.blk[:, 1:NSEL - 2]))
                linked(nc.vector.tensor_reduce(one[:, 2:3], at[:, 1:NSEL - 2], AX.X, ALU.max))
                linked(nc.vector.tensor_scalar(eq, c.blk[:], one[:, 2:3], BIG, ALU.is_equal, ALU.mult))
                for half in range(2):
                    linked(nc.vector.tensor_add(s_sel[:, half * 512:(half + 1) * 512].rearrange("p (n x) -> p n x", x=SELB),
                                                ps[:, half, :].rearrange("p (n x) -> p n x", x=SELB),
                                                eq[:, half * 8:half * 8 + 8].unsqueeze(2).to_broadcast([P, 8, SELB])))
                nc.vector.tensor_reduce(low[:, 2:3], s_sel[:], AX.X, ALU.min).then_inc(a_ready, 1)
                nc.vector.tensor_scalar(s_cmp[:], s_cmp[:], c.gates_s[:, 0:1], None, ALU.mult).then_inc(a_ready, 1)
                for w, s in ((1, s_win), (2, s_sel)):
                    dve.wait_ge(exped, w + 1)
                    linked(nc.vector.reciprocal(tot[:, w:w + 1], tot[:, w:w + 1]))
                    weigh(w, s).then_inc(a_ready, 1)
                dve.wait_ge(p_turn, 1)
                nc.vector.tensor_copy(pc[0:NCS, 1, :], ps[0:NCS, 5, 0:P]).then_inc(p_kept, 1)
                for q in range(3):
                    dve.wait_ge(p_turn, 2 + q)
                    nc.vector.tensor_copy(pT[:, q * 4:q * 4 + 4, :],
                                          ps[:, (3, 4, 2)[q], :].rearrange("p (j x) -> p j x", x=P)).then_inc(p_kept, 1)
                dve.wait_ge(p_turn, 5)
                nc.vector.tensor_copy(pn[:], ps[0:NB, 6, 0:2 * P].rearrange("p (w x) -> p w x", w=2)).then_inc(p_kept, 1)
                dve.wait_ge(v_read, NB)
                for kv2 in range(2):
                    for par in range(2):
                        for a in range(2):
                            src = ps[kv2 * HD:(kv2 + 1) * HD, 0, 0:NB * NH].rearrange("p (b a v j r) -> p a v r j b", a=2, v=2, j=2, r=2)
                            nc.vector.tensor_copy(c.oT[par * HD:(par + 1) * HD, a * 4 + kv2 * 2:a * 4 + kv2 * 2 + 2, SEQ:T],
                                                  src[:, a, kv2, par]).then_inc(o_kept, 1)


def stage_nsa(c):
    with ExitStack() as outer:
        c.kcs = c.buf("kcs", [P, 2, NB, NCS], ctx=outer)
        c.vcs = c.buf("vcs", [NCS, NB, KVW], ctx=outer)
        c.kcp = c.buf("kcp", [P, NKV, NCP], ctx=outer)
        c.vcp = c.buf("vcp", [NCP, KVW], ctx=outer)
        c.kv = c.buf("kv", [P, QT + 1, 3, ROW], ctx=outer)
        c.gates = c.buf("gates", [P, QT + 1, 3 * NH], ctx=outer)
        c.gates_s = c.buf("gates_s", [P, 3], ctx=outer)
        c.qz = c.buf("qz", [P, 2, 2, NB, P], ctx=outer)
        c.knT = c.buf("knT", [P, 2, 2, NB], ctx=outer)
        c.oT = c.xT
        stage_norm(c, "nsa_in", c.hT, c.xT, 0, 0)
        with ExitStack() as queries:
            c.qT = c.buf("qT", [P, KD, T], ctx=queries)
            c.qrT = c.buf("qrT", [P, KD, T], ctx=queries)
            stage_project(c)
            stage_sample_queries(c)
            stage_compress(c)
            stage_prompt_attention(c)
        stage_sample_attention(c)
    w_o = c.dram["nsa_w_o"][0].rearrange("(k p) n -> p k n", p=P)
    with ExitStack() as mine:
        y = c.buf("nsa_y", [P, KD, T], ctx=mine)
        stage_linear(c, "nsa_o", lambda g, ch: w_o[:, :, bass.ts(g, NG)], KD, D // NG, c.oT, evac_copy(y), per=2)
        stage_residual(c, "nsa_out", y, 0, 1)


MAGIC = 1.5 * 2.0 ** 23
TWO_PI = 2.0 * np.pi
COLS = NCH + 2 * NB
HCOLS = NCH + NB
A_COLS = G + GP


def split(x, parts):
    out = []
    for _ in range(parts - 1):
        m, e = np.frexp(x)
        hi = float(np.ldexp(np.round(m * 2 ** 10), e - 10))
        out.append(hi)
        x -= hi
    return [*out, float(np.float32(x))]


class Chain:

    def __init__(self, c, eng, name):
        self.eng, self.sem, self.n = eng, c.sem(name), 0

    def __call__(self, ins):
        self.n += 1
        ins.then_inc(self.sem, 1)
        self.eng.wait_ge(self.sem, self.n)


def complex_axpy(nc, link, out, x, ar, nai, ai, t, u):
    for r in range(2):
        link(nc.vector.tensor_mul(t[:, r], x[:, r], ar))
    link(nc.vector.tensor_mul(u[:, 0], x[:, 1], nai))
    link(nc.vector.tensor_mul(u[:, 1], x[:, 0], ai))
    for r in range(2):
        link(nc.vector.tensor_add(t[:, r], t[:, r], u[:, r]))
    for r in range(2):
        link(nc.vector.tensor_add(out[:, r], out[:, r], t[:, r]))


def stage_ssm_tables(c):
    nc, ps = c.nc, c.psum
    dram = c.dram
    loaded, b_loaded = c.sem("st_loaded"), c.sem("st_b_loaded")
    turned, rows_ready, trig = c.sem("st_turned"), c.sem("st_rows_ready"), c.sem("st_trig")
    act_sem, c_turned, c_kept = c.sem("st_act"), c.sem("st_c_turned"), c.sem("st_c_kept")
    v_ready, v_turned, v_kept = c.sem("st_v_ready"), c.sem("st_v_turned"), c.sem("st_v_kept")
    m_ready, k_done, k_kept, k_written = c.sem("st_m_ready"), c.sem("st_k_done"), c.sem("st_k_kept"), c.sem("st_k_written")
    cos_sem = c.sem("st_cos")
    with ExitStack() as mine:
        def buf(name, shape):
            return c.buf("st_" + name, shape, ctx=mine)
        ag, ap_ = buf("a_g", [G, 2, 2, NS]), buf("a_p", [GP, 2, P])
        zg, zp = buf("z_g", [G, 2, 2, NS]), buf("z_p", [GP, 2, P])
        dg, dp = buf("dt_g", [G, 1]), buf("dt_p", [GP, 2])
        z = buf("z", [P, 2, A_COLS])
        al = buf("alpha", [P, 2, G])
        s1, s2, s3, s4 = (buf(f"s{i}", [P, A_COLS]) for i in range(4))
        ki = c.buf("st_ki", [P, A_COLS], I32, ctx=mine)
        f = buf("f", [P, 2, G])
        crow = buf("c_rows", [P, KD, 2, 2, NS])
        cx, cy = buf("cx", [P, G, CH]), buf("cy", [P, G, CH])
        bx, by = buf("bx", [P, G, CH]), buf("by", [P, G, CH])
        bbx, bby = buf("bbx", [P, G, 2 * CH]), buf("bby", [P, G, CH])
        tmp = buf("tmp", [P, G, CH])
        kz = buf("kz", [P, G // 4, (2 * L - 1) * CH])
        v = buf("v", [P, 8, L, CH])
        pw = buf("pw", [P, 2, L + 1, A_COLS])

        def wide(x, n=G):
            return x.unsqueeze(2).to_broadcast([P, n, CH])

        with nc.Block() as block:
            @block.sync
            def _(sp):
                for i, name in enumerate(("s5_a_re", "s5_a_im")):
                    a = dram[name][0]
                    for d in range(2):
                        sp.dma_start(ag[:, i, d], a).then_inc(loaded, 16)
                    sp.dma_start(ap_[:, i], a.rearrange("(q w) n -> q (w n)", w=2)).then_inc(loaded, 16)
                sp.dma_start(dg[:], dram["s5_log_dt"].rearrange("o g -> g o")).then_inc(loaded, 16)
                sp.dma_start(dp[:], dram["s5_log_dt"].rearrange("o (q w) -> q (o w)", w=2)).then_inc(loaded, 16)
                for i, name in enumerate(("s5_c_re", "s5_c_im")):
                    cc = dram[name][0].rearrange("(k g) c n -> (g c) k n", k=KD)
                    sp.dma_start(crow[:, :, 0, i], cc).then_inc(loaded, 16)
                    sp.dma_start(crow[:, :, 1, 1 - i], cc).then_inc(loaded, 16)
                for i, name in enumerate(("s5_b_re", "s5_b_im")):
                    bb = dram[name][0].rearrange("g n c -> n g c")
                    sp.dma_start(bx[i * NS:(i + 1) * NS], bb).then_inc(b_loaded, 16)
                    sp.dma_start(by[(1 - i) * NS:(2 - i) * NS], bb).then_inc(b_loaded, 16)
                sp.wait_ge(k_kept, 4)
                for q in range(4):
                    sp.dma_start(c.scratch_k.rearrange("(j q) c x -> q c j x", q=4)[q], kz[32 * q:32 * q + CH]).then_inc(k_written, 16)
                sp.wait_ge(k_written, 64)

            @block.scalar
            def _(act):
                act.wait_ge(loaded, 16 * 12)
                nc.scalar.activation(dg[:], dg[:], ACT.Exp).then_inc(act_sem, 1)
                nc.scalar.activation(dp[:], dp[:], ACT.Exp).then_inc(act_sem, 1)
                act.wait_ge(trig, 1)
                nc.scalar.activation(s2[:], s2[:], ACT.Sin).then_inc(cos_sem, 1)
                act.wait_ge(trig, 2)
                nc.scalar.activation(s3[:], s3[:], ACT.Sin).then_inc(cos_sem, 1)

            @block.tensor
            def _(pe):
                pe.wait_ge(rows_ready, 1)
                for i in range(2):
                    nc.tensor.transpose(ps[:, 0, i * P:i * P + G], zg[:, i].rearrange("g d n -> g (d n)"), c.ident[0:G, 0:G])
                    nc.tensor.transpose(ps[:, 0, i * P + G:i * P + A_COLS], zp[:, i], c.ident[0:GP, 0:GP])
                    mm = nc.tensor.transpose(ps[:, 0, 2 * P + i * G:2 * P + (i + 1) * G], ag[:, i].rearrange("g d n -> g (d n)"), c.ident[0:G, 0:G])
                mm.then_inc(turned, 1)
                for w in range(2):
                    for k in range(KD):
                        mm = nc.tensor.transpose(ps[:, 1 + w * 2 + k // 4, k % 4 * P:(k % 4 + 1) * P],
                                                 crow[:, k, w].rearrange("p i n -> p (i n)"), c.ident[:])
                    mm.then_inc(c_turned, 1)
                for k in range(KD):
                    pe.wait_ge(v_ready, k + 1)
                    for g in range(8):
                        if g % 4 == 0 and k * 2 + g // 4 >= 2:
                            pe.wait_ge(v_kept, k * 2 + g // 4 - 1)
                        mm = nc.tensor.transpose(ps[:, 5 + g // 4, g % 4 * P:(g % 4 + 1) * P],
                                                 v[:, g].rearrange("p e c -> p (e c)"), c.ident[:])
                        if g % 4 == 3:
                            mm.then_inc(v_turned, 1)
                pe.wait_ge(m_ready, 1)
                pe.wait_ge(c_kept, 4)
                for g in range(G):
                    q, j = g % 4, g // 4
                    mm = nc.tensor.matmul(ps[32 * q:32 * q + 32, j // 4, j % 4 * P:(j % 4 + 1) * P], bbx[:, g],
                                          c.mx[:, g, 0:L].rearrange("p e c -> p (e c)"), start=True, stop=True)
                    if g % 16 == 15:
                        mm.then_inc(k_done, 1)

            @block.vector
            def _(dve):
                link = Chain(c, dve, "st_link")
                ve = nc.vector
                dve.wait_ge(act_sem, 2)
                for i in range(2):
                    link(ve.tensor_scalar(zg[:, i], ag[:, i], dg[:, 0:1], None, ALU.mult))
                    for w in range(2):
                        link(ve.tensor_scalar(zp[:, i, w * NS:(w + 1) * NS], ap_[:, i, w * NS:(w + 1) * NS], dp[:, w:w + 1], None, ALU.mult))
                dve.sem_inc(rows_ready, 1)
                dve.wait_ge(turned, 1)
                link(ve.tensor_copy(z[:], ps[:, 0, 0:2 * P].rearrange("p (i x) -> p i x", i=2)[:, :, 0:A_COLS]))
                link(ve.tensor_copy(al[:], ps[:, 0, 2 * P:2 * P + 2 * G].rearrange("p (i x) -> p i x", i=2)))
                for shift, out in ((0.0, s2), (0.25, s3)):
                    link(ve.tensor_scalar(s1[:], z[:, 1], 1.0 / TWO_PI, shift, ALU.mult, ALU.add))
                    link(ve.tensor_scalar(s1[:], s1[:], MAGIC, None, ALU.add))
                    link(ve.tensor_scalar(s1[:], s1[:], -MAGIC, None, ALU.add))
                    src = z[:, 1]
                    for part in split(TWO_PI, 3):
                        link(ve.scalar_tensor_tensor(out[:], s1[:], -part, src, ALU.mult, ALU.add))
                        src = out[:]
                    link(ve.tensor_scalar(out[:], out[:], shift * TWO_PI, float(np.float32(3.1415925)), ALU.add, ALU.min))
                    ve.tensor_scalar(out[:], out[:], -float(np.float32(3.1415925)), None, ALU.max).then_inc(trig, 1)
                    dve.wait_ge(trig, 1 if out is s2 else 2)
                link(ve.tensor_scalar(s1[:], z[:, 0], float(1.0 / np.log(2.0)), MAGIC, ALU.mult, ALU.add))
                link(ve.tensor_scalar(s1[:], s1[:], -MAGIC, None, ALU.add))
                link(ve.tensor_scalar(s1[:], s1[:], -126.0, 127.0, ALU.max, ALU.min))
                src = z[:, 0]
                for part in split(float(np.log(2.0)), 3):
                    link(ve.scalar_tensor_tensor(s4[:], s1[:], -part, src, ALU.mult, ALU.add))
                    src = s4[:]
                link(ve.tensor_scalar(ki[:], s1[:], 127.0, None, ALU.add))
                link(ve.tensor_scalar(ki[:], ki[:], 23, None, ALU.logical_shift_left))
                fact = [1.0]
                for i in range(1, 10):
                    fact.append(fact[-1] * i)
                link(ve.tensor_scalar(s1[:], s4[:], 1.0 / fact[9], None, ALU.mult))
                for i in range(8, 0, -1):
                    link(ve.scalar_tensor_tensor(s1[:], s1[:], 1.0 / fact[i], s4[:], ALU.add, ALU.mult))
                link(ve.tensor_scalar(s1[:], s1[:], 1.0, None, ALU.add))
                link(ve.tensor_mul(s1[:], s1[:], ki[:].bitcast(F32)))
                link(ve.memset(pw[:, 0, 0], 1.0))
                link(ve.memset(pw[:, 1, 0], 0.0))
                dve.wait_ge(cos_sem, 2)
                link(ve.tensor_mul(pw[:, 0, 1], s1[:], s3[:]))
                link(ve.tensor_mul(pw[:, 1, 1], s1[:], s2[:]))

                def power(out, x, y):
                    w = out.shape[-1]
                    link(ve.tensor_mul(s1[:, 0:w], x[:, 0], y[:, 0]))
                    link(ve.tensor_mul(s4[:, 0:w], x[:, 1], y[:, 1]))
                    link(ve.tensor_sub(out[:, 0], s1[:, 0:w], s4[:, 0:w]))
                    link(ve.tensor_mul(s1[:, 0:w], x[:, 0], y[:, 1]))
                    link(ve.tensor_mul(s4[:, 0:w], x[:, 1], y[:, 0]))
                    link(ve.tensor_add(out[:, 1], s1[:, 0:w], s4[:, 0:w]))
                for e in range(2, L + 1):
                    power(pw[:, :, e], pw[:, :, e - 1], pw[:, :, 1])
                pair = slice(G, A_COLS)
                link(ve.tensor_copy(c.a1p[:, 0:2], pw[:, :, 1, pair]))
                link(ve.tensor_copy(c.a8p[:, 0:2, 0], pw[:, :, L, pair]))
                for j in range(1, SUP):
                    power(c.a8p[:, 0:2, j], c.a8p[:, 0:2, j - 1], c.a8p[:, 0:2, 0])
                link(ve.tensor_scalar(c.a1p[:, 2], c.a1p[:, 1], -1.0, None, ALU.mult))
                link(ve.tensor_scalar(c.a8p[:, 2], c.a8p[:, 1], -1.0, None, ALU.mult))
                x, y = al[:, 0], al[:, 1]
                n1, n2, den, t = s1[:, 0:G], s2[:, 0:G], s3[:, 0:G], s4[:, 0:G]
                link(ve.tensor_mul(den, x, x))
                link(ve.tensor_mul(t, y, y))
                link(ve.tensor_add(den, den, t))
                link(ve.reciprocal(den, den))
                link(ve.tensor_scalar(n1, pw[:, 0, 1, 0:G], -1.0, None, ALU.add))
                link(ve.tensor_mul(n2, n1, x))
                link(ve.tensor_mul(t, pw[:, 1, 1, 0:G], y))
                link(ve.tensor_add(n2, n2, t))
                link(ve.tensor_mul(f[:, 0], n2, den))
                link(ve.tensor_mul(n2, pw[:, 1, 1, 0:G], x))
                link(ve.tensor_mul(t, n1, y))
                link(ve.tensor_sub(n2, n2, t))
                link(ve.tensor_mul(f[:, 1], n2, den))
                for w in range(2):
                    dve.wait_ge(c_turned, w + 1)
                    for h in range(2):
                        dst, bank = (cx, cy)[w][:, h * 32:(h + 1) * 32], ps[:, 1 + w * 2 + h, :].rearrange("p (g c) -> p g c", c=CH)
                        if w == 0:
                            ve.tensor_scalar(dst, bank, c.sign[:, 0:1], None, ALU.mult).then_inc(c_kept, 1)
                        else:
                            ve.tensor_scalar(dst, bank, -1.0, None, ALU.mult).then_inc(c_kept, 1)
                dve.wait_ge(c_kept, 4)
                dve.wait_ge(b_loaded, 64)
                link(ve.memset(bbx[:], 0.0))
                link(ve.memset(kz[:], 0.0))
                link(ve.tensor_scalar(by[:], by[:], c.sign[:, 0:1], -1.0, ALU.mult, ALU.mult))
                link(ve.tensor_mul(tmp[:], by[:], wide(f[:, 1])))
                link(ve.tensor_mul(bbx[:, :, 0:CH], bx[:], wide(f[:, 0])))
                link(ve.tensor_add(bbx[:, :, 0:CH], bbx[:, :, 0:CH], tmp[:]))
                link(ve.tensor_mul(tmp[:], bx[:], wide(f[:, 1])))
                link(ve.tensor_mul(bby[:], by[:], wide(f[:, 0])))
                link(ve.tensor_sub(bby[:], bby[:], tmp[:]))
                link(ve.tensor_copy(c.mx[:, :, 0, :], cx[:]))
                for e in range(1, L + 1):
                    link(ve.tensor_mul(c.mx[:, :, e, :], cx[:], wide(pw[:, 0, e, 0:G])))
                    link(ve.tensor_mul(tmp[:], cy[:], wide(pw[:, 1, e, 0:G])))
                    link(ve.tensor_add(c.mx[:, :, e, :], c.mx[:, :, e, :], tmp[:]))
                dve.sem_inc(m_ready, 1)
                for k in range(KD):
                    gs = slice(k * 8, k * 8 + 8)
                    if k >= 1:
                        dve.wait_ge(v_turned, 2 * k)
                    link(ve.tensor_copy(v[:, :, 0, :], bbx[:, gs, 0:CH]))
                    for e in range(1, L):
                        link(ve.tensor_mul(v[:, :, e, :], bbx[:, gs, 0:CH], wide(pw[:, 0, e, gs], 8)))
                        link(ve.tensor_mul(tmp[:, 0:8], bby[:, gs], wide(pw[:, 1, e, gs], 8)))
                        link(ve.tensor_add(v[:, :, e, :], v[:, :, e, :], tmp[:, 0:8]))
                    dve.sem_inc(v_ready, 1)
                    for h in range(2):
                        dve.wait_ge(v_turned, 2 * k + h + 1)
                        ve.tensor_copy(c.wb[:, k * 8 + h * 4:k * 8 + h * 4 + 4, :],
                                       ps[:, 5 + h, :].rearrange("p (g x) -> p g x", g=4)).then_inc(v_kept, 1)
                for j in range(4):
                    dve.wait_ge(k_done, j + 1)
                    for q in range(4):
                        ins = ve.tensor_copy(kz[32 * q:32 * q + CH, 4 * j:4 * j + 4, (L - 1) * CH:],
                                             ps[32 * q:32 * q + CH, j, :].rearrange("p (g x) -> p g x", g=4))
                    ins.then_inc(k_kept, 1)


def stage_ssm(c):
    nc, ps = c.nc, c.psum
    dram = c.dram
    sent, back = c.sem("ss_u_sent"), [c.sem(f"ss_u_back{k}") for k in range(KD)]
    cleared, laid = c.sem("ss_cleared"), c.sem("ss_laid")
    xd, xk = c.sem("ss_x_done"), c.sem("ss_x_kept")
    s_in, s_turned, s_kept = c.sem("ss_state_in"), c.sem("ss_state_turned"), c.sem("ss_state_kept")
    with ExitStack() as mine:
        def buf(name, shape, ctx=mine):
            return c.buf("ss_" + name, shape, ctx=ctx)
        ut = buf("ut", [P, G, COLS])
        x = buf("x", [P, 2, GP, COLS])
        h0 = buf("h0", [P, 2, GP, NB])
        with ExitStack() as here:
            xc = buf("xc", [P, KD, L, COLS], here)
            srow = buf("state_rows", [GP, 2 * NB, P], here)
            with nc.Block() as block:
                @block.vector
                def _(dve):
                    nc.vector.memset(xc[:], 0.0).then_inc(cleared, 1)
                    dve.wait_ge(cleared, 1)
                    for k in range(KD):
                        for e in range(L):
                            nc.vector.tensor_copy(xc[:, k, e, 0:NCH],
                                                  c.xT[:, k, 0:SEQ].rearrange("p (n t) -> p t n", t=L)[:, L - 1 - e, :])
                        nc.vector.tensor_copy(xc[:, k, L - 1, NCH:NCH + NB], c.xT[:, k, SEQ:T])
                        nc.vector.tensor_copy(xc[:, k, 0, NCH + NB:], c.xT[:, k, SEQ:T])
                        dve.drain().then_inc(laid, 1)
                    dve.wait_ge(s_turned, 1)
                    nc.vector.tensor_copy(h0[:], ps[:, 7, :].rearrange("p (b i q) -> p i q b", i=2, q=GP)).then_inc(s_kept, 1)
                    for k in range(KD):
                        for par in range(2):
                            dve.wait_ge(xd, k + 1)
                            src = ps[0:NS, k % 3 * 2:k % 3 * 2 + 2, 0:4 * COLS].rearrange("p b (q w x) -> p b q w x", q=2, w=2)
                            for b in range(2):
                                ins = nc.vector.tensor_copy(x[par * NS:(par + 1) * NS, 0, k * 4 + b * 2:k * 4 + b * 2 + 2, :], src[:, b, :, par, :])
                        ins.then_inc(xk, 1)

                @block.scalar
                def _(act):
                    for k in range(KD):
                        for par in range(2):
                            act.wait_ge(xk, k + 1)
                            src = ps[NS:P, k % 3 * 2:k % 3 * 2 + 2, 0:4 * COLS].rearrange("p b (q w x) -> p b q w x", q=2, w=2)
                            for b in range(2):
                                ins = nc.scalar.copy(x[par * NS:(par + 1) * NS, 1, k * 4 + b * 2:k * 4 + b * 2 + 2, :], src[:, b, :, par, :])
                        ins.then_inc(cleared, 1)

                @block.sync
                def _(sp):
                    sp.dma_start(srow[:], dram["state_ssm"][0].rearrange("b i (q w) n -> q (b i) (w n)", w=2)).then_inc(s_in, 16)
                    for k in range(KD):
                        sp.wait_ge(laid, k + 1)
                        sp.dma_start(c.scratch_u[k], xc[:, k]).then_inc(sent, 16)
                        sp.wait_ge(sent, 16 * (k + 1))
                        for e in range(L):
                            sp.dma_start(ut[e * CH:(e + 1) * CH, k * 8:(k + 1) * 8, :],
                                         c.scratch_u[k].rearrange("(g c) e x -> e c g x", c=CH)[e]).then_inc(back[k], 16)

                @block.tensor
                def _(pe):
                    pe.wait_ge(s_in, 16)
                    for i in range(2 * NB):
                        mm = nc.tensor.transpose(ps[:, 7, i * GP:(i + 1) * GP], srow[:, i, :], c.ident[0:GP, 0:GP])
                    mm.then_inc(s_turned, 1)
                    for k in range(KD):
                        pe.wait_ge(back[k], 16 * L)
                        if k >= 3:
                            pe.wait_ge(cleared, 1 + k - 2)
                        for g in range(8):
                            mm = nc.tensor.matmul(ps[:, k % 3 * 2 + g // 4, g % 4 * COLS:(g % 4 + 1) * COLS],
                                                  c.wb[:, k * 8 + g, :], ut[:, k * 8 + g, :], start=True, stop=True)
                        mm.then_inc(xd, 1)

        with ExitStack() as here:
            ta, tb = buf("ta", [P, 2, GP, SUP], here), buf("tb", [P, 2, GP, SUP], here)
            with nc.Block() as block:
                @block.vector
                def _(dve):
                    link = Chain(c, dve, "ss_link")
                    xs = x[:, :, :, 0:NCH].rearrange("p i q (s j) -> p i q s j", j=SUP)

                    def axpy(out, src, table, w):
                        def t3(i):
                            return table[:, i].unsqueeze(2).to_broadcast([P, GP, w])
                        complex_axpy(nc, link, out, src, t3(0), t3(2), t3(1), ta[:, :, :, 0:w], tb[:, :, :, 0:w])
                    for j in range(1, SUP):
                        axpy(xs[:, :, :, :, j], xs[:, :, :, :, j - 1], c.a8p[:, :, 0], SUP)
                    for s in range(1, SUP):
                        axpy(xs[:, :, :, s:s + 1, SUP - 1], xs[:, :, :, s - 1:s, SUP - 1], c.a8p[:, :, SUP - 1], 1)
                    for j in range(SUP - 1):
                        axpy(xs[:, :, :, 1:, j], xs[:, :, :, 0:SUP - 1, SUP - 1], c.a8p[:, :, j], SUP - 1)
                    axpy(x[:, :, :, NCH + NB:], h0[:], c.a1p, NB)

        hx_done, y_done, y_kept, y_sent = c.sem("ss_hx_done"), c.sem("ss_y_done"), c.sem("ss_y_kept"), c.sem("ss_y_sent")
        y_back, t_in, skipped, st_done = [c.sem(f"ss_y_back{i}") for i in range(2)], [c.sem(f"ss_t_in{i}") for i in range(2)], c.sem("ss_skipped"), c.sem("ss_st_done")
        st_kept, st_out, zeroed, hi_done = c.sem("ss_st_kept"), c.sem("ss_st_out"), c.sem("ss_zeroed"), c.sem("ss_hx_im_done")
        with ExitStack() as here:
            hx = buf("hx", [P, 2, 8, HCOLS], here)
            tg = buf("tg", [P, 2, 8, P], here)
            yt = buf("yt", [P, 2, 8, HCOLS], here)
            yc = buf("yc", [P, 2, L, HCOLS], here)
            orow = buf("out_rows", [GP, 2 * NB + 2, P], here)
            with nc.Block() as block:
                @block.sync
                def _(sp):
                    def load_t(k):
                        for e in range(L):
                            sp.dma_start(tg[e * CH:(e + 1) * CH, k % 2],
                                         c.scratch_k[k * 8:(k + 1) * 8, :, e * CH:e * CH + P].rearrange("g c x -> c g x")).then_inc(t_in[k % 2], 16)
                    load_t(0)
                    load_t(1)
                    for k in range(KD):
                        sp.wait_ge(y_kept, 2 * (k + 1))
                        for t in range(L):
                            sp.dma_start(c.scratch_y[k].rearrange("(g c) t x -> t c g x", c=CH)[t], yt[t * CH:(t + 1) * CH, k % 2]).then_inc(y_sent, 16)
                        if k + 2 < KD:
                            load_t(k + 2)
                        sp.wait_ge(y_sent, 16 * L * (k + 1))
                        if k >= 2:
                            sp.wait_ge(skipped, k - 1)
                        sp.dma_start(yc[:, k % 2], c.scratch_y[k]).then_inc(y_back[k % 2], 16)
                    sp.wait_ge(st_kept, 5)
                    sp.dma_start(dram["ssm_sample"][0].rearrange("b i (q w) n -> q (b i) (w n)", w=2), orow[:, 0:2 * NB]).then_inc(st_out, 16)
                    sp.dma_start(dram["ssm_prompt"][0, 0].rearrange("i (q w) n -> q i (w n)", w=2), orow[:, 2 * NB:]).then_inc(st_out, 16)
                    sp.wait_ge(st_out, 32)

                @block.vector
                def _(dve):
                    nc.vector.memset(hx[:], 0.0).then_inc(zeroed, 1)
                    dve.wait_ge(zeroed, 1)

                    def skip(k):
                        dve.wait_ge(y_back[k % 2], 16 * (k // 2 + 1))
                        col = c.cols[:, k:k + 1]
                        nc.vector.scalar_tensor_tensor(c.y[:, k, 0:SEQ].rearrange("p (n t) -> p t n", t=L),
                                                       c.xT[:, k, 0:SEQ].rearrange("p (n t) -> p t n", t=L), col,
                                                       yc[:, k % 2, :, 0:NCH], ALU.mult, ALU.add)
                        nc.vector.scalar_tensor_tensor(c.y[:, k, SEQ:T], c.xT[:, k, SEQ:T], col, yc[:, k % 2, 0, NCH:],
                                                       ALU.mult, ALU.add).then_inc(skipped, 1)

                    for k in range(KD):
                        if k >= 2:
                            dve.wait_ge(y_done, 2 * (k - 1))
                        for i in range(2):
                            for par in range(2):
                                rows = slice(par * NS, (par + 1) * NS)
                                dst = hx[i * NS:(i + 1) * NS, k % 2].rearrange("p (q w) x -> p w q x", w=2)[:, par]
                                nc.vector.tensor_copy(dst[:, :, 1:NCH], x[rows, i, k * 4:k * 4 + 4, 0:NCH - 1])
                                ins = nc.vector.tensor_copy(dst[:, :, NCH:], h0[rows, i, k * 4:k * 4 + 4, :])
                        ins.then_inc(hx_done, 1)
                        if k >= 2:
                            skip(k - 2)
                    skip(KD - 2)
                    skip(KD - 1)
                    for n in range(5):
                        dve.wait_ge(st_done, n + 1)
                        w = 4 if n < 4 else 2
                        nc.vector.tensor_copy(orow[:, 4 * n:4 * n + w, :], ps[0:GP, 4 + n % 2, 0:w * P].rearrange("p (j x) -> p j x", x=P)).then_inc(st_kept, 1)

                @block.scalar
                def _(act):
                    for k in range(KD):
                        if k >= 2:
                            act.wait_ge(y_sent, 16 * L * (k - 1))
                        for h in range(2):
                            act.wait_ge(y_done, 2 * k + h + 1)
                            nc.scalar.copy(yt[:, k % 2, h * 4:h * 4 + 4, :],
                                           ps[:, k % 2 * 2 + h, 0:4 * HCOLS].rearrange("p (g x) -> p g x", g=4)).then_inc(y_kept, 1)

                @block.tensor
                def _(pe):
                    for k in range(KD):
                        pe.wait_ge(t_in[k % 2], 16 * L * (k // 2 + 1))
                        pe.wait_ge(hx_done, k + 1)
                        if k >= 2:
                            pe.wait_ge(y_kept, 2 * (k - 1))
                        for g in range(8):
                            out = ps[:, k % 2 * 2 + g // 4, g % 4 * HCOLS:(g % 4 + 1) * HCOLS]
                            nc.tensor.matmul(out, tg[:, k % 2, g, :], ut[:, k * 8 + g, 0:HCOLS], start=True, stop=False)
                            mm = nc.tensor.matmul(out, c.mx[:, k * 8 + g, 1:].rearrange("p e c -> p (e c)"), hx[:, k % 2, g, :],
                                                  start=False, stop=True)
                            if g % 4 == 3:
                                mm.then_inc(y_done, 1)
                    for n in range(5):
                        if n >= 2:
                            pe.wait_ge(st_kept, n - 1)
                        for j in range(4 if n < 4 else 2):
                            if n < 4:
                                b, i = divmod(n * 4 + j, 2)
                                src = x[:, i, :, NCH + NB + b]
                            else:
                                src = x[:, j, :, NCH - 1]
                            mm = nc.tensor.transpose(ps[0:GP, 4 + n % 2, j * P:(j + 1) * P], src, c.ident[:])
                        mm.then_inc(st_done, 1)


def stage_gelu(c, dst, src):
    nc = c.nc
    done = c.sem("gelu_done")
    with nc.Block() as block:
        @block.scalar
        def _(act):
            for k in range(KD):
                nc.scalar.activation(dst[:, k, :], src[:, k, :], ACT.Gelu_apprx_tanh).then_inc(done, 1)


def evac_glu(dst, y, bias):
    def make(c, name, filled, freed, per, iters, mine):
        nc, ps = c.nc, c.psum
        gated = c.sem(f"{name}_gated")
        tmp = c.buf(f"{name}_sig", [P, 4, HALF], ctx=mine)

        def act_prog(act):
            act.sem_inc(gated, 4)
            with act.Fori(0, iters) as it:
                for b in range(8 * per):
                    act.wait_ge(filled, it * (8 * per) + b + 1)
                    act.wait_ge(gated, it * (8 * per) + b + 1)
                    nc.scalar.activation(tmp[:, b % 4, :], ps[:, b % 8, 0:HALF], ACT.Sigmoid,
                                         bias=bias[:, bass.ds(it * (4 * per) + b // 2, 1)]).then_inc(freed[b % 2], 1)

        def dve_prog(dve):
            with dve.Fori(0, iters) as it:
                for b in range(8 * per):
                    m, h = b // 2, b % 2
                    dve.wait_ge(freed[h], it * (4 * per) + m + 5)
                    tile, cols = bass.ds(it * (4 * per) + m, 1), slice(h * HALF, (h + 1) * HALF)
                    nc.vector.tensor_mul(dst[:, tile, cols], y[:, tile, cols], tmp[:, b % 4:b % 4 + 1, :]).then_inc(gated, 1)
        return act_prog, dve_prog
    return make


def stage_cols(c):
    nc, ps = c.nc, c.psum
    got, turned, kept = c.sem("cols_in"), c.sem("cols_turned"), c.sem("cols_kept")
    with ExitStack() as mine:
        rows = c.buf("cols_rows", [2 * KD, P], ctx=mine)
        with nc.Block() as block:
            @block.sync
            def _(sp):
                for i, name in enumerate(("s5_d", "s5_b_glu")):
                    sp.dma_start(rows[i * KD:(i + 1) * KD], c.dram[name].rearrange("o (k p) -> (o k) p", p=P)).then_inc(got, 16)

            @block.tensor
            def _(pe):
                pe.wait_ge(got, 32)
                nc.tensor.transpose(ps[:, 0, 0:2 * KD], rows[:], c.ident[0:2 * KD, 0:2 * KD]).then_inc(turned, 1)

            @block.vector
            def _(dve):
                dve.wait_ge(turned, 1)
                nc.vector.tensor_copy(c.cols[:], ps[:, 0, 0:2 * KD]).then_inc(kept, 1)


def stage_s5(c):
    nc = c.nc
    c.scratch_k = nc.dram_tensor("scratch_k", (G, CH, (2 * L - 1) * CH), F32, kind="Internal").ap()
    c.scratch_u = nc.dram_tensor("scratch_u", (KD, P, L, COLS), F32, kind="Internal").ap()
    c.scratch_y = nc.dram_tensor("scratch_y", (KD, P, L, HCOLS), F32, kind="Internal").ap()
    with ExitStack() as outer:
        c.y = c.buf("ssm_y", [P, KD, T], ctx=outer)
        c.cols = c.buf("ssm_cols", [P, 2 * KD], ctx=outer)
        stage_cols(c)
        with ExitStack() as tables:
            c.wb = c.buf("wb", [P, G, P], ctx=tables)
            c.mx = c.buf("mx", [P, G, L + 1, CH], ctx=tables)
            c.a1p = c.buf("a1p", [P, 3, GP], ctx=tables)
            c.a8p = c.buf("a8p", [P, 3, SUP, GP], ctx=tables)
            stage_ssm_tables(c)
            stage_norm(c, "ssm_in", c.hT, c.xT, 1, 0)
            stage_ssm(c)
        stage_gelu(c, c.y, c.y)
        w = c.dram["s5_w_glu"][0].rearrange("(k p) n -> p k n", p=P)
        stage_linear(c, "glu", lambda g, ch: w[:, :, bass.ts(g, NG)], KD, D // NG, c.y, evac_glu(c.xT, c.y, c.cols[:, KD:]), per=2)
        stage_residual(c, "ssm_out", c.xT, 1, 1)


def program(nc, dram):
    with ExitStack() as ctx:
        c = Core(nc, ctx, dram)
        c.ident = c.buf("ident", [P, P])
        c.causal = c.buf("causal", [P, SEQ])
        c.cmask = c.buf("cmask", [P, 2 * GRP * QT * NCP])
        c.own = c.buf("own", [P, NB])
        c.group = c.buf("group", [P, P])
        c.over = c.buf("over", [P, NSEL])
        c.blk = c.buf("blk", [P, NSEL])
        c.sign = c.buf("sign", [P, 1])
        c.g_rows = c.buf("g_rows", [8 * KD, P])
        c.g_cols = c.buf("g_cols", [P, 8 * KD])
        c.ones = c.buf("ones", [P, P])
        c.eps = c.buf("eps", [P, 1])
        c.hT = c.buf("hT", [P, KD, T])
        c.xT = c.buf("xT", [P, KD, T])
        c.pages = c.buf("pages", [1, NB * NPAGE], I32)
        with c.part():
            stage_inputs(c)
        with c.part():
            stage_nsa(c)
        with c.part():
            stage_mlp(c, 0)
        with c.part():
            stage_s5(c)
        with c.part():
            stage_mlp(c, 1)
            stage_outputs(c)


OUTPUTS = [
    ("y_prompt", (1, SEQ, D)), ("y_sample", (NB, 1, D)),
    ("kv_cmp_prompt", (1, 1, SEQ, 2, NKV, HD)), ("kv_cmp_sample", (1, NB, 1, 2, NKV, HD)),
    ("kv_sel_prompt", (1, 1, SEQ, 2, NKV, HD)), ("kv_sel_sample", (1, NB, 1, 2, NKV, HD)),
    ("kv_win_prompt", (1, 1, WIN, 2, NKV, HD)), ("kv_win_sample", (1, NB, WIN, 2, NKV, HD)),
    ("ssm_prompt", (1, 1, 2, G, NS)), ("ssm_sample", (1, NB, 2, G, NS)),
]


def kernel(**inputs):
    import concourse.bacc as bacc
    from concourse.bass_utils import run_bass_kernel_spmd

    nc = bacc.Bacc("TRN2", target_bir_lowering=False, num_devices=1)
    arrays, dram = {}, {}
    for name, value in [*inputs.items(), *constants().items()]:
        a = np.ascontiguousarray(value)
        arrays[f"in_{name}"] = a
        dram[name] = nc.dram_tensor(f"in_{name}", a.shape, mybir.dt.from_np(a.dtype), kind="ExternalInput").ap()
    for name, shape in OUTPUTS:
        dram[name] = nc.dram_tensor(f"out_{name}", shape, F32, kind="ExternalOutput").ap()
    program(nc, dram)
    r = run_bass_kernel_spmd(nc, [arrays], core_ids=[0])
    return tuple(r.results[0][f"out_{name}"] for name, _ in OUTPUTS)
```

```python
from contextlib import ExitStack, contextmanager

import numpy as np

import concourse.bass as bass
from concourse import mybir

F32 = mybir.dt.float32
I32 = mybir.dt.int32
ACT = mybir.ActivationFunctionType
ALU = mybir.AluOpType
AX = mybir.AxisListType

P = 128
D = 1024
SEQ = 512
NB = 8
T = SEQ + NB
HALF = T // 2
KD = D // P
QT = SEQ // P
DFF = 4 * D
KF = DFF // P
NH, HD, NKV, GRP = 16, 64, 4, 4
KVW = NKV * HD
ROW = 2 * KVW
PAST, PAGE = 1024, 128
NPAGE = PAST // PAGE
POOL_PAGES = (5 * NB * NPAGE + 3) // 4
WIN = 512
STRIDE = 16
NSUB = PAST // STRIDE
NCS = NSUB - 1
NSUBP = SEQ // STRIDE
NCP = NSUBP - 1
SELB = 64
NSEL = PAST // SELB + 1
SPAIR = STRIDE // 2
SCALE = HD ** -0.5
EPS = 1e-6
BIG = 1e30
G, CH, NS = 64, 16, 64
GP = G // 2
L = 8
NCH = SEQ // L
SUP = 8


def constants():
    half = HD // 2
    inv = (np.float32(10000.0) ** (-np.arange(half, dtype=np.float32) / np.float32(half))).astype(np.float32)
    pos = np.concatenate([np.arange(SEQ), np.full(NB, PAST)]).astype(np.float32)
    ang = pos[:, None] * inv[None, :]
    cos, sin = np.cos(ang).astype(np.float32), np.sin(ang).astype(np.float32)
    rows = np.zeros((P, QT + 1, 2, half), np.float32)
    for t in range(QT + 1):
        n = P if t < QT else NB
        rows[:n, t, 0], rows[:n, t, 1] = cos[t * P:t * P + n], sin[t * P:t * P + n]
    cos_t = np.tile(cos.T, (4, 1))
    sin_t = np.tile(np.concatenate([-sin.T, sin.T]), (2, 1))
    swap = np.zeros((P, P), np.float32)
    for m in range(P):
        swap[m // HD * HD + (m % HD + half) % HD, m] = 1.0
    q = np.arange(P)
    causal = np.where(np.arange(SEQ)[None, :] - (SEQ - P) > q[:, None], BIG, 0.0).astype(np.float32)
    qpos = (np.arange(QT)[None, :] * P + q[:, None])[:, None, :, None]
    cend = (np.arange(NCP) * STRIDE + 2 * STRIDE - 1)[None, None, None, :]
    seen = np.broadcast_to(cend <= qpos, (P, GRP, QT, NCP))
    cmask = np.stack([np.where(seen, 0.0, BIG), seen.astype(np.float32)], 1).astype(np.float32)
    row_b = np.arange(P) // NH
    own = np.where(row_b[:, None] == np.arange(NB)[None, :], 0.0, BIG).astype(np.float32)
    group = (np.arange(P)[:, None] // GRP == np.arange(P)[None, :] // GRP).astype(np.float32)
    c0, s0 = np.arange(NCS) * STRIDE, np.arange(NSEL) * SELB
    over = np.zeros((P, NSEL), np.float32)
    over[:NCS] = (c0[:, None] < s0[None] + SELB) & (c0[:, None] + 2 * STRIDE > s0[None])
    blk = np.broadcast_to(np.arange(NSEL, dtype=np.float32), (P, NSEL))
    sign = np.where(np.arange(P) < NS, 1.0, -1.0).astype(np.float32)[:, None]
    return {
        "c_ident": np.eye(P, dtype=np.float32), "c_swap": swap, "c_ropeT": np.stack([cos_t, sin_t], 1),
        "c_rope": rows, "c_causal": causal, "c_cmask": cmask.reshape(P, -1), "c_own": own,
        "c_group": group, "c_over": over, "c_blk": np.ascontiguousarray(blk), "c_sign": sign,
    }


class Core:

    def __init__(self, nc, ctx, dram):
        self.nc, self.ctx, self.dram, self.sems = nc, ctx, dram, []
        self.psum = ctx.enter_context(nc.psum_tensor("psum", [P, 8, 512], F32))

    def buf(self, name, shape, dt=F32, ctx=None):
        return (ctx or self.ctx).enter_context(self.nc.sbuf_tensor(name, shape, dt))

    def sem(self, name):
        self.sems.append(self.nc.alloc_semaphore(name=name))
        return self.sems[-1]

    @contextmanager
    def part(self):
        self.sems = []
        yield
        self.nc.clear_and_free_semaphores(self.sems)
        self.nc.all_engine_barrier()


def rows_of(t):
    return P if t < QT else NB


def stage_inputs(c):
    nc, ps = c.nc, c.psum
    tables, loaded, x_in = c.sem("tables_loaded"), c.sem("const_loaded"), [c.sem(f"x_in{t}") for t in range(QT + 1)]
    turned, kept = c.sem("x_turned"), c.sem("x_kept")
    preset = c.sem("x_preset")
    with ExitStack() as mine:
        xr = c.buf("x_rows", [P, QT + 1, D], ctx=mine)
        with nc.Block() as block:
            @block.sync
            def _(sp):
                sp.dma_start(c.ident[:], c.dram["c_ident"]).then_inc(loaded, 16)
                sp.dma_start(c.g_rows[:], c.dram["norm_g"].rearrange("l w (k p) -> (l w k) p", p=P)).then_inc(loaded, 16)
                for t in range(QT):
                    sp.dma_start(xr[:, t, :], c.dram["x_prompt"][0, t * P:(t + 1) * P, :]).then_inc(x_in[t], 16)
                sp.dma_start(xr[0:NB, QT, :], c.dram["x_sample"][:, 0, :]).then_inc(x_in[QT], 16)
                for b, name in ((c.causal[:], "c_causal"), (c.cmask[:], "c_cmask"), (c.own[:], "c_own"),
                                (c.group[:], "c_group"), (c.over[:], "c_over"), (c.blk[:], "c_blk"),
                                (c.sign[:], "c_sign")):
                    sp.dma_start(b, c.dram[name]).then_inc(tables, 16)
                sp.dma_start(c.pages[:], c.dram["page_table"].rearrange("b p -> (b p)")[None, :]).then_inc(tables, 16)
                sp.wait_ge(tables, 16 * 8)

            @block.tensor
            def _(pe):
                pe.wait_ge(loaded, 32)
                for i in range(2 * (QT + 1)):
                    t, kk = i // 2, i % 2
                    n = rows_of(t)
                    if kk == 0:
                        pe.wait_ge(x_in[t], 16)
                    if i >= 4:
                        pe.wait_ge(kept, i - 3)
                    for k in range(4):
                        last = nc.tensor.transpose(ps[:, i % 4, k * P:k * P + n],
                                                   xr[0:n, t, (kk * 4 + k) * P:(kk * 4 + k + 1) * P],
                                                   c.ident[0:n, 0:n])
                    last.then_inc(turned, 1)
                nc.tensor.transpose(ps[:, 4, 0:8 * KD], c.g_rows[:], c.ident[0:8 * KD, 0:8 * KD]).then_inc(turned, 1)

            @block.vector
            def _(dve):
                nc.vector.memset(c.ones[:], 1.0 / D).then_inc(preset, 1)
                nc.vector.memset(c.eps[:], EPS).then_inc(preset, 1)
                for i in range(2 * (QT + 1)):
                    t, kk = i // 2, i % 2
                    n = rows_of(t)
                    dve.wait_ge(turned, i + 1)
                    nc.vector.tensor_copy(c.hT[:, kk * 4:kk * 4 + 4, t * P:t * P + n],
                                          ps[:, i % 4, :].rearrange("p (k t) -> p k t", k=4)[:, :, 0:n]).then_inc(kept, 1)
                dve.wait_ge(turned, 2 * (QT + 1) + 1)
                nc.vector.tensor_copy(c.g_cols[:], ps[:, 4, 0:8 * KD]).then_inc(kept, 1)


def rms_parts(c, name, src, sq, rs, src_ready=lambda eng: None):
    nc, ps = c.nc, c.psum
    squared, added, summed, rooted, ready = (c.sem(f"{name}_{x}") for x in ("squared", "added", "summed", "rooted", "ready"))
    rs = rs[:]

    def act_part(act):
        src_ready(act)
        for k in range(KD):
            if k >= 4:
                act.wait_ge(added, k - 3)
            nc.scalar.activation(sq[:, 3 if k == 0 else (k - 1) % 3, :], src[:, k, :], ACT.Square).then_inc(squared, 1)
        act.wait_ge(summed, 1)
        for h in range(2):
            nc.scalar.activation(rs[:, h * HALF:(h + 1) * HALF], ps[:, h, 0:HALF], ACT.Sqrt, bias=c.eps[:]).then_inc(rooted, 1)

    def pe_part(pe):
        pe.wait_ge(added, KD - 1)
        for h in range(2):
            mm = nc.tensor.matmul(ps[:, h, 0:HALF], c.ones[:], sq[:, 3, h * HALF:(h + 1) * HALF], start=True, stop=True)
        mm.then_inc(summed, 1)

    def dve_part(dve):
        src_ready(dve)
        for k in range(1, KD):
            dve.wait_ge(squared, k + 1)
            if k >= 2:
                dve.wait_ge(added, k - 1)
            nc.vector.tensor_add(sq[:, 3, :], sq[:, 3, :], sq[:, (k - 1) % 3, :]).then_inc(added, 1)
        dve.wait_ge(summed, 1)
        dve.wait_ge(rooted, 2)
        nc.vector.reciprocal(rs, rs).then_inc(ready, 1)
        dve.wait_ge(ready, 1)
    return act_part, pe_part, dve_part


def norm_parts(c, name, src, dst, layer, which, sq, rs):
    nc = c.nc
    act_part, pe_part, rms_dve = rms_parts(c, name, src, sq, rs)
    done = c.sem(f"{name}_done")

    def dve_part(dve):
        rms_dve(dve)
        for k in range(KD):
            col = (layer * 4 + which) * KD + k
            nc.vector.scalar_tensor_tensor(dst[:, k, :], src[:, k, :], c.g_cols[:, col:col + 1], rs[:],
                                           ALU.mult, ALU.mult).then_inc(done, 1)
    return act_part, pe_part, dve_part, done


def residual_parts(c, name, y, layer, which, sq, rs, src_ready):
    nc = c.nc
    act_part, pe_part, rms_dve = rms_parts(c, name, y, sq, rs, src_ready)
    scaled, done = c.sem(f"{name}_scaled"), c.sem(f"{name}_done")

    def dve_part(dve):
        rms_dve(dve)
        for k in range(KD):
            col = (layer * 4 + which) * KD + k
            nc.vector.scalar_tensor_tensor(y[:, k, :], y[:, k, :], c.g_cols[:, col:col + 1], rs[:],
                                           ALU.mult, ALU.mult).then_inc(scaled, 1)

    def pool_part(pool):
        for k in range(KD):
            pool.wait_ge(scaled, k + 1)
            nc.gpsimd.tensor_add(c.hT[:, k, :], c.hT[:, k, :], y[:, k, :]).then_inc(done, 1)
    return act_part, pe_part, dve_part, pool_part


CK = 8
NG = 512


class Linear:

    def __init__(self, c, name, weights, kt, groups, per):
        self.c, self.name, self.weights, self.kt, self.groups, self.per = c, name, weights, kt, groups, per
        self.nchunk = kt // CK
        self.loads, self.ahead = groups * self.nchunk, 0
        self.landed = [c.sem(f"{name}_w_landed{s}") for s in range(2)]
        self.read, self.filled = c.sem(f"{name}_w_read"), c.sem(f"{name}_bank_filled")
        self.freed = [c.sem(f"{name}_even_bank_freed"), c.sem(f"{name}_odd_bank_freed")]
        assert per * self.nchunk % 2 == 0 and groups % per == 0

    def load(self, sp, j):
        self.c.nc.sync.dma_start(self.c.w[:, j % 2], self.weights(j // self.nchunk, j % self.nchunk)).then_inc(self.landed[j % 2], 16)

    def wait_read(self, sp, j):
        g, chunk = divmod(j, self.nchunk)
        if chunk == self.nchunk - 1:
            sp.wait_ge(self.filled, 8 * (g + 1))
        else:
            sp.wait_ge(self.read, g * (self.nchunk - 1) + chunk + 1)

    def evacuated(self, eng):
        for sem in self.last:
            eng.wait_ge(sem, 4 + 8 * self.groups // len(self.last))

    def run(self, x, evac, before=None, after=None, then=None):
        c, nc, ps = self.c, self.c.nc, self.c.psum
        name, kt, nchunk, per, filled, freed = self.name, self.kt, self.nchunk, self.per, self.filled, self.freed
        w, body = c.w, per * nchunk
        with ExitStack() as mine:
            act_evac, dve_evac, self.last = evac(c, name, filled, freed, per, self.groups // per, mine)
            with nc.Block() as block:
                @block.sync
                def _(sp):
                    for j in range(self.ahead, self.loads):
                        if j >= 2:
                            self.wait_read(sp, j - 2)
                        self.load(sp, j)
                    if then is not None:
                        for j in range(2):
                            self.wait_read(sp, self.loads - 2 + j)
                            then.load(sp, j)
                        then.ahead = 2

                @block.tensor
                def _(pe):
                    if before is not None:
                        before[1](pe)
                    pe.sem_inc(freed[0], 4)
                    pe.sem_inc(freed[1], 4)
                    with pe.Fori(0, self.groups // per) as it:
                        for j in range(body):
                            s, chunk = j % 2, j % nchunk
                            pe.wait_ge(self.landed[s], it * (16 * body // 2) + 16 * (j // 2 + 1))
                            for k in range(CK):
                                kk = chunk * CK + k
                                if before is not None and j == 0:
                                    pe.wait_ge(before[3], kk + 1)
                                for m in range(NG // P):
                                    for h in range(2):
                                        bank = m * 2 + h
                                        if kk == 0:
                                            pe.wait_ge(freed[h], it * (4 * per) + (j // nchunk) * 4 + m + 1)
                                        mm = nc.tensor.matmul(ps[:, bank, 0:HALF], w[:, s, k, m * P:(m + 1) * P],
                                                              x[:, kk, h * HALF:(h + 1) * HALF],
                                                              start=(kk == 0), stop=(kk == kt - 1))
                                        if kk == kt - 1:
                                            mm.then_inc(filled, 1)
                            if chunk < nchunk - 1:
                                mm.then_inc(self.read, 1)
                    if after is not None:
                        after[1](pe)

                @block.scalar
                def _(act):
                    if before is not None:
                        before[0](act)
                    act_evac(act)
                    if after is not None:
                        after[0](act)

                @block.vector
                def _(dve):
                    if before is not None:
                        before[2](dve)
                    dve_evac(dve)
                    if after is not None:
                        after[2](dve)

                if after is not None:
                    @block.gpsimd
                    def _(pool):
                        after[3](pool)


def evac_copy(dst):
    def make(c, name, filled, freed, per, iters, mine):
        nc, ps = c.nc, c.psum

        def program(eng, copy, h):
            with eng.Fori(0, iters) as it:
                for m in range(4 * per):
                    bank = (m % 4) * 2 + h
                    eng.wait_ge(filled, it * (8 * per) + 2 * m + h + 1)
                    copy(dst[:, bass.ds(it * (4 * per) + m, 1), h * HALF:(h + 1) * HALF],
                         ps[:, bank:bank + 1, 0:HALF]).then_inc(freed[h], 1)
        return (lambda act: program(act, nc.scalar.copy, 0)), (lambda dve: program(dve, nc.vector.tensor_copy, 1)), freed
    return make


def evac_sq_relu(dst):
    def make(c, name, filled, freed, per, iters, mine):
        nc, ps = c.nc, c.psum
        squared = c.sem(f"{name}_squared")
        tmp = c.buf(f"{name}_relu", [P, 4, HALF], ctx=mine)

        def act_prog(act):
            act.sem_inc(squared, 4)
            with act.Fori(0, iters) as it:
                for b in range(8 * per):
                    act.wait_ge(filled, it * (8 * per) + b + 1)
                    act.wait_ge(squared, it * (8 * per) + b + 1)
                    nc.scalar.activation(tmp[:, b % 4, :], ps[:, b % 8, 0:HALF], ACT.Relu).then_inc(freed[b % 2], 1)

        def dve_prog(dve):
            with dve.Fori(0, iters) as it:
                for b in range(8 * per):
                    m, h = b // 2, b % 2
                    dve.wait_ge(freed[h], it * (4 * per) + m + 5)
                    nc.vector.tensor_mul(dst[:, bass.ds(it * (4 * per) + m, 1), h * HALF:(h + 1) * HALF],
                                         tmp[:, b % 4:b % 4 + 1, :], tmp[:, b % 4:b % 4 + 1, :]).then_inc(squared, 1)
        return act_prog, dve_prog, [squared]
    return make


def stage_outputs(c):
    nc, ps = c.nc, c.psum
    turned, kept, out = c.sem("y_turned"), c.sem("y_kept"), c.sem("y_written")
    with ExitStack() as mine:
        yr = c.buf("y_rows", [P, QT + 1, D], ctx=mine)
        with nc.Block() as block:
            @block.tensor
            def _(pe):
                for i in range(2 * (QT + 1)):
                    t, kk = i // 2, i % 2
                    n = rows_of(t)
                    if i >= 4:
                        pe.wait_ge(kept, i - 3)
                    for k in range(4):
                        mm = nc.tensor.transpose(ps[0:n, i % 4, k * P:(k + 1) * P],
                                                 c.hT[:, kk * 4 + k, t * P:t * P + n], c.ident[:])
                    mm.then_inc(turned, 1)

            @block.vector
            def _(dve):
                for i in range(2 * (QT + 1)):
                    t, kk = i // 2, i % 2
                    n = rows_of(t)
                    dve.wait_ge(turned, i + 1)
                    nc.vector.tensor_copy(yr[0:n, t, kk * 512:kk * 512 + 512], ps[0:n, i % 4, :]).then_inc(kept, 1)

            @block.sync
            def _(sp):
                for t in range(QT + 1):
                    sp.wait_ge(kept, 2 * t + 2)
                    dst = c.dram["y_prompt"][0, t * P:(t + 1) * P, :] if t < QT else c.dram["y_sample"][:, 0, :]
                    sp.dma_start(dst, yr[0:rows_of(t), t, :]).then_inc(out, 16)
                sp.wait_ge(out, 16 * (QT + 1))


def columns(w):
    view = w.rearrange("(k p) n -> p k n", p=P)
    return lambda g, chunk: view[:, chunk * CK:(chunk + 1) * CK, bass.ts(g, NG)]


def stage_mix_out(c, lin, x, evac, y, layer, up):
    with ExitStack() as mine:
        sq, rs = c.buf(f"mix_sq{layer}", [P, 4, T], ctx=mine), c.buf(f"mix_rs{layer}", [P, T], ctx=mine)
        lin.run(x, evac, after=residual_parts(c, f"mix_out{layer}", y, layer, 1, sq, rs, lin.evacuated), then=up)


def stage_mlp(c, layer, up):
    with ExitStack() as mine:
        hid = c.buf(f"hidden{layer}", [P, KF, T], ctx=mine)
        sq, rs = c.buf(f"mlp_sq{layer}", [P, 4, T], ctx=mine), c.buf(f"mlp_rs{layer}", [P, T], ctx=mine)
        down = Linear(c, f"mlp_down{layer}", columns(c.dram["mlp_w2"][layer]), KF, D // NG, 1)
        up.run(c.xT, evac_sq_relu(hid), before=norm_parts(c, f"mlp_in{layer}", c.hT, c.xT, layer, 2, sq, rs), then=down)
        down.run(hid, evac_copy(c.xT), after=residual_parts(c, f"mlp_out{layer}", c.xT, layer, 3, sq, rs, down.evacuated))


def mlp_up(c, layer):
    return Linear(c, f"mlp_up{layer}", columns(c.dram["mlp_w1"][layer]), KD, DFF // NG, 2)


def stage_project(c, norm):
    nc, ps = c.nc, c.psum
    w_in = c.dram["nsa_w_in"][0].rearrange("(k p) n -> p k n", p=P)
    nblk = 5
    landed = [c.sem(f"proj_w_landed{s}") for s in range(2)]
    gate_landed, table_landed = c.sem("proj_gate_w_landed"), c.sem("proj_table_landed")
    block_read, filled, freed = c.sem("proj_block_read"), c.sem("proj_bank_filled"), c.sem("proj_bank_freed")
    q_kept, swapped, swap_freed, roped = (c.sem(f"proj_{x}") for x in ("q_kept", "q_swapped", "swap_freed", "q_roped"))
    t1_sem, link, gated, written = c.sem("proj_t1"), c.sem("proj_link"), c.sem("proj_gate_exp"), c.sem("proj_written")
    with ExitStack() as mine:
        w = c.buf("proj_w", [P, 2, KD, NG], ctx=mine)
        wg = c.buf("proj_gate_w", [P, KD, 3 * NH], ctx=mine)
        tmp = c.buf("proj_tmp", [P, T], ctx=mine)
        swap = c.buf("swap", [P, P], ctx=mine)
        rope_t = c.buf("rope_t", [P, 2, T], ctx=mine)
        rope = c.qz[:, 1, 1].rearrange("p b x -> p (b x)")[:, 0:(QT + 1) * HD].rearrange("p (t i d) -> p t i d", i=2, d=HD // 2)
        nq, nrow = 2 * KD, 3 * (QT + 1)
        with nc.Block() as block:
            @block.sync
            def _(sp):
                for b, name in ((swap, "c_swap"), (rope_t, "c_ropeT"), (rope, "c_rope")):
                    sp.dma_start(b[:], c.dram[name]).then_inc(table_landed, 16)
                for j in range(nblk):
                    if j >= 2:
                        sp.wait_ge(block_read, j - 1)
                    sp.dma_start(w[:, j % 2], w_in[:, :, bass.ts(j, NG)]).then_inc(landed[j % 2], 16)
                sp.dma_start(wg[:], w_in[:, :, nblk * NG:]).then_inc(gate_landed, 16)
                compress_first_loads(c, sp)
                names = ("kv_cmp", "kv_sel", "kv_win")
                for b in range(3):
                    for t in range(QT + 1):
                        sp.wait_ge(roped, 8 + b * (QT + 1) + t + 1)
                        if t < QT:
                            dst = c.dram[f"{names[b]}_prompt"][0, 0, t * P:(t + 1) * P].rearrange("t s h d -> t (s h d)")
                        elif b < 2:
                            dst = c.dram[f"{names[b]}_sample"][0, :, 0].rearrange("t s h d -> t (s h d)")
                        else:
                            dst = c.dram["kv_win_sample"][0, :, WIN - 1].rearrange("t s h d -> t (s h d)")
                        sp.dma_start(dst, c.kv[0:rows_of(t), t, b, :]).then_inc(written, 16)
                sp.wait_ge(written, 16 * nrow)

            @block.tensor
            def _(pe):
                step = 0

                def start_bank(k):
                    if k == 0 and step >= 6:
                        pe.wait_ge(freed, step - 5)

                def swap_q(m):
                    pe.wait_ge(q_kept, 2 * (m + 1))
                    if m >= 1:
                        pe.wait_ge(swap_freed, m)
                    for h in range(2):
                        mm = nc.tensor.matmul(ps[:, 6 + h, 0:HALF], swap[:], c.qT[:, m, h * HALF:(h + 1) * HALF],
                                              start=True, stop=True)
                    mm.then_inc(swapped, 1)

                norm[1](pe)
                pe.wait_ge(norm[3], KD)
                pe.wait_ge(table_landed, 48)
                for j in range(2):
                    pe.wait_ge(landed[j], 16)
                    for m in range(4):
                        for h in range(2):
                            for k in range(KD):
                                start_bank(k)
                                mm = nc.tensor.matmul(ps[:, step % 6, 0:HALF], w[:, j, k, m * P:(m + 1) * P],
                                                      c.xT[:, k, h * HALF:(h + 1) * HALF],
                                                      start=(k == 0), stop=(k == KD - 1))
                            mm.then_inc(filled, 1)
                            step += 1
                        if j * 4 + m >= 1:
                            swap_q(j * 4 + m - 1)
                    pe.drain().then_inc(block_read, 1)
                swap_q(KD - 1)
                for b in range(3):
                    pe.wait_ge(landed[b % 2], 16 * (b // 2 + 2))
                    for t in range(QT + 1):
                        n = rows_of(t)
                        for k in range(KD):
                            start_bank(k)
                            mm = nc.tensor.matmul(ps[0:n, step % 6, :], c.xT[:, k, t * P:t * P + n], w[:, b % 2, k, :],
                                                  start=(k == 0), stop=(k == KD - 1))
                        mm.then_inc(filled, 1)
                        step += 1
                    pe.drain().then_inc(block_read, 1)
                pe.wait_ge(gate_landed, 16)
                for t in range(QT + 1):
                    n = rows_of(t)
                    for k in range(KD):
                        start_bank(k)
                        mm = nc.tensor.matmul(ps[0:n, step % 6, 0:3 * NH], c.xT[:, k, t * P:t * P + n], wg[:, k, :],
                                              start=(k == 0), stop=(k == KD - 1))
                    mm.then_inc(filled, 1)
                    step += 1

            @block.scalar
            def _(act):
                norm[0](act)
                step = 0
                for m in range(KD):
                    for h in range(2):
                        act.wait_ge(filled, step + 1)
                        nc.scalar.mul(c.qT[:, m, h * HALF:(h + 1) * HALF], ps[:, step % 6, 0:HALF], -SCALE)\
                            .then_inc(q_kept, 1)
                        act.wait_ge(q_kept, step + 1)
                        act.sem_inc(freed, 1)
                        step += 1
                for b in range(3):
                    for t in range(QT + 1):
                        n = rows_of(t)
                        act.wait_ge(filled, step + 1)
                        nc.scalar.copy(c.kv[0:n, t, b, :], ps[0:n, step % 6, :]).then_inc(freed, 1)
                        step += 1
                for t in range(QT + 1):
                    n = rows_of(t)
                    act.wait_ge(filled, step + 1)
                    nc.scalar.activation(c.gates[0:n, t, :], ps[0:n, step % 6, 0:3 * NH], ACT.Exp, scale=-1.0)\
                        .then_inc(freed, 1)
                    step += 1

            @block.vector
            def _(dve):
                links = 0

                def linked(ins):
                    nonlocal links
                    links += 1
                    ins.then_inc(link, 1)
                    dve.wait_ge(link, links)

                norm[2](dve)
                dve.wait_ge(table_landed, 48)
                for m in range(KD):
                    dve.wait_ge(swapped, m + 1)
                    if m >= 1:
                        dve.wait_ge(roped, m)
                    for h in range(2):
                        cols = slice(h * HALF, (h + 1) * HALF)
                        linked(nc.vector.tensor_mul(tmp[:, cols], ps[:, 6 + h, 0:HALF], rope_t[:, 1, cols]))
                    dve.sem_inc(swap_freed, 1)
                    linked(nc.vector.tensor_mul(c.qrT[:, m, :], c.qT[:, m, :], rope_t[:, 0, :]))
                    nc.vector.tensor_add(c.qrT[:, m, :], c.qrT[:, m, :], tmp[:]).then_inc(roped, 1)
                dve.wait_ge(roped, KD)
                for b in range(3):
                    for t in range(QT + 1):
                        n = rows_of(t)
                        dve.wait_ge(freed, nq + b * (QT + 1) + t + 1)
                        if b == 0:
                            dve.sem_inc(roped, 1)
                            continue
                        k = c.kv[0:n, t, b, 0:KVW].rearrange("p (h s d) -> p h s d", s=2, d=HD // 2)
                        tv = tmp[0:n, 0:KVW].rearrange("p (h s d) -> p h s d", s=2, d=HD // 2)

                        def table(i, heads):
                            return rope[0:n, t, i, :].unsqueeze(1).to_broadcast([n, heads, HD // 2])
                        linked(nc.vector.tensor_mul(tv[:, :, 0, :], k[:, :, 1, :], table(1, NKV)))
                        linked(nc.vector.tensor_mul(tv[:, :, 1, :], k[:, :, 0, :], table(1, NKV)))
                        for s in range(2):
                            linked(nc.vector.tensor_mul(k[:, :, s, :], k[:, :, s, :], table(0, NKV)))
                        linked(nc.vector.tensor_sub(k[:, :, 0, :], k[:, :, 0, :], tv[:, :, 0, :]))
                        nc.vector.tensor_add(k[:, :, 1, :], k[:, :, 1, :], tv[:, :, 1, :]).then_inc(roped, 1)
                        dve.wait_ge(roped, 8 + b * (QT + 1) + t + 1)
                for t in range(QT + 1):
                    n = rows_of(t)
                    dve.wait_ge(freed, nq + nrow + t + 1)
                    linked(nc.vector.tensor_scalar_add(c.gates[0:n, t, :], c.gates[0:n, t, :], 1.0))
                    linked(nc.vector.reciprocal(c.gates[0:n, t, :], c.gates[0:n, t, :]))


RQ = 4


def compress_buffers(c, ctx):
    c.cmp_raw = c.buf("cmp_raw", [P, RQ - 2, 4, ROW], ctx=ctx)
    c.cmp_w1 = c.buf("cmp_w1", [P, 2, STRIDE, 2, HD], ctx=ctx)
    c.cmp_w2 = c.buf("cmp_w2", [HD, 2, 2, HD], ctx=ctx)
    c.cmp_pe_rows = c.buf("cmp_pe_rows", [4 * STRIDE, HD], ctx=ctx)
    c.cmp_w_ready, c.cmp_landed = c.sem("cmp_w_ready"), [c.sem(f"cmp_landed{s}") for s in range(RQ)]


def quad_slot(c, g):
    s = g % RQ
    return c.cmp_raw[:, s] if s < 2 else c.xT[:, 4 * (s - 2):4 * (s - 2) + 4, 0:ROW]


def load_quad(c, sp, g):
    pages = c.dram["cache_kv_cmp"][0].rearrange("g t s h d -> g t (s h d)")
    for j in range(4):
        page = sp.value_load(c.pages[0:1, 4 * g + j:4 * g + j + 1], min_val=0, max_val=POOL_PAGES - 1)
        sp.dma_start(quad_slot(c, g)[:, j, :], pages[bass.ds(page, 1)].rearrange("g t x -> (g t) x"))\
            .then_inc(c.cmp_landed[g % RQ], 16)


def compress_first_loads(c, sp):
    for kv in range(2):
        w = c.dram["nsa_cmp_w1"][0, kv].rearrange("(r t d) e -> r d t e", r=2, d=HD)
        for r in range(2):
            for copy in range(2):
                sp.dma_start(c.cmp_w1[copy * HD:(copy + 1) * HD, kv, :, r], w[r]).then_inc(c.cmp_w_ready, 16)
        for d in range(2):
            sp.dma_start(c.cmp_w2[:, kv, d], c.dram["nsa_cmp_w2"][0, kv]).then_inc(c.cmp_w_ready, 16)
    sp.dma_start(c.cmp_pe_rows[:], c.dram["nsa_cmp_pe"][0].rearrange("v a d -> (v a) d")).then_inc(c.cmp_w_ready, 16)
    for g in range(2):
        load_quad(c, sp, g)


def stage_compress(c):
    nc, ps = c.nc, c.psum
    units, quads = NB // 2 + 1, 4
    steps = 2 * units
    w_ready, landed, pe_turned = c.cmp_w_ready, c.cmp_landed, c.sem("cmp_pe_turned")
    raw, w1, w2, pe_rows = c.cmp_raw, c.cmp_w1, c.cmp_w2, c.cmp_pe_rows
    turned, kept, summed = c.sem("cmp_turned"), [c.sem("cmp_kept_dve"), c.sem("cmp_kept_act")], c.sem("cmp_summed")
    quad_read = c.sem("cmp_quad_read")
    shifted, added, gelued = c.sem("cmp_shifted"), c.sem("cmp_added"), c.sem("cmp_gelued")
    out_filled, out_kept, bias_done, pe_kept = (c.sem(f"cmp_{x}") for x in ("out_filled", "out_kept", "bias_done", "pe_kept"))
    bias_kept = c.sem("cmp_bias_kept")
    with ExitStack() as mine:
        xt = c.buf("cmp_xt", [P, 2, STRIDE, 2 * P], ctx=mine)
        pe_cols = c.buf("cmp_pe_cols", [HD, 4 * STRIDE], ctx=mine)
        bias = c.buf("cmp_bias", [P, 2], ctx=mine)
        tmp = c.buf("cmp_tmp", [HD, 2, 512], ctx=mine)
        gel = c.buf("cmp_gelu", [HD, 2, 512], ctx=mine)

        def shape_of(i):
            return (quads, 2, NSUB, NCS) if i // 2 < units - 1 else (1, 1, NSUBP, NCP)

        turns = [(i, q, hp) for i in range(steps) for q in range(shape_of(i)[0]) for hp in range(2)]
        first = [min(n for n, x in enumerate(turns) if x[0] == i) for i in range(steps)] + [len(turns)]

        def wait_kept(eng, n):
            for e in range(2):
                if (n + 1 - e) // 2 > 0:
                    eng.wait_ge(kept[e], (n + 1 - e) // 2)

        def empty(eng, copy, n):
            i, q, hp = turns[n]
            if n == first[i] + n % 2 and i >= 2:
                eng.wait_ge(summed, i - 1)
            eng.wait_ge(turned, n + 1)
            w = 4 * PAGE // STRIDE
            at = hp * shape_of(i)[0] * w + q * w
            copy(xt[:, i % 2, :, at:at + w], ps[:, n % 3, :].rearrange("p (x t) -> p t x", t=STRIDE)).then_inc(kept[n % 2], 1)

        with nc.Block() as block:
            @block.sync
            def _(sp):
                for g in range(2, NB * NPAGE // 4):
                    if g >= RQ:
                        sp.wait_ge(quad_read, g - RQ + 1)
                    load_quad(c, sp, g)

            @block.tensor
            def _(pe):
                pe.wait_ge(w_ready, 16 * 13)
                nc.tensor.transpose(ps[0:HD, 7, 0:4 * STRIDE], pe_rows[:], c.ident[0:4 * STRIDE, 0:4 * STRIDE]).then_inc(pe_turned, 1)
                pe.wait_ge(pe_kept, 1)
                for kv in range(2):
                    for a in range(2 * STRIDE):
                        mm = nc.tensor.matmul(ps[0:HD, 7, 64 + kv:65 + kv], w1[0:HD, kv, a % STRIDE, a // STRIDE, :],
                                              pe_cols[:, kv * 2 * STRIDE + a:kv * 2 * STRIDE + a + 1],
                                              start=(a == 0), stop=(a == 2 * STRIDE - 1))
                    mm.then_inc(bias_done, 1)

                def tail(i):
                    kv = i % 2
                    nq, nb, per, nk = shape_of(i)
                    pe.wait_ge(gelued, i + 1)
                    if i >= 1:
                        pe.wait_ge(out_kept, i)
                    g = gel[:, i % 2, :]
                    if kv == 0:
                        cols = NKV * nb * nk
                        nc.tensor.matmul(ps[:, 7, 0:cols], w2[:, 0].rearrange("e a f -> e (a f)"), g[:, 0:cols],
                                         start=True, stop=True).then_inc(out_filled, 1)
                    else:
                        for b in range(nb):
                            for h in range(NKV):
                                at = (h * nb + b) * nk
                                mm = nc.tensor.matmul(ps[0:nk, 7, (b * NKV + h) * HD:(b * NKV + h + 1) * HD],
                                                      g[:, at:at + nk], w2[:, 1, 0, :], start=True, stop=True)
                        mm.then_inc(out_filled, 1)

                def turn(n):
                    i, q, hp = turns[n]
                    u, kv = divmod(i, 2)
                    g = u * quads + q
                    if u < units - 1 and kv == 0 and hp == 0:
                        pe.wait_ge(landed[g % RQ], 64 * (g // RQ + 1))
                    if n >= 3:
                        wait_kept(pe, n - 2)
                    cols = slice(kv * KVW + hp * P, kv * KVW + hp * P + P)
                    for j in range(4):
                        src = quad_slot(c, g)[:, j, cols] if u < units - 1 else c.kv[:, j, 0, cols]
                        mm = nc.tensor.transpose(ps[:, n % 3, j * P:(j + 1) * P], src, c.ident[:])
                    mm.then_inc(turned, 1)
                    if u < units - 1 and kv == 1 and hp == 1:
                        pe.wait_ge(turned, n + 1)
                        pe.sem_inc(quad_read, 1)

                def product(i, t):
                    nq, nb, per, nk = shape_of(i)
                    cols = 2 * nb * per
                    if t == 0:
                        wait_kept(pe, first[i + 1])
                        if i >= 2:
                            pe.wait_ge(added, i - 1)
                    for z in range(2):
                        mm = nc.tensor.matmul(ps[:, 3 + i % 2 * 2 + z, 0:cols], w1[z * HD:(z + 1) * HD, i % 2, t].rearrange("p r e -> p (r e)"),
                                              xt[z * HD:(z + 1) * HD, i % 2, t, 0:cols], start=(t == 0), stop=(t == STRIDE - 1))
                    if t == STRIDE - 1:
                        pe.drain().then_inc(summed, 1)

                for i in range(steps + 1):
                    done = 0
                    here = range(first[i], first[i + 1]) if i < steps else range(0)
                    for k, n in enumerate(here):
                        turn(n)
                        if i >= 1:
                            upto = STRIDE * (k + 1) // len(here)
                            for t in range(done, upto):
                                product(i - 1, t)
                            done = upto
                    if i >= 1:
                        for t in range(done, STRIDE):
                            product(i - 1, t)
                    if i >= 2:
                        tail(i - 2)
                tail(steps - 1)

            @block.scalar
            def _(act):
                def finish(i):
                    kv = i % 2
                    nq, nb, per, nk = shape_of(i)
                    cols = NKV * nb * nk
                    if i == 0:
                        act.wait_ge(bias_kept, 1)
                    act.wait_ge(summed, i + 1)
                    if i >= 2:
                        act.wait_ge(gelued, i - 1)
                    t = tmp[:, i % 2, 0:cols].rearrange("p (a z b n) -> p z a b n", z=2, a=2, b=nb)
                    for z in range(2):
                        bank = ps[HD:P, 3 + i % 2 * 2 + z, 0:2 * nb * per].rearrange("p (a b n) -> p a b n", a=2, b=nb)
                        for b in range(nb):
                            ins = nc.scalar.activation(t[:, z, :, b], bank[:, :, b, 1:1 + nk], ACT.Identity, bias=bias[HD:P, kv:kv + 1])
                    ins.then_inc(shifted, 1)
                    act.wait_ge(added, i + 1)
                    if i >= 2:
                        act.wait_ge(out_filled, i - 1)
                    nc.scalar.activation(gel[:, i % 2, 0:cols], tmp[:, i % 2, 0:cols], ACT.Gelu_apprx_tanh).then_inc(gelued, 1)

                for i in range(steps):
                    for n in range(first[i], first[i + 1]):
                        if n % 2 == 1:
                            empty(act, nc.scalar.copy, n)
                    if i >= 1:
                        finish(i - 1)
                finish(steps - 1)

            @block.vector
            def _(dve):
                dve.wait_ge(pe_turned, 1)
                nc.vector.tensor_copy(pe_cols[:], ps[0:HD, 7, 0:4 * STRIDE]).then_inc(pe_kept, 1)
                dve.wait_ge(bias_done, 2)
                nc.vector.tensor_copy(bias[HD:P, :], ps[0:HD, 7, 64:66]).then_inc(bias_kept, 1)

                def copy_out(i):
                    u, kv = divmod(i, 2)
                    nq, nb, per, nk = shape_of(i)
                    dve.wait_ge(out_filled, i + 1)
                    bank = ps[:, 7, :]
                    if kv == 0:
                        v = bank[:, 0:NKV * nb * nk].rearrange("p (h b n) -> p h b n", h=NKV, b=nb)
                        if u == units - 1:
                            nc.vector.tensor_copy(c.kcp[:], v[:, :, 0, :]).then_inc(out_kept, 1)
                        else:
                            for half in range(2):
                                for a in range(2):
                                    ins = nc.vector.tensor_copy(c.kcs[half * HD:(half + 1) * HD, a, 2 * u:2 * u + 2, :],
                                                                v[half * HD:(half + 1) * HD, 2 * a + half])
                            ins.then_inc(out_kept, 1)
                    elif u == units - 1:
                        nc.vector.tensor_copy(c.vcp[0:nk, :], bank[0:nk, 0:KVW]).then_inc(out_kept, 1)
                    else:
                        nc.vector.tensor_copy(c.vcs[0:nk, 2 * u:2 * u + 2, :],
                                              bank[0:nk, :].rearrange("p (b x) -> p b x", b=2)).then_inc(out_kept, 1)

                def add(i):
                    nq, nb, per, nk = shape_of(i)
                    dve.wait_ge(shifted, i + 1)
                    t = tmp[:, i % 2, 0:NKV * nb * nk].rearrange("p (a z b n) -> p z a b n", z=2, a=2, b=nb)
                    for z in range(2):
                        bank = ps[0:HD, 3 + i % 2 * 2 + z, 0:2 * nb * per].rearrange("p (a b n) -> p a b n", a=2, b=nb)
                        for b in range(nb):
                            ins = nc.vector.tensor_add(t[:, z, :, b], bank[:, :, b, 0:nk], t[:, z, :, b])
                    ins.then_inc(added, 1)

                for i in range(steps):
                    for n in range(first[i], first[i + 1]):
                        if n % 2 == 0:
                            empty(dve, nc.vector.tensor_copy, n)
                    if i >= 1:
                        add(i - 1)
                    if i >= 2:
                        copy_out(i - 2)
                add(steps - 1)
                copy_out(steps - 2)
                copy_out(steps - 1)


def stage_prompt_attention(c):
    nc, ps = c.nc, c.psum
    turned, kept = c.sem("att_k_turned"), c.sem("att_k_kept")
    with ExitStack() as mine:
        kT = c.buf("att_kT", [P, 2, NKV, SEQ], ctx=mine)
        pcT = c.buf("att_pcT", [NCP, NH, SEQ], ctx=mine)
        with nc.Block() as block:
            @block.tensor
            def _(pe):
                for n in range(4):
                    kind, a = divmod(n, 2)
                    for t in range(QT):
                        mm = nc.tensor.transpose(ps[:, n, t * P:(t + 1) * P], c.kv[:, t, 1 + kind, a * P:(a + 1) * P], c.ident[:])
                    mm.then_inc(turned, 1)

            @block.vector
            def _(dve):
                for n in range(4):
                    kind, a = divmod(n, 2)
                    dve.wait_ge(turned, n + 1)
                    for to in range(2):
                        nc.vector.tensor_copy(kT[to * HD:(to + 1) * HD, kind, 2 * a, :], ps[0:HD, n, :]).then_inc(kept, 1)

            @block.scalar
            def _(act):
                for n in range(4):
                    kind, a = divmod(n, 2)
                    act.wait_ge(kept, 2 * (n + 1))
                    for to in range(2):
                        nc.scalar.copy(kT[to * HD:(to + 1) * HD, kind, 2 * a + 1, :], ps[HD:P, n, :])

        scored, masked, least_d, subbed, exped, scaled = (c.sem(f"attc_{x}") for x in ("scored", "masked", "least", "sub", "exp", "scaled"))
        turned_p, kept_p, summed, rec, gated, pmasked = (c.sem(f"attc_{x}") for x in ("turned", "kept", "summed", "rec", "gated", "pmasked"))
        with ExitStack() as here:
            sc = c.buf("attc_s", [P, 2, GRP, QT, NCP], ctx=here)
            low = c.buf("attc_low", [P, 2, GRP * QT], ctx=here)
            tot = c.buf("attc_tot", [P, 2, GRP * QT], ctx=here)
            cm = c.cmask[:].rearrange("p (w g t k) -> p w (g t) k", w=2, g=GRP, t=QT)

            def wide(x):
                return x.unsqueeze(2).to_broadcast([P, GRP * QT, NCP])

            with nc.Block() as block:
                @block.tensor
                def _(pe):
                    def turn(h):
                        pe.wait_ge(scaled, h + 1)
                        for g in range(GRP):
                            n = h * GRP + g
                            if n >= 3:
                                pe.wait_ge(kept_p, n - 2)
                            for t in range(QT):
                                mm = nc.tensor.transpose(ps[0:NCP, 4 + n % 3, t * P:(t + 1) * P], sc[:, h % 2, g, t, :], c.ident[:])
                            mm.then_inc(turned_p, 1)
                    for h in range(NKV):
                        for g in range(GRP):
                            head = h * GRP + g
                            rows = slice(head % 2 * HD, head % 2 * HD + HD)
                            for t in range(QT):
                                at = ((h % 2 * 2 + g // 2) * QT + t) * NCP
                                mm = nc.tensor.matmul(ps[:, h // 2 * 2 + g % 2, at:at + NCP], c.qT[rows, head // 2, t * P:(t + 1) * P],
                                                      c.kcp[rows, h, :], start=True, stop=True)
                        mm.then_inc(scored, 1)
                    for h in range(NKV):
                        turn(h)

                @block.vector
                def _(dve):
                    def finish(h):
                        s = sc[:, h % 2].rearrange("p g t k -> p (g t) k")
                        dve.wait_ge(exped, h + 1)
                        nc.vector.tensor_mul(s, s, cm[:, 1]).then_inc(pmasked, 1)
                        dve.wait_ge(pmasked, h + 1)
                        nc.vector.tensor_reduce(tot[:, h % 2, :], s, AX.X, ALU.add).then_inc(summed, 1)
                        dve.wait_ge(summed, h + 1)
                        nc.vector.tensor_scalar_max(tot[:, h % 2, :], tot[:, h % 2, :], 1e-20).then_inc(rec, 1)
                        dve.wait_ge(rec, 3 * h + 1)
                        nc.vector.reciprocal(tot[:, h % 2, :], tot[:, h % 2, :]).then_inc(rec, 1)
                        dve.wait_ge(rec, 3 * h + 2)
                        gate = c.gates[:, 0:QT, :].rearrange("p t (h w) -> p h t w", w=3)[:, h * GRP:(h + 1) * GRP, :, 0]
                        nc.vector.tensor_mul(tot[:, h % 2, :].rearrange("p (g t) -> p g t", g=GRP),
                                             tot[:, h % 2, :].rearrange("p (g t) -> p g t", g=GRP), gate).then_inc(rec, 1)
                        dve.wait_ge(rec, 3 * h + 3)
                        nc.vector.tensor_mul(s, s, wide(tot[:, h % 2, :])).then_inc(scaled, 1)

                    for h in range(NKV):
                        s = sc[:, h % 2].rearrange("p g t k -> p (g t) k")
                        dve.wait_ge(scored, h // 2 * 2 + 2)
                        if h >= 2:
                            dve.wait_ge(turned_p, GRP * (h - 1))
                        for par in range(2):
                            ins = nc.vector.tensor_add(
                                sc[:, h % 2, par::2],
                                ps[:, h // 2 * 2 + par, h % 2 * 2 * QT * NCP:(h % 2 + 1) * 2 * QT * NCP].rearrange("p (g t k) -> p g t k", g=2, t=QT),
                                c.cmask[:].rearrange("p (w g t k) -> p w g t k", w=2, g=GRP, t=QT)[:, 0, par::2])
                        ins.then_inc(masked, 1)
                        dve.wait_ge(masked, h + 1)
                        nc.vector.tensor_reduce(low[:, h % 2, :], s, AX.X, ALU.min).then_inc(least_d, 1)
                        dve.wait_ge(least_d, h + 1)
                        nc.vector.tensor_sub(s, s, wide(low[:, h % 2, :])).then_inc(subbed, 1)
                        if h >= 1:
                            finish(h - 1)
                    finish(NKV - 1)

                @block.scalar
                def _(act):
                    n = 0
                    for h in range(NKV + 1):
                        if h < NKV:
                            act.wait_ge(subbed, h + 1)
                            s = sc[:, h % 2].rearrange("p g t k -> p (g t k)")
                            nc.scalar.activation(s, s, ACT.Exp, scale=-1.0).then_inc(exped, 1)
                        if h >= 1:
                            for g in range(GRP):
                                act.wait_ge(turned_p, n + 1)
                                nc.scalar.copy(pcT[:, n, :], ps[0:NCP, 4 + n % 3, :]).then_inc(kept_p, 1)
                                n += 1

        scored, lowered, exped, recip, scaled, turned_u, kept_u, unit_mul = (
            c.sem(f"att_{x}") for x in ("scored", "lowered", "exped", "recip", "scaled", "turned", "kept", "read"))
        o_filled, o_kept = c.sem("att_o_filled"), c.sem("att_o_kept")
        NU = NH * 2 * QT
        LAG, LAG_PV = 3, 5
        with ExitStack() as here:
            pr = c.buf("att_p", [P, 4, SEQ], ctx=here)
            pT = c.buf("att_pT", [P, 2, QT, SEQ], ctx=here)
            low = c.buf("att_low", [P, 4], ctx=here)
            tot = c.buf("att_tot", [P, 4], ctx=here)

            def unit(n):
                return n // (2 * QT), (n // QT) % 2, n % QT

            with nc.Block() as block:
                @block.tensor
                def _(pe):
                    def scores(n):
                        head, kind, i = unit(n)
                        rows = slice(head % 2 * HD, head % 2 * HD + HD)
                        if n >= 3:
                            pe.wait_ge(lowered, n - 2)
                        nc.tensor.matmul(ps[:, n % 3, 0:(i + 1) * P], c.qrT[rows, head // 2, i * P:(i + 1) * P],
                                         kT[rows, kind, head // GRP, 0:(i + 1) * P], start=True, stop=True).then_inc(scored, 1)

                    def turn(n):
                        head, kind, i = unit(n)
                        pe.wait_ge(scaled, n + 1)
                        if n >= 3:
                            pe.wait_ge(kept_u, n - 2)
                        for j in range(i + 1):
                            mm = nc.tensor.transpose(ps[:, 3 + n % 3, j * P:(j + 1) * P], pr[:, n % 4, j * P:(j + 1) * P], c.ident[:])
                        mm.then_inc(turned_u, 1)

                    def values(n):
                        head, kind, i = unit(n)
                        hp, par = head // 2, head % 2
                        out = ps[par * HD:(par + 1) * HD, 6 + hp % 2, :]
                        if kind == 0:
                            if hp >= 2 and par == 0:
                                pe.wait_ge(o_kept, hp - 1)
                            nc.tensor.matmul(out, c.vcp[0:NCP, head // GRP * HD:(head // GRP + 1) * HD], pcT[:, head, :],
                                             start=True, stop=False)
                        pe.wait_ge(kept_u, n + 1)
                        for j in range(QT):
                            mm = nc.tensor.matmul(out[:, j * P:SEQ],
                                                  c.kv[:, j, 1 + kind, KVW + head // GRP * HD:KVW + (head // GRP + 1) * HD],
                                                  pT[:, kind, j, j * P:SEQ], start=False, stop=(kind == 1 and j == QT - 1))
                        mm.then_inc(o_filled, 1)

                    for n in range(NU + LAG_PV):
                        if n < NU:
                            scores(n)
                        if LAG <= n < NU + LAG:
                            turn(n - LAG)
                        if n >= LAG_PV and (n - LAG_PV) % QT == QT - 1:
                            values(n - LAG_PV)

                @block.vector
                def _(dve):
                    for n in range(NU + 1):
                        if n < NU:
                            head, kind, i = unit(n)
                            w = (i + 1) * P
                            dve.wait_ge(scored, n + 1)
                            if n >= 4:
                                dve.wait_ge(turned_u, n - 3)
                            nc.vector.tensor_tensor_reduce(pr[:, n % 4, 0:w], ps[:, n % 3, 0:w], c.causal[:, SEQ - w:SEQ], 1.0,
                                                           3e38, ALU.add, ALU.min, low[:, n % 4:n % 4 + 1]).then_inc(lowered, 1)
                        if n >= 1:
                            m = n - 1
                            head, kind, i = unit(m)
                            w = (i + 1) * P
                            dve.wait_ge(exped, m + 1)
                            nc.vector.reciprocal(tot[:, m % 4:m % 4 + 1], tot[:, m % 4:m % 4 + 1]).then_inc(recip, 1)
                            dve.wait_ge(recip, m + 1)
                            gate = c.gates[:, i, head * 3 + 1 + kind:head * 3 + 2 + kind]
                            nc.vector.tensor_scalar(pr[:, m % 4, 0:w], pr[:, m % 4, 0:w], tot[:, m % 4:m % 4 + 1], gate,
                                                    ALU.mult, ALU.mult).then_inc(scaled, 1)

                @block.scalar
                def _(act):
                    def keep(n):
                        head, kind, i = unit(n)
                        act.wait_ge(turned_u, n + 1)
                        hk = n // QT
                        if hk >= 2:
                            act.wait_ge(o_filled, hk - 1)
                        nc.scalar.copy(pT[:, kind, 0:i + 1, i * P:(i + 1) * P],
                                       ps[:, 3 + n % 3, 0:(i + 1) * P].rearrange("p (j q) -> p j q", q=P)).then_inc(kept_u, 1)

                    def keep_o(hp):
                        act.wait_ge(o_filled, 4 * (hp + 1))
                        nc.scalar.copy(c.oT[:, hp, 0:SEQ], ps[:, 6 + hp % 2, :]).then_inc(o_kept, 1)

                    for n in range(NU + LAG + 3):
                        if n < NU:
                            head, kind, i = unit(n)
                            w = (i + 1) * P
                            act.wait_ge(lowered, n + 1)
                            nc.scalar.activation(pr[:, n % 4, 0:w], pr[:, n % 4, 0:w], ACT.Exp, scale=-1.0,
                                                 bias=low[:, n % 4:n % 4 + 1], accum_out=tot[:, n % 4:n % 4 + 1]).then_inc(exped, 1)
                        if LAG <= n < NU + LAG:
                            keep(n - LAG)
                        if n >= LAG_PV and (n - LAG_PV) % (4 * QT) == 4 * QT - 1:
                            keep_o((n - LAG_PV) // (4 * QT))


NKC = PAST // P
NWC = WIN // P
NC_S = NKC + NWC


def stage_sample_queries(c):
    nc, ps = c.nc, c.psum
    cleared, put, gates_out, k_turned = c.sem("sq_cleared"), c.sem("sq_put"), c.sem("sq_gates"), c.sem("sq_k_turned")
    k_kept = c.sem("sq_k_kept")
    with nc.Block() as block:
        @block.vector
        def _(dve):
            nc.vector.memset(c.qz[:], 0.0).then_inc(cleared, 1)
            dve.wait_ge(cleared, 1)
            for which, src in enumerate((c.qT, c.qrT)):
                flat = c.qz[:, which].rearrange("p a b x -> p a (b x)")
                for t in range(KD):
                    a, kv2 = t // 4, t // 2 % 2
                    for par in range(2):
                        h = 2 * t + par
                        base = flat[kv2 * HD:(kv2 + 1) * HD, a, :]
                        dst = bass.AP(base.tensor, base.offset + h, [list(base.ap[0]), [P + NH, NB]])
                        nc.vector.tensor_copy(dst, src[par * HD:(par + 1) * HD, t, SEQ:T]).then_inc(put, 1)
            dve.wait_ge(k_turned, 1)
            nc.vector.tensor_copy(c.knT[:], ps[:, 0, 0:4 * NB].rearrange("p (w a b) -> p w a b", w=2, a=2)).then_inc(k_kept, 1)

        @block.tensor
        def _(pe):
            for which in range(2):
                for a in range(2):
                    mm = nc.tensor.transpose(ps[:, 0, (which * 2 + a) * NB:(which * 2 + a + 1) * NB],
                                             c.kv[0:NB, QT, 1 + which, a * P:(a + 1) * P], c.ident[0:NB, 0:NB])
            mm.then_inc(k_turned, 1)

        @block.sync
        def _(sp):
            for b in range(NB):
                sp.dma_start(c.gates_s[b * NH:(b + 1) * NH, :],
                             c.gates[b:b + 1, QT, :].rearrange("o (h w) -> o h w", w=3)).then_inc(gates_out, 16)
            sp.wait_ge(gates_out, 16 * NB)


def stage_sample_attention(c):
    nc, ps = c.nc, c.psum
    sel_pages = c.dram["cache_kv_sel"][0].rearrange("g t s h d -> g t (s h d)")
    win = c.dram["cache_kv_win"][0].rearrange("b (c t) s h d -> b t c (s h d)", t=P)
    win_out = c.dram["kv_win_sample"][0].rearrange("b t s h d -> b t (s h d)")
    RS = 7
    landed, written = [c.sem(f"sa_landed{s}") for s in range(RS)], [c.sem(f"sa_written{s}") for s in range(RS)]
    v_read = c.sem("sa_v_read")
    turned, kept, scored, s_done = c.sem("sa_turned"), c.sem("sa_kept"), c.sem("sa_scored"), c.sem("sa_scores_done")
    link, exped, a_ready = c.sem("sa_link"), c.sem("sa_exp"), c.sem("sa_exp_ready")
    imp_in, imp_out, p_turn, p_kept, o_done, o_kept, o_rows = (
        c.sem(f"sa_{x}") for x in ("imp_in", "imp_out", "p_turned", "p_kept", "o_done", "o_kept", "o_rows"))
    with ExitStack() as mine:
        raw = c.buf("sa_raw", [P, RS, NC_S, KVW], ctx=mine)

        def wait_landed(eng, n):
            eng.wait_ge(landed[n % RS], 16 * (NPAGE + 1) * (n // RS + 1))

        kT = c.buf("sa_kT", [P, 4, 512], ctx=mine)
        s_sel = c.buf("sa_s_sel", [P, PAST + NB], ctx=mine)
        s_win = c.buf("sa_s_win", [P, WIN + NB], ctx=mine)
        s_cmp = c.buf("sa_s_cmp", [P, NCS], ctx=mine)
        low = c.buf("sa_low", [P, 3], ctx=mine)
        tot = c.buf("sa_tot", [P, 3], ctx=mine)
        drop = c.buf("sa_drop", [P, 4, NSEL], ctx=mine)
        one = c.buf("sa_one", [P, 4], ctx=mine)
        pc = c.buf("sa_pcT", [P, 2, P], ctx=mine)
        pT = kT[:, 0:3, :].rearrange("p q (j x) -> p (q j) x", x=P)
        pn = c.buf("sa_pnT", [NB, 2, P], ctx=mine)
        o_r = c.buf("sa_o_rows", [P, 2, KVW], ctx=mine)
        ngroup = NB * 3 * 2
        with nc.Block() as block:
            @block.sync
            def _(sp):
                for n in range(2 * NB):
                    kv, b = divmod(n, NB)
                    s, cols = n % RS, slice(kv * KVW, (kv + 1) * KVW)
                    if n >= RS:
                        m = n - RS
                        if m < NB:
                            sp.wait_ge(turned, 6 * (m + 1))
                        else:
                            sp.wait_ge(v_read, m - NB + 1)
                        sp.wait_ge(written[s], 32 * (n // RS))
                    for j in range(NPAGE):
                        at = b * NPAGE + j
                        page = sp.value_load(c.pages[0:1, at:at + 1], min_val=0, max_val=POOL_PAGES - 1)
                        rows = sel_pages[bass.ds(page, 1), :, :].rearrange("g t x -> (g t) x")
                        sp.dma_start(raw[:, s, j, :], rows[:, cols]).then_inc(landed[s], 16)
                    sp.dma_start(raw[:, s, NKC:, :], win[b, :, :, cols]).then_inc(landed[s], 16)

            @block.gpsimd
            def _(pool):
                for n in range(2 * NB):
                    kv, b = divmod(n, NB)
                    s, cols = n % RS, slice(kv * KVW, (kv + 1) * KVW)
                    wait_landed(pool, n)
                    pool.dma_start(win_out[b, 0:P - 1, cols], raw[1:P, s, NKC, :]).then_inc(written[s], 16)
                    pool.dma_start(win_out[b, P - 1:WIN - 1, cols].rearrange("(c t) x -> t c x", t=P),
                                   raw[:, s, NKC + 1:, :]).then_inc(written[s], 16)
                for s in range(RS):
                    pool.wait_ge(written[s], 32 * len(range(s, 2 * NB, RS)))

            @block.tensor
            def _(pe):
                for a in range(2):
                    for b in range(NB):
                        nc.tensor.matmul(ps[:, 6, 0:NCS], c.qz[:, 0, a, b, :], c.kcs[:, a, b, :],
                                         start=(a == 0 and b == 0), stop=(a == 1 and b == NB - 1))
                for w in range(2):
                    for a in range(2):
                        for b in range(NB):
                            mm = nc.tensor.matmul(ps[:, 7, w * NB:(w + 1) * NB], c.qz[:, 1, a, b, :], c.knT[:, w, a, :],
                                                  start=(a == 0 and b == 0), stop=(a == 1 and b == NB - 1))
                mm.then_inc(s_done, 1)

                def product(n):
                    b, r = divmod(n, 6)
                    part, a = divmod(r, 2)
                    pe.wait_ge(kept, n + 1)
                    nc.tensor.matmul(ps[:, part, :], c.qz[:, 1, a, b, :], kT[:, n % 4, :],
                                     start=(b == 0 and a == 0), stop=(b == NB - 1 and a == 1)).then_inc(scored, 1)

                for n in range(ngroup + 2):
                    if n < ngroup:
                        b, r = divmod(n, 6)
                        part, a = divmod(r, 2)
                        if r == 0:
                            wait_landed(pe, b)
                        if n >= 3:
                            pe.wait_ge(kept, n - 2)
                        for j in range(4):
                            mm = nc.tensor.transpose(ps[:, 3 + n % 3, j * P:(j + 1) * P],
                                                     raw[:, b % RS, part * 4 + j, a * P:(a + 1) * P], c.ident[:])
                        mm.then_inc(turned, 1)
                    if n >= 2:
                        product(n - 2)
                pe.wait_ge(imp_in, 1)
                nc.tensor.transpose(ps[0:NCS, 3, 0:P], s_cmp[:], c.ident[:]).then_inc(imp_out, 1)
                pe.wait_ge(imp_in, 2)
                nc.tensor.matmul(ps[:, 3, P:P + NSEL], pc[0:NCS, 0, :], c.over[0:NCS, :], start=True, stop=True).then_inc(imp_out, 1)
                pe.wait_ge(imp_in, 3)
                nc.tensor.matmul(ps[:, 4, 0:NSEL], c.group[:], drop[:, 0, :], start=True, stop=True).then_inc(imp_out, 1)
                pe.wait_ge(a_ready, 4)
                nc.tensor.transpose(ps[0:NCS, 5, 0:P], s_cmp[:], c.ident[:]).then_inc(p_turn, 1)
                pe.wait_ge(a_ready, 6)
                for q in range(3):
                    if q == 1:
                        pe.wait_ge(p_kept, 1)
                    for j in range(4):
                        src = s_sel[:, (q * 4 + j) * P:(q * 4 + j + 1) * P] if q < 2 else s_win[:, j * P:(j + 1) * P]
                        mm = nc.tensor.transpose(ps[:, (3, 4, 2)[q], j * P:(j + 1) * P], src, c.ident[:])
                    mm.then_inc(p_turn, 1)
                for w in range(2):
                    src = s_win[:, WIN:] if w else s_sel[:, PAST:]
                    mm = nc.tensor.transpose(ps[0:NB, 6, w * P:(w + 1) * P], src, c.ident[:])
                mm.then_inc(p_turn, 1)
                pe.wait_ge(p_kept, 5)
                for bg in range(2):
                    for q in range(4):
                        wait_landed(pe, NB + bg * 4 + q)
                    for j in range(NC_S + 3):
                        for q in range(4):
                            b = bg * 4 + q
                            out, heads = ps[32 * q:32 * q + NH, bg, 0:KVW], slice(b * NH, (b + 1) * NH)
                            if j == 0:
                                lhs, rhs = pc[0:NCS, 1, heads], c.vcs[0:NCS, b, :]
                            elif j < 3:
                                lhs, rhs = pn[:, j - 1, heads], c.kv[0:NB, QT, j, KVW:]
                            else:
                                lhs, rhs = pT[:, j - 3, heads], raw[:, (NB + b) % RS, j - 3, :]
                            mm = nc.tensor.matmul(out, lhs, rhs, start=(j == 0), stop=(j == NC_S + 2), tile_position=(0, 32 * q))
                            if j == NC_S + 2:
                                mm.then_inc(v_read, 1)
                pe.wait_ge(o_rows, 9)
                for bg in range(2):
                    for a in range(2):
                        mm = nc.tensor.transpose(ps[:, 3, (bg * 2 + a) * P:(bg * 2 + a + 1) * P], o_r[:, bg, a * P:(a + 1) * P], c.ident[:])
                mm.then_inc(o_done, 1)

            @block.scalar
            def _(act):
                for n in range(0, ngroup, 2):
                    act.wait_ge(turned, n + 1)
                    if n >= 4:
                        act.wait_ge(scored, n - 3)
                    nc.scalar.copy(kT[:, n % 4, :], ps[:, 3 + n % 3, :]).then_inc(kept, 1)
                    if n + 1 < ngroup:
                        act.wait_ge(turned, n + 2)
                        if n + 1 >= 4:
                            act.wait_ge(scored, n - 2)
                        nc.scalar.copy(kT[:, (n + 1) % 4, :], ps[:, 3 + (n + 1) % 3, :]).then_inc(kept, 1)
                for w, s in enumerate((s_cmp, s_win, s_sel)):
                    act.wait_ge(a_ready, w + 1)
                    nc.scalar.activation(s[:], s[:], ACT.Exp, scale=-1.0, bias=low[:, w:w + 1],
                                         accum_out=tot[:, w:w + 1]).then_inc(exped, 1)

            @block.vector
            def _(dve):
                links = 0

                def linked(ins):
                    nonlocal links
                    links += 1
                    ins.then_inc(link, 1)
                    dve.wait_ge(link, links)

                def weigh(w, s, signal=None):
                    gate = c.gates_s[:, (0, 2, 1)[w]:(0, 2, 1)[w] + 1]
                    return nc.vector.tensor_scalar(s[:], s[:], tot[:, w:w + 1], gate, ALU.mult, ALU.mult)

                dve.wait_ge(s_done, 1)
                linked(nc.vector.tensor_copy(s_cmp[:], ps[:, 6, 0:NCS]))
                linked(nc.vector.tensor_copy(one[:, 0:1], ps[:, 7, 0:1]))
                linked(nc.vector.tensor_add(s_sel[:, PAST:], ps[:, 7, 0:NB], c.own[:]))
                linked(nc.vector.tensor_add(s_win[:, WIN:], ps[:, 7, NB:2 * NB], c.own[:]))
                nc.vector.tensor_reduce(low[:, 0:1], s_cmp[:], AX.X, ALU.min).then_inc(a_ready, 1)
                dve.wait_ge(exped, 1)
                linked(nc.vector.reciprocal(tot[:, 0:1], tot[:, 0:1]))
                nc.vector.tensor_scalar(s_cmp[:], s_cmp[:], tot[:, 0:1], None, ALU.mult).then_inc(imp_in, 1)
                dve.wait_ge(scored, ngroup)
                linked(nc.vector.tensor_copy(s_win[:, 0:WIN], ps[:, 2, :]))
                nc.vector.tensor_reduce(low[:, 1:2], s_win[:], AX.X, ALU.min).then_inc(a_ready, 1)
                dve.wait_ge(imp_out, 1)
                nc.vector.tensor_copy(pc[0:NCS, 0, :], ps[0:NCS, 3, 0:P]).then_inc(imp_in, 1)
                dve.wait_ge(imp_out, 2)
                nc.vector.tensor_copy(drop[:, 0, :], ps[:, 3, P:P + NSEL]).then_inc(imp_in, 1)
                dve.wait_ge(imp_out, 3)
                imp, eq, at = drop[:, 1, :], drop[:, 2, :], drop[:, 3, :]
                linked(nc.vector.tensor_copy(imp, ps[:, 4, 0:NSEL]))
                linked(nc.vector.tensor_reduce(one[:, 1:2], imp[:, 1:NSEL - 2], AX.X, ALU.min))
                linked(nc.vector.tensor_scalar(eq[:, 1:NSEL - 2], imp[:, 1:NSEL - 2], one[:, 1:2], None, ALU.is_equal))
                linked(nc.vector.tensor_mul(at[:, 1:NSEL - 2], eq[:, 1:NSEL - 2], c.blk[:, 1:NSEL - 2]))
                linked(nc.vector.tensor_reduce(one[:, 2:3], at[:, 1:NSEL - 2], AX.X, ALU.max))
                linked(nc.vector.tensor_scalar(eq, c.blk[:], one[:, 2:3], BIG, ALU.is_equal, ALU.mult))
                for half in range(2):
                    linked(nc.vector.tensor_add(s_sel[:, half * 512:(half + 1) * 512].rearrange("p (n x) -> p n x", x=SELB),
                                                ps[:, half, :].rearrange("p (n x) -> p n x", x=SELB),
                                                eq[:, half * 8:half * 8 + 8].unsqueeze(2).to_broadcast([P, 8, SELB])))
                nc.vector.tensor_reduce(low[:, 2:3], s_sel[:], AX.X, ALU.min).then_inc(a_ready, 1)
                nc.vector.tensor_scalar(s_cmp[:], s_cmp[:], c.gates_s[:, 0:1], None, ALU.mult).then_inc(a_ready, 1)
                for w, s in ((1, s_win), (2, s_sel)):
                    dve.wait_ge(exped, w + 1)
                    linked(nc.vector.reciprocal(tot[:, w:w + 1], tot[:, w:w + 1]))
                    weigh(w, s).then_inc(a_ready, 1)
                dve.wait_ge(p_turn, 1)
                nc.vector.tensor_copy(pc[0:NCS, 1, :], ps[0:NCS, 5, 0:P]).then_inc(p_kept, 1)
                for q in range(3):
                    dve.wait_ge(p_turn, 2 + q)
                    nc.vector.tensor_copy(pT[:, q * 4:q * 4 + 4, :],
                                          ps[:, (3, 4, 2)[q], :].rearrange("p (j x) -> p j x", x=P)).then_inc(p_kept, 1)
                dve.wait_ge(p_turn, 5)
                nc.vector.tensor_copy(pn[:], ps[0:NB, 6, 0:2 * P].rearrange("p (w x) -> p w x", w=2)).then_inc(p_kept, 1)
                nc.vector.memset(o_r[:], 0.0).then_inc(o_rows, 1)
                dve.wait_ge(o_rows, 1)
                for b in range(NB):
                    dve.wait_ge(v_read, 4 * (b // 4 + 1))
                    rows = slice(32 * (b % 4), 32 * (b % 4) + NH)
                    nc.vector.tensor_copy(o_r[rows, b // 4, :], ps[rows, b // 4, 0:KVW]).then_inc(o_rows, 1)
                dve.wait_ge(o_done, 1)
                for kv2 in range(2):
                    for par in range(2):
                        for a in range(2):
                            for bg in range(2):
                                src = ps[kv2 * HD:(kv2 + 1) * HD, 3, (bg * 2 + a) * P:(bg * 2 + a + 1) * P]\
                                    .rearrange("p (q a v j r) -> p a v r j q", a=4, v=2, j=2, r=2)
                                nc.vector.tensor_copy(c.oT[par * HD:(par + 1) * HD, a * 4 + kv2 * 2:a * 4 + kv2 * 2 + 2, SEQ + bg * 4:SEQ + bg * 4 + 4],
                                                      src[:, a, kv2, par]).then_inc(o_kept, 1)


def stage_nsa(c):
    with ExitStack() as outer:
        c.kcs = c.buf("kcs", [P, 2, NB, NCS], ctx=outer)
        c.vcs = c.buf("vcs", [NCS, NB, KVW], ctx=outer)
        c.kcp = c.buf("kcp", [P, NKV, NCP], ctx=outer)
        c.vcp = c.buf("vcp", [NCP, KVW], ctx=outer)
        c.kv = c.buf("kv", [P, QT + 1, 3, ROW], ctx=outer)
        c.gates = c.buf("gates", [P, QT + 1, 3 * NH], ctx=outer)
        c.gates_s = c.buf("gates_s", [P, 3], ctx=outer)
        c.qz = c.buf("qz", [P, 2, 2, NB, P], ctx=outer)
        c.knT = c.buf("knT", [P, 2, 2, NB], ctx=outer)
        c.oT = c.xT
        with ExitStack() as queries:
            c.qT = c.buf("qT", [P, KD, T], ctx=queries)
            c.qrT = c.buf("qrT", [P, KD, T], ctx=queries)
            compress_ctx = queries.enter_context(ExitStack())
            compress_buffers(c, compress_ctx)
            stage_project(c, norm_parts(c, "nsa_in", c.hT, c.xT, 0, 0, c.qrT[:, 0:4], c.qrT[:, 4]))
            stage_sample_queries(c)
            stage_compress(c)
            compress_ctx.close()
            stage_prompt_attention(c)
        stage_sample_attention(c)


MAGIC = 1.5 * 2.0 ** 23
TWO_PI = 2.0 * np.pi
COLS = NCH + 2 * NB
HCOLS = NCH + NB
DVE_PAIRS = 21
A_COLS = G + GP


def split(x, parts):
    out = []
    for _ in range(parts - 1):
        m, e = np.frexp(x)
        hi = float(np.ldexp(np.round(m * 2 ** 10), e - 10))
        out.append(hi)
        x -= hi
    return [*out, float(np.float32(x))]


class Chain:

    def __init__(self, c, eng, name):
        self.eng, self.sem, self.n = eng, c.sem(name), 0

    def __call__(self, ins):
        self.n += 1
        ins.then_inc(self.sem, 1)
        self.eng.wait_ge(self.sem, self.n)


def complex_axpy(eng, link, out, x, table, t, u):
    n, w = x.shape[2], x.shape[3]

    def wide(i):
        return table[:, i].unsqueeze(2).to_broadcast([P, n, w])
    link(eng.tensor_mul(t, x, table[:, 0].unsqueeze(1).unsqueeze(3).to_broadcast([P, 2, n, w])))
    link(eng.tensor_mul(u[:, 0], x[:, 1], wide(2)))
    link(eng.tensor_mul(u[:, 1], x[:, 0], wide(1)))
    link(eng.tensor_add(t, t, u))
    link(eng.tensor_add(out, out, t))


def stage_ssm_tables(c, norm):
    nc, ps = c.nc, c.psum
    dram = c.dram
    loaded, b_loaded = c.sem("st_loaded"), c.sem("st_b_loaded")
    turned, rows_ready, trig = c.sem("st_turned"), c.sem("st_rows_ready"), c.sem("st_trig")
    act_sem, c_turned, c_kept = c.sem("st_act"), c.sem("st_c_turned"), c.sem("st_c_kept")
    v_kept = c.sem("st_v_kept")
    m_ready, k_done, k_kept, k_written = c.sem("st_m_ready"), c.sem("st_k_done"), c.sem("st_k_kept"), c.sem("st_k_written")
    cos_sem, pw_ready, b_ready = c.sem("st_cos"), c.sem("st_powers_ready"), c.sem("st_b_ready")
    v_ready, v_turned = [c.sem("st_v_ready_pool"), c.sem("st_v_ready_dve")], [c.sem("st_v_turned_pool"), c.sem("st_v_turned_dve")]
    v_order = [(0, 0), (1, 0), (2, 0), (3, 0), (5, 1), (4, 0), (6, 1), (7, 1)]
    with ExitStack() as mine:
        def buf(name, shape):
            return c.buf("st_" + name, shape, ctx=mine)
        ag, ap_ = buf("a_g", [G, 2, 2, NS]), buf("a_p", [GP, 2, P])
        zg, zp = buf("z_g", [G, 2, 2, NS]), buf("z_p", [GP, 2, P])
        dg, dp = buf("dt_g", [G, 1]), buf("dt_p", [GP, 2])
        z = buf("z", [P, 2, A_COLS])
        al = buf("alpha", [P, 2, G])
        s1, s2, s3, s4 = (buf(f"s{i}", [P, A_COLS]) for i in range(4))
        ki = c.buf("st_ki", [P, A_COLS], I32, ctx=mine)
        f = buf("f", [P, 2, G])
        crow = buf("c_rows", [P, KD, 2, 2, NS])
        cx, cy = buf("cx", [P, G, CH]), buf("cy", [P, G, CH])
        bx, by = buf("bx", [P, G, CH]), buf("by", [P, G, CH])
        bbx, bby = buf("bbx", [P, G, 2 * CH]), buf("bby", [P, G, CH])
        tmp = buf("tmp", [P, G, CH])
        kz = buf("kz", [P, G // 4, (2 * L - 1) * CH])
        v = buf("v", [P, 2, 8, L, CH])
        tmp_p = c.y[:, 5:7].rearrange("p k t -> p (k t)")[:, 0:G * CH].rearrange("p (g c) -> p g c", c=CH)
        q1, q2 = buf("q1", [P, GP]), buf("q2", [P, GP])
        pw = buf("pw", [P, 2, L + 1, A_COLS])

        def wide(x, n=G):
            return x.unsqueeze(2).to_broadcast([P, n, CH])

        with nc.Block() as block:
            @block.sync
            def _(sp):
                for i, name in enumerate(("s5_a_re", "s5_a_im")):
                    a = dram[name][0]
                    for d in range(2):
                        sp.dma_start(ag[:, i, d], a).then_inc(loaded, 16)
                    sp.dma_start(ap_[:, i], a.rearrange("(q w) n -> q (w n)", w=2)).then_inc(loaded, 16)
                sp.dma_start(dg[:], dram["s5_log_dt"].rearrange("o g -> g o")).then_inc(loaded, 16)
                sp.dma_start(dp[:], dram["s5_log_dt"].rearrange("o (q w) -> q (o w)", w=2)).then_inc(loaded, 16)
                for i, name in enumerate(("s5_c_re", "s5_c_im")):
                    cc = dram[name][0].rearrange("(k g) c n -> (g c) k n", k=KD)
                    sp.dma_start(crow[:, :, 0, i], cc).then_inc(loaded, 16)
                    sp.dma_start(crow[:, :, 1, 1 - i], cc).then_inc(loaded, 16)
                for i, name in enumerate(("s5_b_re", "s5_b_im")):
                    bb = dram[name][0].rearrange("g n c -> n g c")
                    sp.dma_start(bx[i * NS:(i + 1) * NS], bb).then_inc(b_loaded, 16)
                    sp.dma_start(by[(1 - i) * NS:(2 - i) * NS], bb).then_inc(b_loaded, 16)
                sp.wait_ge(k_kept, 4)
                for q in range(4):
                    sp.dma_start(c.scratch_k.rearrange("(j q) c x -> q c j x", q=4)[q], kz[32 * q:32 * q + CH]).then_inc(k_written, 16)
                sp.wait_ge(k_written, 64)

            @block.scalar
            def _(act):
                norm[0](act)
                act.wait_ge(loaded, 16 * 12)
                nc.scalar.activation(dg[:], dg[:], ACT.Exp).then_inc(act_sem, 1)
                nc.scalar.activation(dp[:], dp[:], ACT.Exp).then_inc(act_sem, 1)
                act.wait_ge(trig, 1)
                nc.scalar.activation(s2[:], s2[:], ACT.Sin).then_inc(cos_sem, 1)
                act.wait_ge(trig, 2)
                nc.scalar.activation(s3[:], s3[:], ACT.Sin).then_inc(cos_sem, 1)
                seen = [0, 0]
                for k, who in v_order:
                    for h in range(2):
                        seen[who] += 1
                        act.wait_ge(v_turned[who], seen[who])
                        nc.scalar.copy(c.wb[:, k * 8 + h * 4:k * 8 + h * 4 + 4, :],
                                       ps[:, 5 + h, :].rearrange("p (g x) -> p g x", g=4)).then_inc(v_kept, 1)

            def make_v(eng, ve, link, k, who, done, t):
                gs = slice(k * 8, k * 8 + 8)
                if done >= 1:
                    eng.wait_ge(v_turned[who], 2 * done)
                link(ve.tensor_copy(v[:, who, :, 0, :], bbx[:, gs, 0:CH]))
                for e in range(1, L):
                    link(ve.tensor_mul(v[:, who, :, e, :], bbx[:, gs, 0:CH], wide(pw[:, 0, e, gs], 8)))
                    link(ve.tensor_mul(t[:, 0:8], bby[:, gs], wide(pw[:, 1, e, gs], 8)))
                    link(ve.tensor_add(v[:, who, :, e, :], v[:, who, :, e, :], t[:, 0:8]))
                eng.sem_inc(v_ready[who], 1)

            @block.gpsimd
            def _(pool):
                link = Chain(c, pool, "st_pool_link")
                ve = nc.gpsimd
                link(ve.memset(bbx[:], 0.0))
                link(ve.memset(kz[:], 0.0))
                pool.wait_ge(b_loaded, 64)
                link(ve.tensor_scalar(by[:], by[:], c.sign[:, 0:1], -1.0, ALU.mult, ALU.mult))
                pool.wait_ge(pw_ready, 1)
                link(ve.tensor_mul(tmp_p, by[:], wide(f[:, 1])))
                link(ve.tensor_mul(bbx[:, :, 0:CH], bx[:], wide(f[:, 0])))
                link(ve.tensor_add(bbx[:, :, 0:CH], bbx[:, :, 0:CH], tmp_p))
                link(ve.tensor_mul(tmp_p, bx[:], wide(f[:, 1])))
                link(ve.tensor_mul(bby[:], by[:], wide(f[:, 0])))
                link(ve.tensor_sub(bby[:], bby[:], tmp_p))
                pool.sem_inc(b_ready, 1)
                done = 0
                for k, who in v_order:
                    if who == 0:
                        make_v(pool, ve, link, k, who, done, tmp_p)
                        done += 1
                pair = slice(G, A_COLS)
                link(ve.tensor_copy(c.a1p[:, 0:2], pw[:, :, 1, pair]))
                link(ve.tensor_copy(c.a8p[:, 0:2, 0], pw[:, :, L, pair]))
                for j in range(1, SUP):
                    x, y, out = c.a8p[:, 0:2, j - 1], c.a8p[:, 0:2, 0], c.a8p[:, 0:2, j]
                    link(ve.tensor_mul(q1[:], x[:, 0], y[:, 0]))
                    link(ve.tensor_mul(q2[:], x[:, 1], y[:, 1]))
                    link(ve.tensor_sub(out[:, 0], q1[:], q2[:]))
                    link(ve.tensor_mul(q1[:], x[:, 0], y[:, 1]))
                    link(ve.tensor_mul(q2[:], x[:, 1], y[:, 0]))
                    link(ve.tensor_add(out[:, 1], q1[:], q2[:]))
                link(ve.tensor_scalar(c.a1p[:, 2], c.a1p[:, 1], -1.0, None, ALU.mult))
                link(ve.tensor_scalar(c.a8p[:, 2], c.a8p[:, 1], -1.0, None, ALU.mult))

            @block.tensor
            def _(pe):
                norm[1](pe)
                pe.wait_ge(norm[3], KD)
                pe.wait_ge(rows_ready, 1)
                for i in range(2):
                    nc.tensor.transpose(ps[:, 0, i * P:i * P + G], zg[:, i].rearrange("g d n -> g (d n)"), c.ident[0:G, 0:G])
                    nc.tensor.transpose(ps[:, 0, i * P + G:i * P + A_COLS], zp[:, i], c.ident[0:GP, 0:GP])
                    mm = nc.tensor.transpose(ps[:, 0, 2 * P + i * G:2 * P + (i + 1) * G], ag[:, i].rearrange("g d n -> g (d n)"), c.ident[0:G, 0:G])
                mm.then_inc(turned, 1)
                for w in range(2):
                    for k in range(KD):
                        mm = nc.tensor.transpose(ps[:, 1 + w * 2 + k // 4, k % 4 * P:(k % 4 + 1) * P],
                                                 crow[:, k, w].rearrange("p i n -> p (i n)"), c.ident[:])
                    mm.then_inc(c_turned, 1)
                seen = [0, 0]
                for n, (k, who) in enumerate(v_order):
                    seen[who] += 1
                    pe.wait_ge(v_ready[who], seen[who])
                    for g in range(8):
                        if g % 4 == 0 and n >= 1:
                            pe.wait_ge(v_kept, 2 * n + g // 4 - 1)
                        mm = nc.tensor.transpose(ps[:, 5 + g // 4, g % 4 * P:(g % 4 + 1) * P],
                                                 v[:, who, g].rearrange("p e c -> p (e c)"), c.ident[:])
                        if g % 4 == 3:
                            mm.then_inc(v_turned[who], 1)
                pe.wait_ge(m_ready, 1)
                pe.wait_ge(c_kept, 4)
                for g in range(G):
                    q, j = g % 4, g // 4
                    mm = nc.tensor.matmul(ps[32 * q:32 * q + 32, j // 4, j % 4 * P:(j % 4 + 1) * P], bbx[:, g],
                                          c.mx[:, g, 0:L].rearrange("p e c -> p (e c)"), start=True, stop=True)
                    if g % 16 == 15:
                        mm.then_inc(k_done, 1)

            @block.vector
            def _(dve):
                link = Chain(c, dve, "st_link")
                ve = nc.vector
                norm[2](dve)
                dve.wait_ge(act_sem, 2)
                for i in range(2):
                    link(ve.tensor_scalar(zg[:, i], ag[:, i], dg[:, 0:1], None, ALU.mult))
                    for w in range(2):
                        link(ve.tensor_scalar(zp[:, i, w * NS:(w + 1) * NS], ap_[:, i, w * NS:(w + 1) * NS], dp[:, w:w + 1], None, ALU.mult))
                dve.sem_inc(rows_ready, 1)
                dve.wait_ge(turned, 1)
                link(ve.tensor_copy(z[:], ps[:, 0, 0:2 * P].rearrange("p (i x) -> p i x", i=2)[:, :, 0:A_COLS]))
                link(ve.tensor_copy(al[:], ps[:, 0, 2 * P:2 * P + 2 * G].rearrange("p (i x) -> p i x", i=2)))
                for shift, out in ((0.0, s2), (0.25, s3)):
                    link(ve.tensor_scalar(s1[:], z[:, 1], 1.0 / TWO_PI, shift, ALU.mult, ALU.add))
                    link(ve.tensor_scalar(s1[:], s1[:], MAGIC, None, ALU.add))
                    link(ve.tensor_scalar(s1[:], s1[:], -MAGIC, None, ALU.add))
                    src = z[:, 1]
                    for part in split(TWO_PI, 3):
                        link(ve.scalar_tensor_tensor(out[:], s1[:], -part, src, ALU.mult, ALU.add))
                        src = out[:]
                    link(ve.tensor_scalar(out[:], out[:], shift * TWO_PI, float(np.float32(3.1415925)), ALU.add, ALU.min))
                    ve.tensor_scalar(out[:], out[:], -float(np.float32(3.1415925)), None, ALU.max).then_inc(trig, 1)
                    dve.wait_ge(trig, 1 if out is s2 else 2)
                link(ve.tensor_scalar(s1[:], z[:, 0], float(1.0 / np.log(2.0)), MAGIC, ALU.mult, ALU.add))
                link(ve.tensor_scalar(s1[:], s1[:], -MAGIC, None, ALU.add))
                link(ve.tensor_scalar(s1[:], s1[:], -126.0, 127.0, ALU.max, ALU.min))
                src = z[:, 0]
                for part in split(float(np.log(2.0)), 3):
                    link(ve.scalar_tensor_tensor(s4[:], s1[:], -part, src, ALU.mult, ALU.add))
                    src = s4[:]
                link(ve.tensor_scalar(ki[:], s1[:], 127.0, None, ALU.add))
                link(ve.tensor_scalar(ki[:], ki[:], 23, None, ALU.logical_shift_left))
                fact = [1.0]
                for i in range(1, 10):
                    fact.append(fact[-1] * i)
                link(ve.tensor_scalar(s1[:], s4[:], 1.0 / fact[9], None, ALU.mult))
                for i in range(8, 0, -1):
                    link(ve.scalar_tensor_tensor(s1[:], s1[:], 1.0 / fact[i], s4[:], ALU.add, ALU.mult))
                link(ve.tensor_scalar(s1[:], s1[:], 1.0, None, ALU.add))
                link(ve.tensor_mul(s1[:], s1[:], ki[:].bitcast(F32)))
                link(ve.memset(pw[:, 0, 0], 1.0))
                link(ve.memset(pw[:, 1, 0], 0.0))
                dve.wait_ge(cos_sem, 2)
                link(ve.tensor_mul(pw[:, 0, 1], s1[:], s3[:]))
                link(ve.tensor_mul(pw[:, 1, 1], s1[:], s2[:]))

                def power(out, x, y):
                    w = out.shape[-1]
                    link(ve.tensor_mul(s1[:, 0:w], x[:, 0], y[:, 0]))
                    link(ve.tensor_mul(s4[:, 0:w], x[:, 1], y[:, 1]))
                    link(ve.tensor_sub(out[:, 0], s1[:, 0:w], s4[:, 0:w]))
                    link(ve.tensor_mul(s1[:, 0:w], x[:, 0], y[:, 1]))
                    link(ve.tensor_mul(s4[:, 0:w], x[:, 1], y[:, 0]))
                    link(ve.tensor_add(out[:, 1], s1[:, 0:w], s4[:, 0:w]))
                for e in range(2, L + 1):
                    power(pw[:, :, e], pw[:, :, e - 1], pw[:, :, 1])
                x, y = al[:, 0], al[:, 1]
                n1, n2, den, t = s1[:, 0:G], s2[:, 0:G], s3[:, 0:G], s4[:, 0:G]
                link(ve.tensor_mul(den, x, x))
                link(ve.tensor_mul(t, y, y))
                link(ve.tensor_add(den, den, t))
                link(ve.reciprocal(den, den))
                link(ve.tensor_scalar(n1, pw[:, 0, 1, 0:G], -1.0, None, ALU.add))
                link(ve.tensor_mul(n2, n1, x))
                link(ve.tensor_mul(t, pw[:, 1, 1, 0:G], y))
                link(ve.tensor_add(n2, n2, t))
                link(ve.tensor_mul(f[:, 0], n2, den))
                link(ve.tensor_mul(n2, pw[:, 1, 1, 0:G], x))
                link(ve.tensor_mul(t, n1, y))
                link(ve.tensor_sub(n2, n2, t))
                link(ve.tensor_mul(f[:, 1], n2, den))
                dve.sem_inc(pw_ready, 1)
                for w in range(2):
                    dve.wait_ge(c_turned, w + 1)
                    for h in range(2):
                        dst, bank = (cx, cy)[w][:, h * 32:(h + 1) * 32], ps[:, 1 + w * 2 + h, :].rearrange("p (g c) -> p g c", c=CH)
                        if w == 0:
                            ve.tensor_scalar(dst, bank, c.sign[:, 0:1], None, ALU.mult).then_inc(c_kept, 1)
                        else:
                            ve.tensor_scalar(dst, bank, -1.0, None, ALU.mult).then_inc(c_kept, 1)
                dve.wait_ge(c_kept, 4)
                link(ve.tensor_copy(c.mx[:, :, 0, :], cx[:]))
                for e in range(1, L + 1):
                    link(ve.tensor_mul(c.mx[:, :, e, :], cx[:], wide(pw[:, 0, e, 0:G])))
                    link(ve.tensor_mul(tmp[:], cy[:], wide(pw[:, 1, e, 0:G])))
                    link(ve.tensor_add(c.mx[:, :, e, :], c.mx[:, :, e, :], tmp[:]))
                dve.sem_inc(m_ready, 1)
                dve.wait_ge(b_ready, 1)
                done = 0
                for k, who in v_order:
                    if who == 1:
                        make_v(dve, ve, link, k, who, done, tmp)
                        done += 1
                for j in range(4):
                    dve.wait_ge(k_done, j + 1)
                    for q in range(4):
                        ins = ve.tensor_copy(kz[32 * q:32 * q + CH, 4 * j:4 * j + 4, (L - 1) * CH:],
                                             ps[32 * q:32 * q + CH, j, :].rearrange("p (g x) -> p g x", g=4))
                    ins.then_inc(k_kept, 1)


def stage_ssm(c):
    nc, ps = c.nc, c.psum
    dram = c.dram
    sent, back = [c.sem(f"ss_u_sent{e}") for e in range(L)], c.sem("ss_u_back")
    cleared, laid = c.sem("ss_cleared"), c.sem("ss_laid")
    xd, xk = c.sem("ss_x_done"), c.sem("ss_x_kept")
    t_in = c.sem("ss_t_in")
    s_in, s_turned, s_kept = c.sem("ss_state_in"), c.sem("ss_state_turned"), c.sem("ss_state_kept")
    with ExitStack() as mine:
        def buf(name, shape, ctx=mine):
            return c.buf("ss_" + name, shape, ctx=ctx)
        ut = buf("ut", [P, G, COLS])
        x = buf("x", [P, 2, GP, COLS])
        h0 = buf("h0", [P, 2, GP, NB])
        with ExitStack() as here:
            xc = buf("xc", [P, L, KD, COLS], here)
            srow = buf("state_rows", [GP, 2 * NB, P], here)
            with nc.Block() as block:
                @block.vector
                def _(dve):
                    nc.vector.memset(xc[:, :, :, NCH:], 0.0).then_inc(cleared, 1)
                    dve.wait_ge(cleared, 1)
                    nc.vector.tensor_copy(xc[:, L - 1, :, NCH:NCH + NB], c.xT[:, :, SEQ:T])
                    nc.vector.tensor_copy(xc[:, 0, :, NCH + NB:], c.xT[:, :, SEQ:T])
                    for e in range(L):
                        nc.vector.tensor_copy(xc[:, e, :, 0:NCH], c.xT[:, :, 0:SEQ].rearrange("p k (n t) -> p t k n", t=L)[:, L - 1 - e])
                        dve.drain().then_inc(laid, 1)
                    dve.wait_ge(s_turned, 1)
                    nc.vector.tensor_copy(h0[:], ps[:, 7, :].rearrange("p (b i q) -> p i q b", i=2, q=GP)).then_inc(s_kept, 1)
                    for k in range(KD):
                        for par in range(2):
                            dve.wait_ge(xd, k + 1)
                            src = ps[0:NS, k % 3 * 2:k % 3 * 2 + 2, 0:4 * COLS].rearrange("p b (q w x) -> p b q w x", q=2, w=2)
                            for b in range(2):
                                ins = nc.vector.tensor_copy(x[par * NS:(par + 1) * NS, 0, k * 4 + b * 2:k * 4 + b * 2 + 2, :], src[:, b, :, par, :])
                        ins.then_inc(xk, 1)

                @block.scalar
                def _(act):
                    for k in range(KD):
                        for par in range(2):
                            act.wait_ge(xk, k + 1)
                            src = ps[NS:P, k % 3 * 2:k % 3 * 2 + 2, 0:4 * COLS].rearrange("p b (q w x) -> p b q w x", q=2, w=2)
                            for b in range(2):
                                ins = nc.scalar.copy(x[par * NS:(par + 1) * NS, 1, k * 4 + b * 2:k * 4 + b * 2 + 2, :], src[:, b, :, par, :])
                        ins.then_inc(cleared, 1)

                @block.sync
                def _(sp):
                    sp.dma_start(srow[:], dram["state_ssm"][0].rearrange("b i (q w) n -> q (b i) (w n)", w=2)).then_inc(s_in, 16)
                    for e in range(L):
                        sp.wait_ge(laid, e + 1)
                        sp.dma_start(c.scratch_u[:, e], xc[:, e].rearrange("p k x -> p (k x)")).then_inc(sent[e], 16)
                    for e in range(L):
                        sp.wait_ge(sent[e], 16)
                        sp.dma_start(ut[e * CH:(e + 1) * CH].rearrange("p (g k) x -> p g (k x)", k=KD),
                                     c.scratch_u.rearrange("(g c) e x -> e c g x", c=CH)[e]).then_inc(back, 16)

                @block.tensor
                def _(pe):
                    pe.wait_ge(s_in, 16)
                    for i in range(2 * NB):
                        mm = nc.tensor.transpose(ps[:, 7, i * GP:(i + 1) * GP], srow[:, i, :], c.ident[0:GP, 0:GP])
                    mm.then_inc(s_turned, 1)
                    pe.wait_ge(back, 16 * L)
                    for k in range(KD):
                        if k >= 3:
                            pe.wait_ge(cleared, 1 + k - 2)
                        for g in range(8):
                            mm = nc.tensor.matmul(ps[:, k % 3 * 2 + g // 4, g % 4 * COLS:(g % 4 + 1) * COLS],
                                                  c.wb[:, k * 8 + g, :], ut[:, g * KD + k, :], start=True, stop=True)
                        mm.then_inc(xd, 1)

        with ExitStack() as here:
            ta, tb = buf("ta", [P, 2, GP, SUP], here), buf("tb", [P, 2, GP, SUP], here)
            with nc.Block() as block:
                def carry(eng, ve, link, q0, q1):
                    qs = slice(q0, q1)
                    xs = x[:, :, qs, 0:NCH].rearrange("p i q (s j) -> p i q s j", j=SUP)

                    def axpy(out, src, table, w):
                        complex_axpy(ve, link, out, src, table, ta[:, :, qs, 0:w], tb[:, :, qs, 0:w])
                    for j in range(1, SUP):
                        axpy(xs[:, :, :, :, j], xs[:, :, :, :, j - 1], c.a8p[:, :, 0, qs], SUP)
                    for s in range(1, SUP):
                        axpy(xs[:, :, :, s:s + 1, SUP - 1], xs[:, :, :, s - 1:s, SUP - 1], c.a8p[:, :, SUP - 1, qs], 1)
                    for j in range(SUP - 1):
                        axpy(xs[:, :, :, 1:, j], xs[:, :, :, 0:SUP - 1, SUP - 1], c.a8p[:, :, j, qs], SUP - 1)
                    axpy(x[:, :, qs, NCH + NB:], h0[:, :, qs], c.a1p[:, :, qs], NB)

                @block.vector
                def _(dve):
                    carry(dve, nc.vector, Chain(c, dve, "ss_link"), 0, DVE_PAIRS)

                @block.gpsimd
                def _(pool):
                    carry(pool, nc.gpsimd, Chain(c, pool, "ss_pool_link"), DVE_PAIRS, GP)

                @block.sync
                def _(sp):
                    for e in range(L):
                        sp.dma_start(c.wb[e * CH:(e + 1) * CH], c.scratch_k[:, :, e * CH:e * CH + P].rearrange("g c x -> c g x")).then_inc(t_in, 16)

        hx_done, y_done, y_kept, y_sent = c.sem("ss_hx_done"), c.sem("ss_y_done"), c.sem("ss_y_kept"), c.sem("ss_y_sent")
        y_back, skipped, st_done = [c.sem(f"ss_y_back{i}") for i in range(2)], c.sem("ss_skipped"), c.sem("ss_st_done")
        st_kept, st_out, zeroed, hi_done = c.sem("ss_st_kept"), c.sem("ss_st_out"), c.sem("ss_zeroed"), c.sem("ss_hx_im_done")
        with ExitStack() as here:
            hx = buf("hx", [P, 2, 8, HCOLS], here)
            yt = buf("yt", [P, 2, 8, 2, HCOLS], here)
            yc = buf("yc", [P, 2, L, 2, HCOLS], here)
            orow = buf("out_rows", [GP, 2 * NB + 2, P], here)
            with nc.Block() as block:
                @block.sync
                def _(sp):
                    for j in range(KD // 2):
                        sp.wait_ge(y_kept, 4 * (j + 1))
                        for t in range(L):
                            sp.dma_start(c.scratch_y[j].rearrange("g c t x -> t c g x")[t],
                                         yt[t * CH:(t + 1) * CH, j % 2].rearrange("p g k x -> p g (k x)")).then_inc(y_sent, 16)
                        sp.wait_ge(y_sent, 16 * L * (j + 1))
                        if j >= 2:
                            sp.wait_ge(skipped, 2 * (j - 1))
                        sp.dma_start(yc[:, j % 2].rearrange("p t k x -> p t (k x)"),
                                     c.scratch_y[j].rearrange("g c t x -> (g c) t x")).then_inc(y_back[j % 2], 16)
                    sp.wait_ge(st_kept, 5)
                    sp.dma_start(dram["ssm_sample"][0].rearrange("b i (q w) n -> q (b i) (w n)", w=2), orow[:, 0:2 * NB]).then_inc(st_out, 16)
                    sp.dma_start(dram["ssm_prompt"][0, 0].rearrange("i (q w) n -> q i (w n)", w=2), orow[:, 2 * NB:]).then_inc(st_out, 16)
                    sp.wait_ge(st_out, 32)

                @block.vector
                def _(dve):
                    nc.vector.memset(hx[:], 0.0).then_inc(zeroed, 1)
                    dve.wait_ge(zeroed, 1)

                    def skip(k):
                        dve.wait_ge(y_back[k // 2 % 2], 16 * (k // 4 + 1))
                        col = c.cols[:, k:k + 1]
                        nc.vector.scalar_tensor_tensor(c.y[:, k, 0:SEQ].rearrange("p (n t) -> p t n", t=L),
                                                       c.xT[:, k, 0:SEQ].rearrange("p (n t) -> p t n", t=L), col,
                                                       yc[:, k // 2 % 2, :, k % 2, 0:NCH], ALU.mult, ALU.add)
                        nc.vector.scalar_tensor_tensor(c.y[:, k, SEQ:T], c.xT[:, k, SEQ:T], col, yc[:, k // 2 % 2, 0, k % 2, NCH:],
                                                       ALU.mult, ALU.add).then_inc(skipped, 1)

                    for k in range(KD):
                        if k >= 2:
                            dve.wait_ge(y_done, 2 * (k - 1))
                        for i in range(2):
                            for par in range(2):
                                rows = slice(par * NS, (par + 1) * NS)
                                dst = hx[i * NS:(i + 1) * NS, k % 2].rearrange("p (q w) x -> p w q x", w=2)[:, par]
                                nc.vector.tensor_copy(dst[:, :, 1:NCH], x[rows, i, k * 4:k * 4 + 4, 0:NCH - 1])
                                ins = nc.vector.tensor_copy(dst[:, :, NCH:], h0[rows, i, k * 4:k * 4 + 4, :])
                        ins.then_inc(hx_done, 1)
                        if k >= 4:
                            skip(k - 4)
                    for k in range(KD - 4, KD):
                        skip(k)
                    for n in range(5):
                        dve.wait_ge(st_done, n + 1)
                        w = 4 if n < 4 else 2
                        nc.vector.tensor_copy(orow[:, 4 * n:4 * n + w, :], ps[0:GP, 4 + n % 2, 0:w * P].rearrange("p (j x) -> p j x", x=P)).then_inc(st_kept, 1)

                @block.scalar
                def _(act):
                    for k in range(KD):
                        if k >= 4:
                            act.wait_ge(y_sent, 16 * L * (k // 2 - 1))
                        for h in range(2):
                            act.wait_ge(y_done, 2 * k + h + 1)
                            nc.scalar.copy(yt[:, k // 2 % 2, h * 4:h * 4 + 4, k % 2, :],
                                           ps[:, k % 2 * 2 + h, 0:4 * HCOLS].rearrange("p (g x) -> p g x", g=4)).then_inc(y_kept, 1)

                @block.tensor
                def _(pe):
                    for k in range(KD):
                        if k == 0:
                            pe.wait_ge(t_in, 16 * L)
                        pe.wait_ge(hx_done, k + 1)
                        if k >= 2:
                            pe.wait_ge(y_kept, 2 * (k - 1))
                        for g in range(8):
                            out = ps[:, k % 2 * 2 + g // 4, g % 4 * HCOLS:(g % 4 + 1) * HCOLS]
                            nc.tensor.matmul(out, c.wb[:, k * 8 + g, :], ut[:, g * KD + k, 0:HCOLS], start=True, stop=False)
                            mm = nc.tensor.matmul(out, c.mx[:, k * 8 + g, 1:].rearrange("p e c -> p (e c)"), hx[:, k % 2, g, :],
                                                  start=False, stop=True)
                            if g % 4 == 3:
                                mm.then_inc(y_done, 1)
                    for n in range(5):
                        if n >= 2:
                            pe.wait_ge(st_kept, n - 1)
                        for j in range(4 if n < 4 else 2):
                            if n < 4:
                                b, i = divmod(n * 4 + j, 2)
                                src = x[:, i, :, NCH + NB + b]
                            else:
                                src = x[:, j, :, NCH - 1]
                            mm = nc.tensor.transpose(ps[0:GP, 4 + n % 2, j * P:(j + 1) * P], src, c.ident[:])
                        mm.then_inc(st_done, 1)


def stage_gelu(c, dst, src):
    nc = c.nc
    done = c.sem("gelu_done")
    with nc.Block() as block:
        @block.scalar
        def _(act):
            for k in range(KD):
                nc.scalar.activation(dst[:, k, :], src[:, k, :], ACT.Gelu_apprx_tanh).then_inc(done, 1)


def evac_glu(dst, y, bias):
    def make(c, name, filled, freed, per, iters, mine):
        nc, ps = c.nc, c.psum
        gated = c.sem(f"{name}_gated")
        tmp = c.buf(f"{name}_sig", [P, 4, HALF], ctx=mine)

        def act_prog(act):
            act.sem_inc(gated, 4)
            with act.Fori(0, iters) as it:
                for b in range(8 * per):
                    act.wait_ge(filled, it * (8 * per) + b + 1)
                    act.wait_ge(gated, it * (8 * per) + b + 1)
                    nc.scalar.activation(tmp[:, b % 4, :], ps[:, b % 8, 0:HALF], ACT.Sigmoid,
                                         bias=bias[:, bass.ds(it * (4 * per) + b // 2, 1)]).then_inc(freed[b % 2], 1)

        def dve_prog(dve):
            with dve.Fori(0, iters) as it:
                for b in range(8 * per):
                    m, h = b // 2, b % 2
                    dve.wait_ge(freed[h], it * (4 * per) + m + 5)
                    tile, cols = bass.ds(it * (4 * per) + m, 1), slice(h * HALF, (h + 1) * HALF)
                    nc.vector.tensor_mul(dst[:, tile, cols], y[:, tile, cols], tmp[:, b % 4:b % 4 + 1, :]).then_inc(gated, 1)
        return act_prog, dve_prog, [gated]
    return make


def stage_cols(c):
    nc, ps = c.nc, c.psum
    got, turned, kept = c.sem("cols_in"), c.sem("cols_turned"), c.sem("cols_kept")
    with ExitStack() as mine:
        rows = c.buf("cols_rows", [2 * KD, P], ctx=mine)
        with nc.Block() as block:
            @block.sync
            def _(sp):
                for i, name in enumerate(("s5_d", "s5_b_glu")):
                    sp.dma_start(rows[i * KD:(i + 1) * KD], c.dram[name].rearrange("o (k p) -> (o k) p", p=P)).then_inc(got, 16)

            @block.tensor
            def _(pe):
                pe.wait_ge(got, 32)
                nc.tensor.transpose(ps[:, 0, 0:2 * KD], rows[:], c.ident[0:2 * KD, 0:2 * KD]).then_inc(turned, 1)

            @block.vector
            def _(dve):
                dve.wait_ge(turned, 1)
                nc.vector.tensor_copy(c.cols[:], ps[:, 0, 0:2 * KD]).then_inc(kept, 1)


def stage_s5(c):
    nc = c.nc
    c.scratch_k = nc.dram_tensor("scratch_k", (G, CH, (2 * L - 1) * CH), F32, kind="Internal").ap()
    c.scratch_u = nc.dram_tensor("scratch_u", (P, L, KD * COLS), F32, kind="Internal").ap()
    c.scratch_y = nc.dram_tensor("scratch_y", (KD // 2, 8, CH, L, 2 * HCOLS), F32, kind="Internal").ap()
    stage_cols(c)
    with ExitStack() as tables:
        c.wb = c.buf("wb", [P, G, P], ctx=tables)
        c.mx = c.buf("mx", [P, G, L + 1, CH], ctx=tables)
        c.a1p = c.buf("a1p", [P, 3, GP], ctx=tables)
        c.a8p = c.buf("a8p", [P, 3, SUP, GP], ctx=tables)
        stage_ssm_tables(c, norm_parts(c, "ssm_in", c.hT, c.xT, 1, 0, c.y[:, 0:4], c.y[:, 4]))
        stage_ssm(c)
    stage_gelu(c, c.y, c.y)


def program(nc, dram):
    with ExitStack() as ctx:
        c = Core(nc, ctx, dram)
        c.ident = c.buf("ident", [P, P])
        c.causal = c.buf("causal", [P, SEQ])
        c.cmask = c.buf("cmask", [P, 2 * GRP * QT * NCP])
        c.own = c.buf("own", [P, NB])
        c.group = c.buf("group", [P, P])
        c.over = c.buf("over", [P, NSEL])
        c.blk = c.buf("blk", [P, NSEL])
        c.sign = c.buf("sign", [P, 1])
        c.g_rows = c.buf("g_rows", [8 * KD, P])
        c.g_cols = c.buf("g_cols", [P, 8 * KD])
        c.ones = c.buf("ones", [P, P])
        c.eps = c.buf("eps", [P, 1])
        c.hT = c.buf("hT", [P, KD, T])
        c.xT = c.buf("xT", [P, KD, T])
        c.pages = c.buf("pages", [1, NB * NPAGE], I32)
        with c.part():
            stage_inputs(c)
        with c.part():
            stage_nsa(c)
        with c.part(), ExitStack() as mine:
            c.w = c.buf("w0", [P, 2, CK, NG], ctx=mine)
            out = Linear(c, "nsa_o", columns(c.dram["nsa_w_o"][0]), KD, D // NG, 2)
            up = mlp_up(c, 0)
            with ExitStack() as here:
                y = c.buf("nsa_y", [P, KD, T], ctx=here)
                stage_mix_out(c, out, c.oT, evac_copy(y), y, 0, up)
            stage_mlp(c, 0, up)
        with ExitStack() as outer:
            c.y = c.buf("ssm_y", [P, KD, T], ctx=outer)
            c.cols = c.buf("ssm_cols", [P, 2 * KD], ctx=outer)
            with c.part():
                stage_s5(c)
            with c.part(), ExitStack() as mine:
                c.w = c.buf("w1", [P, 2, CK, NG], ctx=mine)
                glu = Linear(c, "glu", columns(c.dram["s5_w_glu"][0]), KD, D // NG, 2)
                up = mlp_up(c, 1)
                stage_mix_out(c, glu, c.y, evac_glu(c.xT, c.y, c.cols[:, KD:]), c.xT, 1, up)
                stage_mlp(c, 1, up)
                stage_outputs(c)


OUTPUTS = [
    ("y_prompt", (1, SEQ, D)), ("y_sample", (NB, 1, D)),
    ("kv_cmp_prompt", (1, 1, SEQ, 2, NKV, HD)), ("kv_cmp_sample", (1, NB, 1, 2, NKV, HD)),
    ("kv_sel_prompt", (1, 1, SEQ, 2, NKV, HD)), ("kv_sel_sample", (1, NB, 1, 2, NKV, HD)),
    ("kv_win_prompt", (1, 1, WIN, 2, NKV, HD)), ("kv_win_sample", (1, NB, WIN, 2, NKV, HD)),
    ("ssm_prompt", (1, 1, 2, G, NS)), ("ssm_sample", (1, NB, 2, G, NS)),
]


def kernel(**inputs):
    import concourse.bacc as bacc
    from concourse.bass_utils import run_bass_kernel_spmd

    nc = bacc.Bacc("TRN2", target_bir_lowering=False, num_devices=1)
    arrays, dram = {}, {}
    for name, value in [*inputs.items(), *constants().items()]:
        a = np.ascontiguousarray(value)
        arrays[f"in_{name}"] = a
        dram[name] = nc.dram_tensor(f"in_{name}", a.shape, mybir.dt.from_np(a.dtype), kind="ExternalInput").ap()
    for name, shape in OUTPUTS:
        dram[name] = nc.dram_tensor(f"out_{name}", shape, F32, kind="ExternalOutput").ap()
    program(nc, dram)
    r = run_bass_kernel_spmd(nc, [arrays], core_ids=[0])
    return tuple(r.results[0][f"out_{name}"] for name, _ in OUTPUTS)
```

```python
from contextlib import ExitStack, contextmanager

import numpy as np

import concourse.bass as bass
from concourse import mybir

F32 = mybir.dt.float32
I32 = mybir.dt.int32
ACT = mybir.ActivationFunctionType
ALU = mybir.AluOpType
AX = mybir.AxisListType

P = 128
D = 1024
SEQ = 512
NB = 8
T = SEQ + NB
HALF = T // 2
KD = D // P
QT = SEQ // P
DFF = 4 * D
KF = DFF // P
NH, HD, NKV, GRP = 16, 64, 4, 4
KVW = NKV * HD
ROW = 2 * KVW
PAST, PAGE = 1024, 128
NPAGE = PAST // PAGE
POOL_PAGES = (5 * NB * NPAGE + 3) // 4
WIN = 512
STRIDE = 16
NSUB = PAST // STRIDE
NCS = NSUB - 1
NSUBP = SEQ // STRIDE
NCP = NSUBP - 1
SELB = 64
NSEL = PAST // SELB + 1
SCALE = HD ** -0.5
EPS = 1e-6
BIG = 1e30
G, CH, NS = 64, 16, 64
GP = G // 2
L = 8
NCH = SEQ // L
SUP = 8


def constants():
    half = HD // 2
    inv = (np.float32(10000.0) ** (-np.arange(half, dtype=np.float32) / np.float32(half))).astype(np.float32)
    pos = np.concatenate([np.arange(SEQ), np.full(NB, PAST)]).astype(np.float32)
    ang = pos[:, None] * inv[None, :]
    cos, sin = np.cos(ang).astype(np.float32), np.sin(ang).astype(np.float32)
    rows = np.zeros((P, QT + 1, 2, half), np.float32)
    for t in range(QT + 1):
        n = P if t < QT else NB
        rows[:n, t, 0], rows[:n, t, 1] = cos[t * P:t * P + n], sin[t * P:t * P + n]
    cos_t = np.tile(cos.T, (4, 1))
    sin_t = np.tile(np.concatenate([-sin.T, sin.T]), (2, 1))
    swap = np.zeros((P, P), np.float32)
    for m in range(P):
        swap[m // HD * HD + (m % HD + half) % HD, m] = 1.0
    q = np.arange(P)
    causal = np.where(np.arange(SEQ)[None, :] - (SEQ - P) > q[:, None], BIG, 0.0).astype(np.float32)
    qpos = (np.arange(QT)[None, :] * P + q[:, None])[:, None, :, None]
    cend = (np.arange(NCP) * STRIDE + 2 * STRIDE - 1)[None, None, None, :]
    seen = np.broadcast_to(cend <= qpos, (P, GRP, QT, NCP))
    cmask = np.stack([np.where(seen, 0.0, BIG), seen.astype(np.float32)], 1).astype(np.float32)
    row_b = np.arange(P) // NH
    own = np.where(row_b[:, None] == np.arange(NB)[None, :], 0.0, BIG).astype(np.float32)
    group = (np.arange(P)[:, None] // GRP == np.arange(P)[None, :] // GRP).astype(np.float32)
    c0, s0 = np.arange(NCS) * STRIDE, np.arange(NSEL) * SELB
    over = np.zeros((P, NSEL), np.float32)
    over[:NCS] = (c0[:, None] < s0[None] + SELB) & (c0[:, None] + 2 * STRIDE > s0[None])
    blk = np.broadcast_to(np.arange(NSEL, dtype=np.float32), (P, NSEL))
    sign = np.where(np.arange(P) < NS, 1.0, -1.0).astype(np.float32)[:, None]
    return {
        "c_ident": np.eye(P, dtype=np.float32), "c_swap": swap, "c_ropeT": np.stack([cos_t, sin_t], 1),
        "c_rope": rows, "c_causal": causal, "c_cmask": cmask.reshape(P, -1), "c_own": own,
        "c_group": group, "c_over": over, "c_blk": np.ascontiguousarray(blk), "c_sign": sign,
    }


class Core:

    def __init__(self, nc, ctx, dram):
        self.nc, self.ctx, self.dram, self.sems = nc, ctx, dram, []
        self.psum = ctx.enter_context(nc.psum_tensor("psum", [P, 8, 512], F32))

    def buf(self, name, shape, dt=F32, ctx=None):
        return (ctx or self.ctx).enter_context(self.nc.sbuf_tensor(name, shape, dt))

    def sem(self, name):
        self.sems.append(self.nc.alloc_semaphore(name=name))
        return self.sems[-1]

    @contextmanager
    def part(self):
        self.sems = []
        yield
        self.nc.clear_and_free_semaphores(self.sems)
        self.nc.all_engine_barrier()


def rows_of(t):
    return P if t < QT else NB


def stage_inputs(c):
    nc, ps = c.nc, c.psum
    tables, loaded, x_in = c.sem("tables_loaded"), c.sem("const_loaded"), [c.sem(f"x_in{t}") for t in range(QT + 1)]
    turned, kept = c.sem("x_turned"), c.sem("x_kept")
    preset = c.sem("x_preset")
    s5_in = c.sem("s5_rows_in")
    with ExitStack() as mine:
        xr = c.buf("x_rows", [P, QT + 1, D], ctx=mine)
        g_rows = c.buf("g_rows", [8 * KD, P], ctx=mine)
        a_g, a_p, d_rows = c.buf("a_g", [G, 2, 2, NS], ctx=mine), c.buf("a_p", [GP, 2, P], ctx=mine), c.buf("d_rows", [2 * KD, P], ctx=mine)
        with nc.Block() as block:
            @block.sync
            def _(sp):
                sp.dma_start(c.ident[:], c.dram["c_ident"]).then_inc(loaded, 16)
                sp.dma_start(g_rows[:], c.dram["norm_g"].rearrange("l w (k p) -> (l w k) p", p=P)).then_inc(loaded, 16)
                for t in range(QT):
                    sp.dma_start(xr[:, t, :], c.dram["x_prompt"][0, t * P:(t + 1) * P, :]).then_inc(x_in[t], 16)
                sp.dma_start(xr[0:NB, QT, :], c.dram["x_sample"][:, 0, :]).then_inc(x_in[QT], 16)
                for b, name in ((c.causal[:], "c_causal"), (c.cmask[:], "c_cmask"), (c.own[:], "c_own"),
                                (c.group[:], "c_group"), (c.over[:], "c_over"), (c.blk[:], "c_blk"),
                                (c.sign[:], "c_sign")):
                    sp.dma_start(b, c.dram[name]).then_inc(tables, 16)
                sp.dma_start(c.pages[:], c.dram["page_table"].rearrange("b p -> (b p)")[None, :]).then_inc(tables, 16)
                for i, name in enumerate(("s5_a_re", "s5_a_im")):
                    a = c.dram[name][0]
                    for d in range(2):
                        sp.dma_start(a_g[:, i, d], a).then_inc(s5_in, 16)
                    sp.dma_start(a_p[:, i], a.rearrange("(q w) n -> q (w n)", w=2)).then_inc(s5_in, 16)
                for i, name in enumerate(("s5_d", "s5_b_glu")):
                    sp.dma_start(d_rows[i * KD:(i + 1) * KD], c.dram[name].rearrange("o (k p) -> (o k) p", p=P)).then_inc(s5_in, 16)
                sp.wait_ge(tables, 16 * 8)

            @block.tensor
            def _(pe):
                pe.wait_ge(loaded, 32)
                for i in range(2 * (QT + 1)):
                    t, kk = i // 2, i % 2
                    n = rows_of(t)
                    if kk == 0:
                        pe.wait_ge(x_in[t], 16)
                    if i >= 4:
                        pe.wait_ge(kept, i - 3)
                    for k in range(4):
                        last = nc.tensor.transpose(ps[:, i % 4, k * P:k * P + n],
                                                   xr[0:n, t, (kk * 4 + k) * P:(kk * 4 + k + 1) * P],
                                                   c.ident[0:n, 0:n])
                    last.then_inc(turned, 1)
                nc.tensor.transpose(ps[:, 4, 0:8 * KD], g_rows[:], c.ident[0:8 * KD, 0:8 * KD]).then_inc(turned, 1)
                pe.wait_ge(s5_in, 16 * 8)
                for i in range(2):
                    nc.tensor.transpose(ps[:, 5, i * P:i * P + G], a_g[:, i].rearrange("g d n -> g (d n)"), c.ident[0:G, 0:G])
                    nc.tensor.transpose(ps[:, 5, i * P + G:i * P + G + GP], a_p[:, i], c.ident[0:GP, 0:GP])
                nc.tensor.transpose(ps[:, 5, 2 * P:2 * P + 2 * KD], d_rows[:], c.ident[0:2 * KD, 0:2 * KD]).then_inc(turned, 1)

            @block.vector
            def _(dve):
                nc.vector.memset(c.ones[:], 1.0 / D).then_inc(preset, 1)
                nc.vector.memset(c.eps[:], EPS).then_inc(preset, 1)
                for i in range(2 * (QT + 1)):
                    t, kk = i // 2, i % 2
                    n = rows_of(t)
                    dve.wait_ge(turned, i + 1)
                    nc.vector.tensor_copy(c.hT[:, kk * 4:kk * 4 + 4, t * P:t * P + n],
                                          ps[:, i % 4, :].rearrange("p (k t) -> p k t", k=4)[:, :, 0:n]).then_inc(kept, 1)
                dve.wait_ge(turned, 2 * (QT + 1) + 1)
                nc.vector.tensor_copy(c.g_cols[:], ps[:, 4, 0:8 * KD]).then_inc(kept, 1)
                dve.wait_ge(turned, 2 * (QT + 1) + 2)
                nc.vector.tensor_copy(c.al[:], ps[:, 5, 0:2 * P].rearrange("p (i x) -> p i x", i=2)[:, :, 0:G + GP]).then_inc(kept, 1)
                nc.vector.tensor_copy(c.cols[:], ps[:, 5, 2 * P:2 * P + 2 * KD]).then_inc(kept, 1)


def rms_parts(c, name, src, sq, rs, src_ready=lambda eng: None):
    nc, ps = c.nc, c.psum
    squared, added, summed, rooted, ready = (c.sem(f"{name}_{x}") for x in ("squared", "added", "summed", "rooted", "ready"))
    rs = rs[:]

    def act_part(act):
        src_ready(act)
        for k in range(KD):
            if k >= 4:
                act.wait_ge(added, k - 3)
            nc.scalar.activation(sq[:, 3 if k == 0 else (k - 1) % 3, :], src[:, k, :], ACT.Square).then_inc(squared, 1)
        act.wait_ge(summed, 1)
        for h in range(2):
            nc.scalar.activation(rs[:, h * HALF:(h + 1) * HALF], ps[:, h, 0:HALF], ACT.Sqrt, bias=c.eps[:]).then_inc(rooted, 1)

    def pe_part(pe):
        pe.wait_ge(added, KD - 1)
        for h in range(2):
            mm = nc.tensor.matmul(ps[:, h, 0:HALF], c.ones[:], sq[:, 3, h * HALF:(h + 1) * HALF], start=True, stop=True)
        mm.then_inc(summed, 1)

    def dve_part(dve):
        src_ready(dve)
        for k in range(1, KD):
            dve.wait_ge(squared, k + 1)
            if k >= 2:
                dve.wait_ge(added, k - 1)
            nc.vector.tensor_add(sq[:, 3, :], sq[:, 3, :], sq[:, (k - 1) % 3, :]).then_inc(added, 1)
        dve.wait_ge(summed, 1)
        dve.wait_ge(rooted, 2)
        nc.vector.reciprocal(rs, rs).then_inc(ready, 1)
        dve.wait_ge(ready, 1)
    return act_part, pe_part, dve_part


def norm_parts(c, name, src, dst, layer, which, sq, rs):
    nc = c.nc
    act_part, pe_part, rms_dve = rms_parts(c, name, src, sq, rs)
    done = c.sem(f"{name}_done")

    def dve_part(dve):
        rms_dve(dve)
        for k in range(KD):
            col = (layer * 4 + which) * KD + k
            nc.vector.scalar_tensor_tensor(dst[:, k, :], src[:, k, :], c.g_cols[:, col:col + 1], rs[:],
                                           ALU.mult, ALU.mult).then_inc(done, 1)
    return act_part, pe_part, dve_part, done


def residual_parts(c, name, y, layer, which, sq, rs, src_ready):
    nc = c.nc
    act_part, pe_part, rms_dve = rms_parts(c, name, y, sq, rs, src_ready)
    scaled, done, done_dve = c.sem(f"{name}_scaled"), c.sem(f"{name}_done_pool"), c.sem(f"{name}_done_dve")

    def dve_part(dve):
        rms_dve(dve)
        for k in range(KD):
            col = (layer * 4 + which) * KD + k
            nc.vector.scalar_tensor_tensor(y[:, k, :], y[:, k, :], c.g_cols[:, col:col + 1], rs[:],
                                           ALU.mult, ALU.mult).then_inc(scaled, 1)
            if k % 2 == 1 and k > 1:
                dve.wait_ge(scaled, k)
                nc.vector.tensor_add(c.hT[:, k - 1, :], c.hT[:, k - 1, :], y[:, k - 1, :]).then_inc(done_dve, 1)
        dve.wait_ge(scaled, KD)
        nc.vector.tensor_add(c.hT[:, KD - 1, :], c.hT[:, KD - 1, :], y[:, KD - 1, :]).then_inc(done_dve, 1)

    def pool_part(pool):
        for k in (0, 1, 3, 5):
            pool.wait_ge(scaled, k + 1)
            nc.gpsimd.tensor_add(c.hT[:, k, :], c.hT[:, k, :], y[:, k, :]).then_inc(done, 1)
    return act_part, pe_part, dve_part, pool_part


CK = 8
NG = 512


class Linear:

    def __init__(self, c, name, weights, kt, groups, per):
        self.c, self.name, self.weights, self.kt, self.groups, self.per = c, name, weights, kt, groups, per
        self.nchunk = kt // CK
        self.loads, self.ahead = groups * self.nchunk, 0
        self.landed = [c.sem(f"{name}_w_landed{s}") for s in range(2)]
        self.read, self.filled = c.sem(f"{name}_w_read"), c.sem(f"{name}_bank_filled")
        self.freed = [c.sem(f"{name}_even_bank_freed"), c.sem(f"{name}_odd_bank_freed")]
        assert per * self.nchunk % 2 == 0 and groups % per == 0

    def load(self, sp, j):
        self.c.nc.sync.dma_start(self.c.w[:, j % 2], self.weights(j // self.nchunk, j % self.nchunk)).then_inc(self.landed[j % 2], 16)

    def wait_read(self, sp, j):
        g, chunk = divmod(j, self.nchunk)
        if chunk == self.nchunk - 1:
            sp.wait_ge(self.filled, 8 * (g + 1))
        else:
            sp.wait_ge(self.read, g * (self.nchunk - 1) + chunk + 1)

    def evacuated(self, eng):
        for sem in self.last:
            eng.wait_ge(sem, 4 + 8 * self.groups // len(self.last))

    def run(self, x, evac, before=None, after=None, then=None, side=None):
        c, nc, ps = self.c, self.c.nc, self.c.psum
        name, kt, nchunk, per, filled, freed = self.name, self.kt, self.nchunk, self.per, self.filled, self.freed
        w, body = c.w, per * nchunk
        with ExitStack() as mine:
            act_evac, dve_evac, self.last = evac(c, name, filled, freed, per, self.groups // per, mine)
            with nc.Block() as block:
                @block.sync
                def _(sp):
                    for j in range(self.ahead, self.loads):
                        if j >= 2:
                            self.wait_read(sp, j - 2)
                        self.load(sp, j)
                    if then is not None:
                        for j in range(2):
                            self.wait_read(sp, self.loads - 2 + j)
                            then.load(sp, j)
                        then.ahead = 2

                @block.tensor
                def _(pe):
                    if before is not None:
                        before[1](pe)
                    pe.sem_inc(freed[0], 4)
                    pe.sem_inc(freed[1], 4)
                    with pe.Fori(0, self.groups // per) as it:
                        for j in range(body):
                            s, chunk = j % 2, j % nchunk
                            pe.wait_ge(self.landed[s], it * (16 * body // 2) + 16 * (j // 2 + 1))
                            for k in range(CK):
                                kk = chunk * CK + k
                                if before is not None and j == 0:
                                    pe.wait_ge(before[3], kk + 1)
                                for m in range(NG // P):
                                    for h in range(2):
                                        bank = m * 2 + h
                                        if kk == 0:
                                            pe.wait_ge(freed[h], it * (4 * per) + (j // nchunk) * 4 + m + 1)
                                        mm = nc.tensor.matmul(ps[:, bank, 0:HALF], w[:, s, k, m * P:(m + 1) * P],
                                                              x[:, kk, h * HALF:(h + 1) * HALF],
                                                              start=(kk == 0), stop=(kk == kt - 1))
                                        if kk == kt - 1:
                                            mm.then_inc(filled, 1)
                            if chunk < nchunk - 1:
                                mm.then_inc(self.read, 1)
                    if after is not None:
                        after[1](pe)

                @block.scalar
                def _(act):
                    if before is not None:
                        before[0](act)
                    if side is not None:
                        side[0](act)
                    act_evac(act)
                    if after is not None:
                        after[0](act)

                @block.vector
                def _(dve):
                    if before is not None:
                        before[2](dve)
                    if side is not None:
                        side[1](dve)
                    dve_evac(dve)
                    if after is not None:
                        after[2](dve)

                if after is not None:
                    @block.gpsimd
                    def _(pool):
                        if side is not None:
                            side[2](pool)
                        after[3](pool)


def evac_copy(dst):
    def make(c, name, filled, freed, per, iters, mine):
        nc, ps = c.nc, c.psum

        def program(eng, copy, h):
            with eng.Fori(0, iters) as it:
                for m in range(4 * per):
                    bank = (m % 4) * 2 + h
                    eng.wait_ge(filled, it * (8 * per) + 2 * m + h + 1)
                    copy(dst[:, bass.ds(it * (4 * per) + m, 1), h * HALF:(h + 1) * HALF],
                         ps[:, bank:bank + 1, 0:HALF]).then_inc(freed[h], 1)
        return (lambda act: program(act, nc.scalar.copy, 0)), (lambda dve: program(dve, nc.vector.tensor_copy, 1)), freed
    return make


def evac_sq_relu(dst):
    def make(c, name, filled, freed, per, iters, mine):
        nc, ps = c.nc, c.psum
        squared = c.sem(f"{name}_squared")
        tmp = c.buf(f"{name}_relu", [P, 4, HALF], ctx=mine)

        def act_prog(act):
            act.sem_inc(squared, 4)
            with act.Fori(0, iters) as it:
                for b in range(8 * per):
                    act.wait_ge(filled, it * (8 * per) + b + 1)
                    act.wait_ge(squared, it * (8 * per) + b + 1)
                    nc.scalar.activation(tmp[:, b % 4, :], ps[:, b % 8, 0:HALF], ACT.Relu).then_inc(freed[b % 2], 1)

        def dve_prog(dve):
            with dve.Fori(0, iters) as it:
                for b in range(8 * per):
                    m, h = b // 2, b % 2
                    dve.wait_ge(freed[h], it * (4 * per) + m + 5)
                    nc.vector.tensor_mul(dst[:, bass.ds(it * (4 * per) + m, 1), h * HALF:(h + 1) * HALF],
                                         tmp[:, b % 4:b % 4 + 1, :], tmp[:, b % 4:b % 4 + 1, :]).then_inc(squared, 1)
        return act_prog, dve_prog, [squared]
    return make


def stage_outputs(c):
    nc, ps = c.nc, c.psum
    turned, kept, out = c.sem("y_turned"), c.sem("y_kept"), c.sem("y_written")
    with ExitStack() as mine:
        yr = c.buf("y_rows", [P, QT + 1, D], ctx=mine)
        with nc.Block() as block:
            @block.tensor
            def _(pe):
                for i in range(2 * (QT + 1)):
                    t, kk = i // 2, i % 2
                    n = rows_of(t)
                    if i >= 4:
                        pe.wait_ge(kept, i - 3)
                    for k in range(4):
                        mm = nc.tensor.transpose(ps[0:n, i % 4, k * P:(k + 1) * P],
                                                 c.hT[:, kk * 4 + k, t * P:t * P + n], c.ident[:])
                    mm.then_inc(turned, 1)

            @block.vector
            def _(dve):
                for i in range(2 * (QT + 1)):
                    t, kk = i // 2, i % 2
                    n = rows_of(t)
                    dve.wait_ge(turned, i + 1)
                    nc.vector.tensor_copy(yr[0:n, t, kk * 512:kk * 512 + 512], ps[0:n, i % 4, :]).then_inc(kept, 1)

            @block.sync
            def _(sp):
                for t in range(QT + 1):
                    sp.wait_ge(kept, 2 * t + 2)
                    dst = c.dram["y_prompt"][0, t * P:(t + 1) * P, :] if t < QT else c.dram["y_sample"][:, 0, :]
                    sp.dma_start(dst, yr[0:rows_of(t), t, :]).then_inc(out, 16)
                sp.wait_ge(out, 16 * (QT + 1))


def columns(w):
    view = w.rearrange("(k p) n -> p k n", p=P)
    return lambda g, chunk: view[:, chunk * CK:(chunk + 1) * CK, bass.ts(g, NG)]


def stage_mix_out(c, lin, x, evac, y, layer, up, before=None):
    with ExitStack() as mine:
        sq, rs = c.buf(f"mix_sq{layer}", [P, 4, T], ctx=mine), c.buf(f"mix_rs{layer}", [P, T], ctx=mine)
        lin.run(x, evac, before=before, after=residual_parts(c, f"mix_out{layer}", y, layer, 1, sq, rs, lin.evacuated), then=up)


def stage_mlp(c, layer, up, side=None):
    with ExitStack() as mine:
        hid = c.buf(f"hidden{layer}", [P, KF, T], ctx=mine)
        sq, rs = c.buf(f"mlp_sq{layer}", [P, 4, T], ctx=mine), c.buf(f"mlp_rs{layer}", [P, T], ctx=mine)
        down = Linear(c, f"mlp_down{layer}", columns(c.dram["mlp_w2"][layer]), KF, D // NG, 1)
        up.run(c.xT, evac_sq_relu(hid), before=norm_parts(c, f"mlp_in{layer}", c.hT, c.xT, layer, 2, sq, rs), then=down)
        down.run(hid, evac_copy(c.xT), side=side and side(mine), after=residual_parts(c, f"mlp_out{layer}", c.xT, layer, 3, sq, rs, down.evacuated))


def mlp_up(c, layer):
    return Linear(c, f"mlp_up{layer}", columns(c.dram["mlp_w1"][layer]), KD, DFF // NG, 2)


def stage_project(c, norm):
    nc, ps = c.nc, c.psum
    w_in = c.dram["nsa_w_in"][0].rearrange("(k p) n -> p k n", p=P)
    nblk = 5
    landed = [c.sem(f"proj_w_landed{s}") for s in range(2)]
    gate_landed, table_landed = c.sem("proj_gate_w_landed"), c.sem("proj_table_landed")
    block_read, filled, freed = c.sem("proj_block_read"), c.sem("proj_bank_filled"), c.sem("proj_bank_freed")
    q_kept, swapped, swap_freed, roped = (c.sem(f"proj_{x}") for x in ("q_kept", "q_swapped", "swap_freed", "q_roped"))
    t1_sem, link, gated, written = c.sem("proj_t1"), c.sem("proj_link"), c.sem("proj_gate_exp"), c.sem("proj_written")
    with ExitStack() as mine:
        w = c.buf("proj_w", [P, 2, KD, NG], ctx=mine)
        wg = c.buf("proj_gate_w", [P, KD, 3 * NH], ctx=mine)
        tmp = c.buf("proj_tmp", [P, T], ctx=mine)
        swap = c.buf("swap", [P, P], ctx=mine)
        rope_t = c.buf("rope_t", [P, 2, T], ctx=mine)
        rope = c.qz[:, 1, 1].rearrange("p b x -> p (b x)")[:, 0:(QT + 1) * HD].rearrange("p (t i d) -> p t i d", i=2, d=HD // 2)
        nq, nrow = 2 * KD, 3 * (QT + 1)
        with nc.Block() as block:
            @block.sync
            def _(sp):
                for b, name in ((swap, "c_swap"), (rope_t, "c_ropeT"), (rope, "c_rope")):
                    sp.dma_start(b[:], c.dram[name]).then_inc(table_landed, 16)
                for j in range(nblk):
                    if j >= 2:
                        sp.wait_ge(block_read, j - 1)
                    sp.dma_start(w[:, j % 2], w_in[:, :, bass.ts(j, NG)]).then_inc(landed[j % 2], 16)
                sp.dma_start(wg[:], w_in[:, :, nblk * NG:]).then_inc(gate_landed, 16)
                compress_first_loads(c, sp)
                names = ("kv_cmp", "kv_sel", "kv_win")
                for b in range(3):
                    for t in range(QT + 1):
                        sp.wait_ge(roped, 8 + b * (QT + 1) + t + 1)
                        if t < QT:
                            dst = c.dram[f"{names[b]}_prompt"][0, 0, t * P:(t + 1) * P].rearrange("t s h d -> t (s h d)")
                        elif b < 2:
                            dst = c.dram[f"{names[b]}_sample"][0, :, 0].rearrange("t s h d -> t (s h d)")
                        else:
                            dst = c.dram["kv_win_sample"][0, :, WIN - 1].rearrange("t s h d -> t (s h d)")
                        sp.dma_start(dst, c.kv[0:rows_of(t), t, b, :]).then_inc(written, 16)
                sp.wait_ge(written, 16 * nrow)

            @block.tensor
            def _(pe):
                step = 0

                def start_bank(k):
                    if k == 0 and step >= 6:
                        pe.wait_ge(freed, step - 5)

                def swap_q(m):
                    pe.wait_ge(q_kept, 2 * (m + 1))
                    if m >= 1:
                        pe.wait_ge(swap_freed, m)
                    for h in range(2):
                        mm = nc.tensor.matmul(ps[:, 6 + h, 0:HALF], swap[:], c.qT[:, m, h * HALF:(h + 1) * HALF],
                                              start=True, stop=True)
                    mm.then_inc(swapped, 1)

                norm[1](pe)
                pe.wait_ge(norm[3], KD)
                pe.wait_ge(table_landed, 48)
                for j in range(2):
                    pe.wait_ge(landed[j], 16)
                    for m in range(4):
                        for h in range(2):
                            for k in range(KD):
                                start_bank(k)
                                mm = nc.tensor.matmul(ps[:, step % 6, 0:HALF], w[:, j, k, m * P:(m + 1) * P],
                                                      c.xT[:, k, h * HALF:(h + 1) * HALF],
                                                      start=(k == 0), stop=(k == KD - 1))
                            mm.then_inc(filled, 1)
                            step += 1
                        if j * 4 + m >= 1:
                            swap_q(j * 4 + m - 1)
                    pe.drain().then_inc(block_read, 1)
                swap_q(KD - 1)
                for b in range(3):
                    pe.wait_ge(landed[b % 2], 16 * (b // 2 + 2))
                    for t in range(QT + 1):
                        n = rows_of(t)
                        for k in range(KD):
                            start_bank(k)
                            mm = nc.tensor.matmul(ps[0:n, step % 6, :], c.xT[:, k, t * P:t * P + n], w[:, b % 2, k, :],
                                                  start=(k == 0), stop=(k == KD - 1))
                        mm.then_inc(filled, 1)
                        step += 1
                    pe.drain().then_inc(block_read, 1)
                pe.wait_ge(gate_landed, 16)
                for t in range(QT + 1):
                    n = rows_of(t)
                    for k in range(KD):
                        start_bank(k)
                        mm = nc.tensor.matmul(ps[0:n, step % 6, 0:3 * NH], c.xT[:, k, t * P:t * P + n], wg[:, k, :],
                                              start=(k == 0), stop=(k == KD - 1))
                    mm.then_inc(filled, 1)
                    step += 1

            @block.scalar
            def _(act):
                norm[0](act)
                step = 0
                for m in range(KD):
                    for h in range(2):
                        act.wait_ge(filled, step + 1)
                        nc.scalar.mul(c.qT[:, m, h * HALF:(h + 1) * HALF], ps[:, step % 6, 0:HALF], -SCALE)\
                            .then_inc(q_kept, 1)
                        act.wait_ge(q_kept, step + 1)
                        act.sem_inc(freed, 1)
                        step += 1
                for b in range(3):
                    for t in range(QT + 1):
                        n = rows_of(t)
                        act.wait_ge(filled, step + 1)
                        nc.scalar.copy(c.kv[0:n, t, b, :], ps[0:n, step % 6, :]).then_inc(freed, 1)
                        step += 1
                for t in range(QT + 1):
                    n = rows_of(t)
                    act.wait_ge(filled, step + 1)
                    nc.scalar.activation(c.gates[0:n, t, :], ps[0:n, step % 6, 0:3 * NH], ACT.Exp, scale=-1.0)\
                        .then_inc(freed, 1)
                    step += 1

            @block.vector
            def _(dve):
                links = 0

                def linked(ins):
                    nonlocal links
                    links += 1
                    ins.then_inc(link, 1)
                    dve.wait_ge(link, links)

                norm[2](dve)
                dve.wait_ge(table_landed, 48)
                for m in range(KD):
                    dve.wait_ge(swapped, m + 1)
                    if m >= 1:
                        dve.wait_ge(roped, m)
                    for h in range(2):
                        cols = slice(h * HALF, (h + 1) * HALF)
                        linked(nc.vector.tensor_mul(tmp[:, cols], ps[:, 6 + h, 0:HALF], rope_t[:, 1, cols]))
                    dve.sem_inc(swap_freed, 1)
                    linked(nc.vector.tensor_mul(c.qrT[:, m, :], c.qT[:, m, :], rope_t[:, 0, :]))
                    nc.vector.tensor_add(c.qrT[:, m, :], c.qrT[:, m, :], tmp[:]).then_inc(roped, 1)
                dve.wait_ge(roped, KD)
                for b in range(3):
                    for t in range(QT + 1):
                        n = rows_of(t)
                        dve.wait_ge(freed, nq + b * (QT + 1) + t + 1)
                        if b == 0:
                            dve.sem_inc(roped, 1)
                            continue
                        k = c.kv[0:n, t, b, 0:KVW].rearrange("p (h s d) -> p h s d", s=2, d=HD // 2)
                        tv = tmp[0:n, 0:KVW].rearrange("p (h s d) -> p h s d", s=2, d=HD // 2)

                        def table(i, heads):
                            return rope[0:n, t, i, :].unsqueeze(1).to_broadcast([n, heads, HD // 2])
                        linked(nc.vector.tensor_mul(tv[:, :, 0, :], k[:, :, 1, :], table(1, NKV)))
                        linked(nc.vector.tensor_mul(tv[:, :, 1, :], k[:, :, 0, :], table(1, NKV)))
                        for s in range(2):
                            linked(nc.vector.tensor_mul(k[:, :, s, :], k[:, :, s, :], table(0, NKV)))
                        linked(nc.vector.tensor_sub(k[:, :, 0, :], k[:, :, 0, :], tv[:, :, 0, :]))
                        nc.vector.tensor_add(k[:, :, 1, :], k[:, :, 1, :], tv[:, :, 1, :]).then_inc(roped, 1)
                        dve.wait_ge(roped, 8 + b * (QT + 1) + t + 1)
                for t in range(QT + 1):
                    n = rows_of(t)
                    dve.wait_ge(freed, nq + nrow + t + 1)
                    linked(nc.vector.tensor_scalar_add(c.gates[0:n, t, :], c.gates[0:n, t, :], 1.0))
                    linked(nc.vector.reciprocal(c.gates[0:n, t, :], c.gates[0:n, t, :]))


RQ = 4


def compress_buffers(c, ctx):
    c.cmp_raw = c.buf("cmp_raw", [P, RQ - 2, 4, ROW], ctx=ctx)
    c.cmp_w1 = c.buf("cmp_w1", [P, 2, STRIDE, 2, HD], ctx=ctx)
    c.cmp_w2 = c.buf("cmp_w2", [HD, 2, 2, HD], ctx=ctx)
    c.cmp_pe_rows = c.buf("cmp_pe_rows", [4 * STRIDE, HD], ctx=ctx)
    c.cmp_w_ready, c.cmp_landed = c.sem("cmp_w_ready"), [c.sem(f"cmp_landed{s}") for s in range(RQ)]


def quad_slot(c, g):
    s = g % RQ
    return c.cmp_raw[:, s] if s < 2 else c.xT[:, 4 * (s - 2):4 * (s - 2) + 4, 0:ROW]


def load_quad(c, sp, g):
    pages = c.dram["cache_kv_cmp"][0].rearrange("g t s h d -> g t (s h d)")
    for j in range(4):
        page = sp.value_load(c.pages[0:1, 4 * g + j:4 * g + j + 1], min_val=0, max_val=POOL_PAGES - 1)
        sp.dma_start(quad_slot(c, g)[:, j, :], pages[bass.ds(page, 1)].rearrange("g t x -> (g t) x"))\
            .then_inc(c.cmp_landed[g % RQ], 16)


def compress_first_loads(c, sp):
    for kv in range(2):
        w = c.dram["nsa_cmp_w1"][0, kv].rearrange("(r t d) e -> r d t e", r=2, d=HD)
        for r in range(2):
            for copy in range(2):
                sp.dma_start(c.cmp_w1[copy * HD:(copy + 1) * HD, kv, :, r], w[r]).then_inc(c.cmp_w_ready, 16)
        for d in range(2):
            sp.dma_start(c.cmp_w2[:, kv, d], c.dram["nsa_cmp_w2"][0, kv]).then_inc(c.cmp_w_ready, 16)
    sp.dma_start(c.cmp_pe_rows[:], c.dram["nsa_cmp_pe"][0].rearrange("v a d -> (v a) d")).then_inc(c.cmp_w_ready, 16)
    for g in range(2):
        load_quad(c, sp, g)


def stage_compress(c):
    nc, ps = c.nc, c.psum
    units, quads = NB // 2 + 1, 4
    steps = 2 * units
    w_ready, landed, pe_turned = c.cmp_w_ready, c.cmp_landed, c.sem("cmp_pe_turned")
    raw, w1, w2, pe_rows = c.cmp_raw, c.cmp_w1, c.cmp_w2, c.cmp_pe_rows
    turned, kept, summed = c.sem("cmp_turned"), [c.sem("cmp_kept_dve"), c.sem("cmp_kept_act")], c.sem("cmp_summed")
    quad_read = c.sem("cmp_quad_read")
    shifted, added, gelued = c.sem("cmp_shifted"), c.sem("cmp_added"), c.sem("cmp_gelued")
    out_filled, out_kept, bias_done, pe_kept = (c.sem(f"cmp_{x}") for x in ("out_filled", "out_kept", "bias_done", "pe_kept"))
    bias_kept = c.sem("cmp_bias_kept")
    queries_pool, new_keys_pe, new_keys_dve = sample_query_parts(c)
    with ExitStack() as mine:
        xt = c.buf("cmp_xt", [P, 2, STRIDE, 2 * P], ctx=mine)
        pe_cols = c.kcp[0:HD].rearrange("p h n -> p (h n)")[:, 0:4 * STRIDE]
        bias = c.buf("cmp_bias", [P, 2], ctx=mine)
        tmp = c.buf("cmp_tmp", [HD, 2, 512], ctx=mine)
        gel = c.buf("cmp_gelu", [HD, 2, 512], ctx=mine)

        def shape_of(i):
            return (quads, 2, NSUB, NCS) if i // 2 < units - 1 else (1, 1, NSUBP, NCP)

        turns = [(i, q, hp) for i in range(steps) for q in range(shape_of(i)[0]) for hp in range(2)]
        first = [min(n for n, x in enumerate(turns) if x[0] == i) for i in range(steps)] + [len(turns)]

        def wait_kept(eng, n):
            for e in range(2):
                if (n + 1 - e) // 2 > 0:
                    eng.wait_ge(kept[e], (n + 1 - e) // 2)

        def empty(eng, copy, n):
            i, q, hp = turns[n]
            if n == first[i] + n % 2 and i >= 2:
                eng.wait_ge(summed, i - 1)
            eng.wait_ge(turned, n + 1)
            w = 4 * PAGE // STRIDE
            at = hp * shape_of(i)[0] * w + q * w
            copy(xt[:, i % 2, :, at:at + w], ps[:, n % 3, :].rearrange("p (x t) -> p t x", t=STRIDE)).then_inc(kept[n % 2], 1)

        with nc.Block() as block:
            @block.gpsimd
            def _(pool):
                queries_pool(pool)

            @block.sync
            def _(sp):
                for g in range(2, NB * NPAGE // 4):
                    if g >= RQ:
                        sp.wait_ge(quad_read, g - RQ + 1)
                    load_quad(c, sp, g)

            @block.tensor
            def _(pe):
                new_keys_pe(pe)
                pe.wait_ge(w_ready, 16 * 13)
                nc.tensor.transpose(ps[0:HD, 7, 0:4 * STRIDE], pe_rows[:], c.ident[0:4 * STRIDE, 0:4 * STRIDE]).then_inc(pe_turned, 1)
                pe.wait_ge(pe_kept, 1)
                for kv in range(2):
                    for a in range(2 * STRIDE):
                        mm = nc.tensor.matmul(ps[0:HD, 7, 64 + kv:65 + kv], w1[0:HD, kv, a % STRIDE, a // STRIDE, :],
                                              pe_cols[:, kv * 2 * STRIDE + a:kv * 2 * STRIDE + a + 1],
                                              start=(a == 0), stop=(a == 2 * STRIDE - 1))
                    mm.then_inc(bias_done, 1)

                def tail(i):
                    kv = i % 2
                    nq, nb, per, nk = shape_of(i)
                    pe.wait_ge(gelued, i + 1)
                    if i >= 1:
                        pe.wait_ge(out_kept, i)
                    g = gel[:, i % 2, :]
                    if kv == 0:
                        cols = NKV * nb * nk
                        nc.tensor.matmul(ps[:, 7, 0:cols], w2[:, 0].rearrange("e a f -> e (a f)"), g[:, 0:cols],
                                         start=True, stop=True).then_inc(out_filled, 1)
                    else:
                        for b in range(nb):
                            for h in range(NKV):
                                at = (h * nb + b) * nk
                                mm = nc.tensor.matmul(ps[0:nk, 7, (b * NKV + h) * HD:(b * NKV + h + 1) * HD],
                                                      g[:, at:at + nk], w2[:, 1, 0, :], start=True, stop=True)
                        mm.then_inc(out_filled, 1)

                def turn(n):
                    i, q, hp = turns[n]
                    u, kv = divmod(i, 2)
                    g = u * quads + q
                    if u < units - 1 and kv == 0 and hp == 0:
                        pe.wait_ge(landed[g % RQ], 64 * (g // RQ + 1))
                    if n >= 3:
                        wait_kept(pe, n - 2)
                    cols = slice(kv * KVW + hp * P, kv * KVW + hp * P + P)
                    for j in range(4):
                        src = quad_slot(c, g)[:, j, cols] if u < units - 1 else c.kv[:, j, 0, cols]
                        mm = nc.tensor.transpose(ps[:, n % 3, j * P:(j + 1) * P], src, c.ident[:])
                    mm.then_inc(turned, 1)
                    if u < units - 1 and kv == 1 and hp == 1:
                        pe.wait_ge(turned, n + 1)
                        pe.sem_inc(quad_read, 1)

                def product(i, t):
                    nq, nb, per, nk = shape_of(i)
                    cols = 2 * nb * per
                    if t == 0:
                        wait_kept(pe, first[i + 1])
                        if i >= 2:
                            pe.wait_ge(added, i - 1)
                    for z in range(2):
                        mm = nc.tensor.matmul(ps[:, 3 + i % 2 * 2 + z, 0:cols], w1[z * HD:(z + 1) * HD, i % 2, t].rearrange("p r e -> p (r e)"),
                                              xt[z * HD:(z + 1) * HD, i % 2, t, 0:cols], start=(t == 0), stop=(t == STRIDE - 1))
                    if t == STRIDE - 1:
                        pe.drain().then_inc(summed, 1)

                for i in range(steps + 1):
                    done = 0
                    here = range(first[i], first[i + 1]) if i < steps else range(0)
                    for k, n in enumerate(here):
                        turn(n)
                        if i >= 1:
                            upto = STRIDE * (k + 1) // len(here)
                            for t in range(done, upto):
                                product(i - 1, t)
                            done = upto
                    if i >= 1:
                        for t in range(done, STRIDE):
                            product(i - 1, t)
                    if i >= 2:
                        tail(i - 2)
                tail(steps - 1)

            @block.scalar
            def _(act):
                def finish(i):
                    kv = i % 2
                    nq, nb, per, nk = shape_of(i)
                    cols = NKV * nb * nk
                    if i == 0:
                        act.wait_ge(bias_kept, 1)
                    act.wait_ge(summed, i + 1)
                    if i >= 2:
                        act.wait_ge(gelued, i - 1)
                    t = tmp[:, i % 2, 0:cols].rearrange("p (a z b n) -> p z a b n", z=2, a=2, b=nb)
                    for z in range(2):
                        bank = ps[HD:P, 3 + i % 2 * 2 + z, 0:2 * nb * per].rearrange("p (a b n) -> p a b n", a=2, b=nb)
                        for b in range(nb):
                            ins = nc.scalar.activation(t[:, z, :, b], bank[:, :, b, 1:1 + nk], ACT.Identity, bias=bias[HD:P, kv:kv + 1])
                    ins.then_inc(shifted, 1)
                    act.wait_ge(added, i + 1)
                    if i >= 2:
                        act.wait_ge(out_filled, i - 1)
                    nc.scalar.activation(gel[:, i % 2, 0:cols], tmp[:, i % 2, 0:cols], ACT.Gelu_apprx_tanh).then_inc(gelued, 1)

                for i in range(steps):
                    for n in range(first[i], first[i + 1]):
                        if n % 2 == 1:
                            empty(act, nc.scalar.copy, n)
                    if i >= 1:
                        finish(i - 1)
                finish(steps - 1)

            @block.vector
            def _(dve):
                new_keys_dve(dve)
                dve.wait_ge(pe_turned, 1)
                nc.vector.tensor_copy(pe_cols, ps[0:HD, 7, 0:4 * STRIDE]).then_inc(pe_kept, 1)
                dve.wait_ge(bias_done, 2)
                nc.vector.tensor_copy(bias[HD:P, :], ps[0:HD, 7, 64:66]).then_inc(bias_kept, 1)

                def copy_out(i):
                    u, kv = divmod(i, 2)
                    nq, nb, per, nk = shape_of(i)
                    dve.wait_ge(out_filled, i + 1)
                    bank = ps[:, 7, :]
                    if kv == 0:
                        v = bank[:, 0:NKV * nb * nk].rearrange("p (h b n) -> p h b n", h=NKV, b=nb)
                        if u == units - 1:
                            nc.vector.tensor_copy(c.kcp[:], v[:, :, 0, :]).then_inc(out_kept, 1)
                        else:
                            for half in range(2):
                                for a in range(2):
                                    ins = nc.vector.tensor_copy(c.kcs[half * HD:(half + 1) * HD, a, 2 * u:2 * u + 2, :],
                                                                v[half * HD:(half + 1) * HD, 2 * a + half])
                            ins.then_inc(out_kept, 1)
                    elif u == units - 1:
                        nc.vector.tensor_copy(c.vcp[0:nk, :], bank[0:nk, 0:KVW]).then_inc(out_kept, 1)
                    else:
                        nc.vector.tensor_copy(c.vcs[0:nk, 2 * u:2 * u + 2, :],
                                              bank[0:nk, :].rearrange("p (b x) -> p b x", b=2)).then_inc(out_kept, 1)

                def add(i):
                    nq, nb, per, nk = shape_of(i)
                    dve.wait_ge(shifted, i + 1)
                    t = tmp[:, i % 2, 0:NKV * nb * nk].rearrange("p (a z b n) -> p z a b n", z=2, a=2, b=nb)
                    for z in range(2):
                        bank = ps[0:HD, 3 + i % 2 * 2 + z, 0:2 * nb * per].rearrange("p (a b n) -> p a b n", a=2, b=nb)
                        for b in range(nb):
                            ins = nc.vector.tensor_add(t[:, z, :, b], bank[:, :, b, 0:nk], t[:, z, :, b])
                    ins.then_inc(added, 1)

                for i in range(steps):
                    for n in range(first[i], first[i + 1]):
                        if n % 2 == 0:
                            empty(dve, nc.vector.tensor_copy, n)
                    if i >= 1:
                        add(i - 1)
                    if i >= 2:
                        copy_out(i - 2)
                add(steps - 1)
                copy_out(steps - 2)
                copy_out(steps - 1)


def stage_prompt_attention(c):
    nc, ps = c.nc, c.psum
    turned, kept = c.sem("att_k_turned"), c.sem("att_k_kept")
    with ExitStack() as mine:
        kT = c.buf("att_kT", [P, 2, NKV, SEQ], ctx=mine)
        pcT = c.buf("att_pcT", [NCP, NH, SEQ], ctx=mine)
        with nc.Block() as block:
            @block.tensor
            def _(pe):
                for n in range(4):
                    kind, a = divmod(n, 2)
                    for t in range(QT):
                        mm = nc.tensor.transpose(ps[:, n, t * P:(t + 1) * P], c.kv[:, t, 1 + kind, a * P:(a + 1) * P], c.ident[:])
                    mm.then_inc(turned, 1)

            @block.vector
            def _(dve):
                for n in range(4):
                    kind, a = divmod(n, 2)
                    dve.wait_ge(turned, n + 1)
                    for to in range(2):
                        nc.vector.tensor_copy(kT[to * HD:(to + 1) * HD, kind, 2 * a, :], ps[0:HD, n, :]).then_inc(kept, 1)

            @block.scalar
            def _(act):
                for n in range(4):
                    kind, a = divmod(n, 2)
                    act.wait_ge(kept, 2 * (n + 1))
                    for to in range(2):
                        nc.scalar.copy(kT[to * HD:(to + 1) * HD, kind, 2 * a + 1, :], ps[HD:P, n, :])

        scored, masked, least_d, subbed, exped, scaled = (c.sem(f"attc_{x}") for x in ("scored", "masked", "least", "sub", "exp", "scaled"))
        turned_p, kept_p, summed, rec, gated, pmasked = (c.sem(f"attc_{x}") for x in ("turned", "kept", "summed", "rec", "gated", "pmasked"))
        with ExitStack() as here:
            kcz = c.buf("attc_kcz", [P, NKV, 2, NCP], ctx=here)
            spread = c.sem("attc_spread")
            sc = c.buf("attc_s", [P, 2, GRP, QT, NCP], ctx=here)
            low = c.buf("attc_low", [P, 2, GRP * QT], ctx=here)
            tot = c.buf("attc_tot", [P, 2, GRP * QT], ctx=here)
            cm = c.cmask[:].rearrange("p (w g t k) -> p w (g t) k", w=2, g=GRP, t=QT)

            def wide(x):
                return x.unsqueeze(2).to_broadcast([P, GRP * QT, NCP])

            with nc.Block() as block:
                @block.tensor
                def _(pe):
                    def turn(h):
                        pe.wait_ge(scaled, h + 1)
                        for g in range(GRP):
                            n = h * GRP + g
                            if n >= 3:
                                pe.wait_ge(kept_p, n - 2)
                            for t in range(QT):
                                mm = nc.tensor.transpose(ps[0:NCP, 4 + n % 3, t * P:(t + 1) * P], sc[:, h % 2, g, t, :], c.ident[:])
                            mm.then_inc(turned_p, 1)
                    pe.wait_ge(spread, 3)
                    for h in range(NKV):
                        for j in range(GRP // 2):
                            for t in range(QT):
                                at = (j * QT + t) * 2 * NCP
                                mm = nc.tensor.matmul(ps[:, h, at:at + 2 * NCP], c.qT[:, h * GRP // 2 + j, t * P:(t + 1) * P],
                                                      kcz[:, h].rearrange("p w k -> p (w k)"), start=True, stop=True)
                        mm.then_inc(scored, 1)
                    for h in range(NKV):
                        turn(h)

                @block.vector
                def _(dve):
                    def finish(h):
                        s = sc[:, h % 2].rearrange("p g t k -> p (g t) k")
                        dve.wait_ge(exped, h + 1)
                        nc.vector.tensor_mul(s, s, cm[:, 1]).then_inc(pmasked, 1)
                        dve.wait_ge(pmasked, h + 1)
                        nc.vector.tensor_reduce(tot[:, h % 2, :], s, AX.X, ALU.add).then_inc(summed, 1)
                        dve.wait_ge(summed, h + 1)
                        nc.vector.tensor_scalar_max(tot[:, h % 2, :], tot[:, h % 2, :], 1e-20).then_inc(rec, 1)
                        dve.wait_ge(rec, 3 * h + 1)
                        nc.vector.reciprocal(tot[:, h % 2, :], tot[:, h % 2, :]).then_inc(rec, 1)
                        dve.wait_ge(rec, 3 * h + 2)
                        gate = c.gates[:, 0:QT, :].rearrange("p t (h w) -> p h t w", w=3)[:, h * GRP:(h + 1) * GRP, :, 0]
                        nc.vector.tensor_mul(tot[:, h % 2, :].rearrange("p (g t) -> p g t", g=GRP),
                                             tot[:, h % 2, :].rearrange("p (g t) -> p g t", g=GRP), gate).then_inc(rec, 1)
                        dve.wait_ge(rec, 3 * h + 3)
                        nc.vector.tensor_mul(s, s, wide(tot[:, h % 2, :])).then_inc(scaled, 1)

                    nc.vector.memset(kcz[:], 0.0).then_inc(spread, 1)
                    dve.wait_ge(spread, 1)
                    for w in range(2):
                        rows = slice(w * HD, (w + 1) * HD)
                        nc.vector.tensor_copy(kcz[rows, :, w, :], c.kcp[rows]).then_inc(spread, 1)
                    for h in range(NKV):
                        s = sc[:, h % 2].rearrange("p g t k -> p (g t) k")
                        dve.wait_ge(scored, h + 1)
                        if h >= 2:
                            dve.wait_ge(turned_p, GRP * (h - 1))
                        for par in range(2):
                            ins = nc.vector.tensor_add(
                                sc[:, h % 2, par::2],
                                ps[:, h, 0:GRP * QT * NCP].rearrange("p (j t w k) -> p w j t k", j=2, t=QT, w=2)[:, par],
                                c.cmask[:].rearrange("p (w g t k) -> p w g t k", w=2, g=GRP, t=QT)[:, 0, par::2])
                        ins.then_inc(masked, 1)
                        dve.wait_ge(masked, h + 1)
                        nc.vector.tensor_reduce(low[:, h % 2, :], s, AX.X, ALU.min).then_inc(least_d, 1)
                        dve.wait_ge(least_d, h + 1)
                        nc.vector.tensor_sub(s, s, wide(low[:, h % 2, :])).then_inc(subbed, 1)
                        if h >= 1:
                            finish(h - 1)
                    finish(NKV - 1)

                @block.scalar
                def _(act):
                    n = 0
                    for h in range(NKV + 1):
                        if h < NKV:
                            act.wait_ge(subbed, h + 1)
                            s = sc[:, h % 2].rearrange("p g t k -> p (g t k)")
                            nc.scalar.activation(s, s, ACT.Exp, scale=-1.0).then_inc(exped, 1)
                        if h >= 1:
                            for g in range(GRP):
                                act.wait_ge(turned_p, n + 1)
                                nc.scalar.copy(pcT[:, n, :], ps[0:NCP, 4 + n % 3, :]).then_inc(kept_p, 1)
                                n += 1

        scored, lowered, exped, recip, scaled, turned_u, kept_u, unit_mul = (
            c.sem(f"att_{x}") for x in ("scored", "lowered", "exped", "recip", "scaled", "turned", "kept", "read"))
        o_filled, o_kept = c.sem("att_o_filled"), c.sem("att_o_kept")
        NU = NH * 2 * QT
        LAG, LAG_PV = 3, 5
        with ExitStack() as here:
            pr = c.buf("att_p", [P, 4, SEQ], ctx=here)
            pT = c.buf("att_pT", [P, 2, QT, SEQ], ctx=here)
            low = c.buf("att_low", [P, 4], ctx=here)
            tot = c.buf("att_tot", [P, 4], ctx=here)

            def unit(n):
                return n // (2 * QT), (n // QT) % 2, n % QT

            with nc.Block() as block:
                @block.tensor
                def _(pe):
                    def scores(n):
                        head, kind, i = unit(n)
                        rows = slice(head % 2 * HD, head % 2 * HD + HD)
                        if n >= 3:
                            pe.wait_ge(lowered, n - 2)
                        nc.tensor.matmul(ps[:, n % 3, 0:(i + 1) * P], c.qrT[rows, head // 2, i * P:(i + 1) * P],
                                         kT[rows, kind, head // GRP, 0:(i + 1) * P], start=True, stop=True).then_inc(scored, 1)

                    def turn(n):
                        head, kind, i = unit(n)
                        pe.wait_ge(scaled, n + 1)
                        if n >= 3:
                            pe.wait_ge(kept_u, n - 2)
                        for j in range(i + 1):
                            mm = nc.tensor.transpose(ps[:, 3 + n % 3, j * P:(j + 1) * P], pr[:, n % 4, j * P:(j + 1) * P], c.ident[:])
                        mm.then_inc(turned_u, 1)

                    def values(n):
                        head, kind, i = unit(n)
                        hp, par = head // 2, head % 2
                        out = ps[par * HD:(par + 1) * HD, 6 + hp % 2, :]
                        if kind == 0:
                            if hp >= 2 and par == 0:
                                pe.wait_ge(o_kept, hp - 1)
                            nc.tensor.matmul(out, c.vcp[0:NCP, head // GRP * HD:(head // GRP + 1) * HD], pcT[:, head, :],
                                             start=True, stop=False)
                        pe.wait_ge(kept_u, n + 1)
                        for j in range(QT):
                            mm = nc.tensor.matmul(out[:, j * P:SEQ],
                                                  c.kv[:, j, 1 + kind, KVW + head // GRP * HD:KVW + (head // GRP + 1) * HD],
                                                  pT[:, kind, j, j * P:SEQ], start=False, stop=(kind == 1 and j == QT - 1))
                        mm.then_inc(o_filled, 1)

                    for n in range(NU + LAG_PV):
                        if n < NU:
                            scores(n)
                        if LAG <= n < NU + LAG:
                            turn(n - LAG)
                        if n >= LAG_PV and (n - LAG_PV) % QT == QT - 1:
                            values(n - LAG_PV)

                @block.vector
                def _(dve):
                    for n in range(NU + 1):
                        if n < NU:
                            head, kind, i = unit(n)
                            w = (i + 1) * P
                            dve.wait_ge(scored, n + 1)
                            if n >= 4:
                                dve.wait_ge(turned_u, n - 3)
                            nc.vector.tensor_tensor_reduce(pr[:, n % 4, 0:w], ps[:, n % 3, 0:w], c.causal[:, SEQ - w:SEQ], 1.0,
                                                           3e38, ALU.add, ALU.min, low[:, n % 4:n % 4 + 1]).then_inc(lowered, 1)
                        if n >= 1:
                            m = n - 1
                            head, kind, i = unit(m)
                            w = (i + 1) * P
                            dve.wait_ge(exped, m + 1)
                            nc.vector.reciprocal(tot[:, m % 4:m % 4 + 1], tot[:, m % 4:m % 4 + 1]).then_inc(recip, 1)
                            dve.wait_ge(recip, m + 1)
                            gate = c.gates[:, i, head * 3 + 1 + kind:head * 3 + 2 + kind]
                            nc.vector.tensor_scalar(pr[:, m % 4, 0:w], pr[:, m % 4, 0:w], tot[:, m % 4:m % 4 + 1], gate,
                                                    ALU.mult, ALU.mult).then_inc(scaled, 1)

                @block.scalar
                def _(act):
                    def keep(n):
                        head, kind, i = unit(n)
                        act.wait_ge(turned_u, n + 1)
                        hk = n // QT
                        if hk >= 2:
                            act.wait_ge(o_filled, hk - 1)
                        nc.scalar.copy(pT[:, kind, 0:i + 1, i * P:(i + 1) * P],
                                       ps[:, 3 + n % 3, 0:(i + 1) * P].rearrange("p (j q) -> p j q", q=P)).then_inc(kept_u, 1)

                    def keep_o(hp):
                        act.wait_ge(o_filled, 4 * (hp + 1))
                        nc.scalar.copy(c.oT[:, hp, 0:SEQ], ps[:, 6 + hp % 2, :]).then_inc(o_kept, 1)

                    for n in range(NU + LAG + 3):
                        if n < NU:
                            head, kind, i = unit(n)
                            w = (i + 1) * P
                            act.wait_ge(lowered, n + 1)
                            nc.scalar.activation(pr[:, n % 4, 0:w], pr[:, n % 4, 0:w], ACT.Exp, scale=-1.0,
                                                 bias=low[:, n % 4:n % 4 + 1], accum_out=tot[:, n % 4:n % 4 + 1]).then_inc(exped, 1)
                        if LAG <= n < NU + LAG:
                            keep(n - LAG)
                        if n >= LAG_PV and (n - LAG_PV) % (4 * QT) == 4 * QT - 1:
                            keep_o((n - LAG_PV) // (4 * QT))


NKC = PAST // P
NWC = WIN // P
NC_S = NKC + NWC


def sample_query_parts(c):
    nc, ps = c.nc, c.psum
    cleared, put, gates_out, k_turned = c.sem("sq_cleared"), c.sem("sq_put"), c.sem("sq_gates"), c.sem("sq_k_turned")
    k_kept = c.sem("sq_k_kept")

    def pool_part(pool):
        for b in range(NB):
            pool.dma_start(c.gates_s[b * NH:(b + 1) * NH, :],
                           c.gates[b:b + 1, QT, :].rearrange("o (h w) -> o h w", w=3)).then_inc(gates_out, 16)
        nc.gpsimd.memset(c.qz[:], 0.0).then_inc(cleared, 1)
        pool.wait_ge(cleared, 1)
        for which, src in enumerate((c.qT, c.qrT)):
            flat = c.qz[:, which].rearrange("p a b x -> p a (b x)")
            for t in range(KD):
                a, kv2 = t // 4, t // 2 % 2
                for par in range(2):
                    h = 2 * t + par
                    base = flat[kv2 * HD:(kv2 + 1) * HD, a, :]
                    dst = bass.AP(base.tensor, base.offset + h, [list(base.ap[0]), [P + NH, NB]])
                    nc.gpsimd.tensor_copy(dst, src[par * HD:(par + 1) * HD, t, SEQ:T]).then_inc(put, 1)
        pool.wait_ge(gates_out, 16 * NB)

    def pe_part(pe):
        for which in range(2):
            for a in range(2):
                mm = nc.tensor.transpose(ps[:, 6, (which * 2 + a) * NB:(which * 2 + a + 1) * NB],
                                         c.kv[0:NB, QT, 1 + which, a * P:(a + 1) * P], c.ident[0:NB, 0:NB])
        mm.then_inc(k_turned, 1)

    def dve_part(dve):
        dve.wait_ge(k_turned, 1)
        nc.vector.tensor_copy(c.knT[:], ps[:, 6, 0:4 * NB].rearrange("p (w a b) -> p w a b", w=2, a=2)).then_inc(k_kept, 1)
    return pool_part, pe_part, dve_part


def stage_sample_attention(c):
    nc, ps = c.nc, c.psum
    sel_pages = c.dram["cache_kv_sel"][0].rearrange("g t s h d -> g t (s h d)")
    win = c.dram["cache_kv_win"][0].rearrange("b (c t) s h d -> b t c (s h d)", t=P)
    win_out = c.dram["kv_win_sample"][0].rearrange("b t s h d -> b t (s h d)")
    RS = 7
    landed = [[c.sem(f"sa_{kv}_landed{s}") for s in range(RS)] for kv in "kv"]
    written = [c.sem(f"sa_written{s}") for s in range(RS)]
    v_read = c.sem("sa_v_read")
    turned, kept, scored, s_done = c.sem("sa_turned"), c.sem("sa_kept"), c.sem("sa_scored"), c.sem("sa_scores_done")
    link, exped, a_ready = c.sem("sa_link"), c.sem("sa_exp"), c.sem("sa_exp_ready")
    imp_in, imp_out, p_turn, p_kept, o_done, o_kept, o_rows = (
        c.sem(f"sa_{x}") for x in ("imp_in", "imp_out", "p_turned", "p_kept", "o_done", "o_kept", "o_rows"))
    with ExitStack() as mine:
        raw = c.buf("sa_raw", [P, RS, NC_S, KVW], ctx=mine)

        def wait_landed(eng, n):
            kv, b = divmod(n, NB)
            eng.wait_ge(landed[kv][n % RS], 16 * (NPAGE + 1) * (b // RS + 1))

        kT = c.buf("sa_kT", [P, 4, 512], ctx=mine)
        s_sel = c.buf("sa_s_sel", [P, PAST + NB], ctx=mine)
        s_win = c.buf("sa_s_win", [P, WIN + NB], ctx=mine)
        s_cmp = c.buf("sa_s_cmp", [P, NCS], ctx=mine)
        low = c.buf("sa_low", [P, 3], ctx=mine)
        tot = c.buf("sa_tot", [P, 3], ctx=mine)
        drop = c.buf("sa_drop", [P, 4, NSEL], ctx=mine)
        one = c.buf("sa_one", [P, 4], ctx=mine)
        pc = c.buf("sa_pcT", [P, 2, P], ctx=mine)
        pT = kT[:, 0:3, :].rearrange("p q (j x) -> p (q j) x", x=P)
        pn = c.buf("sa_pnT", [NB, 2, P], ctx=mine)
        o_r = c.buf("sa_o_rows", [P, 2, KVW], ctx=mine)
        ngroup = NB * 3 * 2
        def load(eng, n):
            kv, b = divmod(n, NB)
            s, cols = n % RS, slice(kv * KVW, (kv + 1) * KVW)
            if n >= RS:
                m = n - RS
                if m < NB:
                    eng.wait_ge(turned, 6 * (m + 1))
                else:
                    eng.wait_ge(v_read, m - NB + 1)
                eng.wait_ge(written[s], 32 * (n // RS))
            for j in range(NPAGE):
                at = b * NPAGE + j
                page = eng.value_load(c.pages[0:1, at:at + 1], min_val=0, max_val=POOL_PAGES - 1)
                rows = sel_pages[bass.ds(page, 1), :, :].rearrange("g t x -> (g t) x")
                eng.dma_start(raw[:, s, j, :], rows[:, cols]).then_inc(landed[kv][s], 16)
            eng.dma_start(raw[:, s, NKC:, :], win[b, :, :, cols]).then_inc(landed[kv][s], 16)

        def shift(eng, n):
            kv, b = divmod(n, NB)
            s, cols = n % RS, slice(kv * KVW, (kv + 1) * KVW)
            wait_landed(eng, n)
            eng.dma_start(win_out[b, 0:P - 1, cols], raw[1:P, s, NKC, :]).then_inc(written[s], 16)
            eng.dma_start(win_out[b, P - 1:WIN - 1, cols].rearrange("(c t) x -> t c x", t=P), raw[:, s, NKC + 1:, :]).then_inc(written[s], 16)

        with nc.Block() as block:
            @block.sync
            def _(sp):
                for n in range(NB):
                    load(sp, n)
                    if n >= 2:
                        shift(sp, n - 2)
                for n in range(NB - 2, 2 * NB):
                    shift(sp, n)
                for s in range(RS):
                    sp.wait_ge(written[s], 32 * len(range(s, 2 * NB, RS)))

            @block.gpsimd
            def _(pool):
                for n in range(NB, 2 * NB):
                    load(pool, n)

            @block.tensor
            def _(pe):
                for a in range(2):
                    for b in range(NB):
                        nc.tensor.matmul(ps[:, 6, 0:NCS], c.qz[:, 0, a, b, :], c.kcs[:, a, b, :],
                                         start=(a == 0 and b == 0), stop=(a == 1 and b == NB - 1))
                for w in range(2):
                    for a in range(2):
                        for b in range(NB):
                            mm = nc.tensor.matmul(ps[:, 7, w * NB:(w + 1) * NB], c.qz[:, 1, a, b, :], c.knT[:, w, a, :],
                                                  start=(a == 0 and b == 0), stop=(a == 1 and b == NB - 1))
                mm.then_inc(s_done, 1)

                def product(n):
                    b, r = divmod(n, 6)
                    part, a = divmod(r, 2)
                    pe.wait_ge(kept, n + 1)
                    nc.tensor.matmul(ps[:, part, :], c.qz[:, 1, a, b, :], kT[:, n % 4, :],
                                     start=(b == 0 and a == 0), stop=(b == NB - 1 and a == 1)).then_inc(scored, 1)

                for n in range(ngroup + 2):
                    if n < ngroup:
                        b, r = divmod(n, 6)
                        part, a = divmod(r, 2)
                        if r == 0:
                            wait_landed(pe, b)
                        if n >= 3:
                            pe.wait_ge(kept, n - 2)
                        for j in range(4):
                            mm = nc.tensor.transpose(ps[:, 3 + n % 3, j * P:(j + 1) * P],
                                                     raw[:, b % RS, part * 4 + j, a * P:(a + 1) * P], c.ident[:])
                        mm.then_inc(turned, 1)
                    if n >= 2:
                        product(n - 2)
                pe.wait_ge(imp_in, 1)
                nc.tensor.transpose(ps[0:NCS, 3, 0:P], s_cmp[:], c.ident[:]).then_inc(imp_out, 1)
                pe.wait_ge(imp_in, 2)
                nc.tensor.matmul(ps[:, 3, P:P + NSEL], pc[0:NCS, 0, :], c.over[0:NCS, :], start=True, stop=True).then_inc(imp_out, 1)
                pe.wait_ge(imp_in, 3)
                nc.tensor.matmul(ps[:, 4, 0:NSEL], c.group[:], drop[:, 0, :], start=True, stop=True).then_inc(imp_out, 1)
                pe.wait_ge(a_ready, 4)
                nc.tensor.transpose(ps[0:NCS, 5, 0:P], s_cmp[:], c.ident[:]).then_inc(p_turn, 1)
                pe.wait_ge(a_ready, 6)
                for q in range(3):
                    if q == 1:
                        pe.wait_ge(p_kept, 1)
                    for j in range(4):
                        src = s_sel[:, (q * 4 + j) * P:(q * 4 + j + 1) * P] if q < 2 else s_win[:, j * P:(j + 1) * P]
                        mm = nc.tensor.transpose(ps[:, (3, 4, 2)[q], j * P:(j + 1) * P], src, c.ident[:])
                    mm.then_inc(p_turn, 1)
                for w in range(2):
                    src = s_win[:, WIN:] if w else s_sel[:, PAST:]
                    mm = nc.tensor.transpose(ps[0:NB, 6, w * P:(w + 1) * P], src, c.ident[:])
                mm.then_inc(p_turn, 1)
                pe.wait_ge(p_kept, 5)
                for bg in range(2):
                    for q in range(4):
                        wait_landed(pe, NB + bg * 4 + q)
                    for j in range(NC_S + 3):
                        for q in range(4):
                            b = bg * 4 + q
                            out, heads = ps[32 * q:32 * q + NH, bg, 0:KVW], slice(b * NH, (b + 1) * NH)
                            if j == 0:
                                lhs, rhs = pc[0:NCS, 1, heads], c.vcs[0:NCS, b, :]
                            elif j < 3:
                                lhs, rhs = pn[:, j - 1, heads], c.kv[0:NB, QT, j, KVW:]
                            else:
                                lhs, rhs = pT[:, j - 3, heads], raw[:, (NB + b) % RS, j - 3, :]
                            mm = nc.tensor.matmul(out, lhs, rhs, start=(j == 0), stop=(j == NC_S + 2), tile_position=(0, 32 * q))
                            if j == NC_S + 2:
                                mm.then_inc(v_read, 1)
                pe.wait_ge(o_rows, 9)
                for bg in range(2):
                    for a in range(2):
                        mm = nc.tensor.transpose(ps[:, 3, (bg * 2 + a) * P:(bg * 2 + a + 1) * P], o_r[:, bg, a * P:(a + 1) * P], c.ident[:])
                mm.then_inc(o_done, 1)

            @block.scalar
            def _(act):
                for n in range(0, ngroup, 2):
                    act.wait_ge(turned, n + 1)
                    if n >= 4:
                        act.wait_ge(scored, n - 3)
                    nc.scalar.copy(kT[:, n % 4, :], ps[:, 3 + n % 3, :]).then_inc(kept, 1)
                    if n + 1 < ngroup:
                        act.wait_ge(turned, n + 2)
                        if n + 1 >= 4:
                            act.wait_ge(scored, n - 2)
                        nc.scalar.copy(kT[:, (n + 1) % 4, :], ps[:, 3 + (n + 1) % 3, :]).then_inc(kept, 1)
                for w, s in enumerate((s_cmp, s_win, s_sel)):
                    act.wait_ge(a_ready, w + 1)
                    nc.scalar.activation(s[:], s[:], ACT.Exp, scale=-1.0, bias=low[:, w:w + 1],
                                         accum_out=tot[:, w:w + 1]).then_inc(exped, 1)

            @block.vector
            def _(dve):
                links = 0

                def linked(ins):
                    nonlocal links
                    links += 1
                    ins.then_inc(link, 1)
                    dve.wait_ge(link, links)

                def weigh(w, s, signal=None):
                    gate = c.gates_s[:, (0, 2, 1)[w]:(0, 2, 1)[w] + 1]
                    return nc.vector.tensor_scalar(s[:], s[:], tot[:, w:w + 1], gate, ALU.mult, ALU.mult)

                dve.wait_ge(s_done, 1)
                linked(nc.vector.tensor_copy(s_cmp[:], ps[:, 6, 0:NCS]))
                linked(nc.vector.tensor_copy(one[:, 0:1], ps[:, 7, 0:1]))
                linked(nc.vector.tensor_add(s_sel[:, PAST:], ps[:, 7, 0:NB], c.own[:]))
                linked(nc.vector.tensor_add(s_win[:, WIN:], ps[:, 7, NB:2 * NB], c.own[:]))
                nc.vector.tensor_reduce(low[:, 0:1], s_cmp[:], AX.X, ALU.min).then_inc(a_ready, 1)
                dve.wait_ge(exped, 1)
                linked(nc.vector.reciprocal(tot[:, 0:1], tot[:, 0:1]))
                nc.vector.tensor_scalar(s_cmp[:], s_cmp[:], tot[:, 0:1], None, ALU.mult).then_inc(imp_in, 1)
                dve.wait_ge(scored, ngroup)
                linked(nc.vector.tensor_copy(s_win[:, 0:WIN], ps[:, 2, :]))
                nc.vector.tensor_reduce(low[:, 1:2], s_win[:], AX.X, ALU.min).then_inc(a_ready, 1)
                dve.wait_ge(imp_out, 1)
                nc.vector.tensor_copy(pc[0:NCS, 0, :], ps[0:NCS, 3, 0:P]).then_inc(imp_in, 1)
                dve.wait_ge(imp_out, 2)
                nc.vector.tensor_copy(drop[:, 0, :], ps[:, 3, P:P + NSEL]).then_inc(imp_in, 1)
                dve.wait_ge(imp_out, 3)
                imp, eq, at = drop[:, 1, :], drop[:, 2, :], drop[:, 3, :]
                linked(nc.vector.tensor_copy(imp, ps[:, 4, 0:NSEL]))
                linked(nc.vector.tensor_reduce(one[:, 1:2], imp[:, 1:NSEL - 2], AX.X, ALU.min))
                linked(nc.vector.tensor_scalar(eq[:, 1:NSEL - 2], imp[:, 1:NSEL - 2], one[:, 1:2], None, ALU.is_equal))
                linked(nc.vector.tensor_mul(at[:, 1:NSEL - 2], eq[:, 1:NSEL - 2], c.blk[:, 1:NSEL - 2]))
                linked(nc.vector.tensor_reduce(one[:, 2:3], at[:, 1:NSEL - 2], AX.X, ALU.max))
                linked(nc.vector.tensor_scalar(eq, c.blk[:], one[:, 2:3], BIG, ALU.is_equal, ALU.mult))
                for half in range(2):
                    linked(nc.vector.tensor_add(s_sel[:, half * 512:(half + 1) * 512].rearrange("p (n x) -> p n x", x=SELB),
                                                ps[:, half, :].rearrange("p (n x) -> p n x", x=SELB),
                                                eq[:, half * 8:half * 8 + 8].unsqueeze(2).to_broadcast([P, 8, SELB])))
                nc.vector.tensor_reduce(low[:, 2:3], s_sel[:], AX.X, ALU.min).then_inc(a_ready, 1)
                nc.vector.tensor_scalar(s_cmp[:], s_cmp[:], c.gates_s[:, 0:1], None, ALU.mult).then_inc(a_ready, 1)
                for w, s in ((1, s_win), (2, s_sel)):
                    dve.wait_ge(exped, w + 1)
                    linked(nc.vector.reciprocal(tot[:, w:w + 1], tot[:, w:w + 1]))
                    weigh(w, s).then_inc(a_ready, 1)
                dve.wait_ge(p_turn, 1)
                nc.vector.tensor_copy(pc[0:NCS, 1, :], ps[0:NCS, 5, 0:P]).then_inc(p_kept, 1)
                for q in range(3):
                    dve.wait_ge(p_turn, 2 + q)
                    nc.vector.tensor_copy(pT[:, q * 4:q * 4 + 4, :],
                                          ps[:, (3, 4, 2)[q], :].rearrange("p (j x) -> p j x", x=P)).then_inc(p_kept, 1)
                dve.wait_ge(p_turn, 5)
                nc.vector.tensor_copy(pn[:], ps[0:NB, 6, 0:2 * P].rearrange("p (w x) -> p w x", w=2)).then_inc(p_kept, 1)
                nc.vector.memset(o_r[:], 0.0).then_inc(o_rows, 1)
                dve.wait_ge(o_rows, 1)
                for b in range(NB):
                    dve.wait_ge(v_read, 4 * (b // 4 + 1))
                    rows = slice(32 * (b % 4), 32 * (b % 4) + NH)
                    nc.vector.tensor_copy(o_r[rows, b // 4, :], ps[rows, b // 4, 0:KVW]).then_inc(o_rows, 1)
                dve.wait_ge(o_done, 1)
                for kv2 in range(2):
                    for par in range(2):
                        for a in range(2):
                            for bg in range(2):
                                src = ps[kv2 * HD:(kv2 + 1) * HD, 3, (bg * 2 + a) * P:(bg * 2 + a + 1) * P]\
                                    .rearrange("p (q a v j r) -> p a v r j q", a=4, v=2, j=2, r=2)
                                nc.vector.tensor_copy(c.oT[par * HD:(par + 1) * HD, a * 4 + kv2 * 2:a * 4 + kv2 * 2 + 2, SEQ + bg * 4:SEQ + bg * 4 + 4],
                                                      src[:, a, kv2, par]).then_inc(o_kept, 1)


def stage_nsa(c):
    with ExitStack() as outer:
        c.kcs = c.buf("kcs", [P, 2, NB, NCS], ctx=outer)
        c.vcs = c.buf("vcs", [NCS, NB, KVW], ctx=outer)
        c.kcp = c.buf("kcp", [P, NKV, NCP], ctx=outer)
        c.vcp = c.buf("vcp", [NCP, KVW], ctx=outer)
        c.kv = c.buf("kv", [P, QT + 1, 3, ROW], ctx=outer)
        c.gates = c.buf("gates", [P, QT + 1, 3 * NH], ctx=outer)
        c.gates_s = c.buf("gates_s", [P, 3], ctx=outer)
        c.qz = c.buf("qz", [P, 2, 2, NB, P], ctx=outer)
        c.knT = c.buf("knT", [P, 2, 2, NB], ctx=outer)
        c.oT = c.xT
        with ExitStack() as queries:
            c.qT = c.buf("qT", [P, KD, T], ctx=queries)
            c.qrT = c.buf("qrT", [P, KD, T], ctx=queries)
            compress_ctx = queries.enter_context(ExitStack())
            compress_buffers(c, compress_ctx)
            stage_project(c, norm_parts(c, "nsa_in", c.hT, c.xT, 0, 0, c.qrT[:, 0:4], c.qrT[:, 4]))
            stage_compress(c)
            compress_ctx.close()
            stage_prompt_attention(c)
        stage_sample_attention(c)


MAGIC = 1.5 * 2.0 ** 23
TWO_PI = 2.0 * np.pi
COLS = NCH + 2 * NB
HCOLS = NCH + NB
DVE_GROUPS = 40
C_BANKS = (2, 3, 4, 7)
DVE_PAIRS = 23
A_COLS = G + GP


def split(x, parts):
    out = []
    for _ in range(parts - 1):
        m, e = np.frexp(x)
        hi = float(np.ldexp(np.round(m * 2 ** 10), e - 10))
        out.append(hi)
        x -= hi
    return [*out, float(np.float32(x))]


class Chain:

    def __init__(self, c, eng, name):
        self.eng, self.sem, self.n = eng, c.sem(name), 0

    def __call__(self, ins):
        self.n += 1
        ins.then_inc(self.sem, 1)
        self.eng.wait_ge(self.sem, self.n)


def complex_axpy(eng, link, out, x, table, t, u):
    n, w = x.shape[2], x.shape[3]

    def wide(i):
        return table[:, i].unsqueeze(2).to_broadcast([P, n, w])
    link(eng.tensor_mul(t, x, table[:, 0].unsqueeze(1).unsqueeze(3).to_broadcast([P, 2, n, w])))
    link(eng.tensor_mul(u[:, 0], x[:, 1], wide(2)))
    link(eng.tensor_mul(u[:, 1], x[:, 0], wide(1)))
    link(eng.tensor_add(t, t, u))
    link(eng.tensor_add(out, out, t))


def ssm_side(c, keep):
    nc, dram = c.nc, c.dram
    c.scratch_v = nc.dram_tensor("scratch_v", (P, KD, 8 * P), F32, kind="Internal").ap()
    dt_loaded, b_loaded, act_sem, cos_sem = c.sem("sd_dt_loaded"), c.sem("sd_b_loaded"), c.sem("sd_act"), c.sem("sd_cos")
    trig, pw_ready = c.sem("sd_trig"), c.sem("sd_powers_ready")
    v_out = [c.sem(f"sd_v_out{i}") for i in range(2)]
    c.ut = c.buf("ut", [P, G, COLS], ctx=keep)
    flat = c.ut[:].rearrange("p g x -> p (g x)")
    n_pw, n_bbx = 2 * (L + 1) * A_COLS, G * 2 * CH
    c.pw = flat[:, 0:n_pw].rearrange("p (i e x) -> p i e x", i=2, e=L + 1)
    c.bbx = flat[:, n_pw:n_pw + n_bbx].rearrange("p (g x) -> p g x", g=G)
    c.bby = flat[:, n_pw + n_bbx:n_pw + n_bbx + G * CH].rearrange("p (g x) -> p g x", g=G)
    c.a1p = c.buf("a1p", [P, 3, GP], ctx=keep)
    c.a8p = c.buf("a8p", [P, 3, SUP, GP], ctx=keep)

    def parts(mine):
        def buf(name, shape, dt=F32):
            return c.buf("sd_" + name, shape, dt, ctx=mine)
        s1, s2, s3, s4 = (buf(f"s{i}", [P, A_COLS]) for i in range(4))
        ki, z, dt, f = buf("ki", [P, A_COLS], I32), buf("z", [P, 2, A_COLS]), buf("dt", [P, A_COLS]), buf("f", [P, 2, G])
        bx, by, tmp_p = buf("bx", [P, G, CH]), buf("by", [P, G, CH]), buf("tmp", [P, G, CH])
        q1, q2 = buf("q1", [P, GP]), buf("q2", [P, GP])
        v = buf("v", [P, 2, 8, L, CH])
        pw, al = c.pw, c.al

        def wide(x, n=G):
            return x.unsqueeze(2).to_broadcast([P, n, CH])

        def act_part(act):
            log_dt = dram["s5_log_dt"]
            act.dma_start(dt[:, 0:G], log_dt.to_broadcast([P, G])).then_inc(dt_loaded, 16)
            for i, name in enumerate(("s5_b_re", "s5_b_im")):
                bb = dram[name][0].rearrange("g n c -> n g c")
                act.dma_start(bx[i * NS:(i + 1) * NS], bb).then_inc(b_loaded, 16)
                act.dma_start(by[(1 - i) * NS:(2 - i) * NS], bb).then_inc(b_loaded, 16)
            act.wait_ge(dt_loaded, 16)
            for w in range(2):
                half = slice(w * NS, (w + 1) * NS)
                nc.scalar.activation(dt[half, G:], dt[half, 0:G].rearrange("p (q w) -> p w q", w=2)[:, w], ACT.Exp).then_inc(act_sem, 1)
            act.wait_ge(act_sem, 2)
            nc.scalar.activation(dt[:, 0:G], dt[:, 0:G], ACT.Exp).then_inc(act_sem, 1)
            act.wait_ge(trig, 1)
            nc.scalar.activation(s2[:], s2[:], ACT.Sin).then_inc(cos_sem, 1)
            act.wait_ge(trig, 2)
            nc.scalar.activation(s3[:], s3[:], ACT.Sin).then_inc(cos_sem, 1)

        def dve_part(dve):
            link = Chain(c, dve, "sd_link")
            ve = nc.vector
            dve.wait_ge(act_sem, 3)
            for i in range(2):
                link(ve.tensor_mul(z[:, i], al[:, i], dt[:]))
            for shift, out in ((0.0, s2), (0.25, s3)):
                link(ve.tensor_scalar(s1[:], z[:, 1], 1.0 / TWO_PI, shift, ALU.mult, ALU.add))
                link(ve.tensor_scalar(s1[:], s1[:], MAGIC, None, ALU.add))
                link(ve.tensor_scalar(s1[:], s1[:], -MAGIC, None, ALU.add))
                src = z[:, 1]
                for part in split(TWO_PI, 3):
                    link(ve.scalar_tensor_tensor(out[:], s1[:], -part, src, ALU.mult, ALU.add))
                    src = out[:]
                link(ve.tensor_scalar(out[:], out[:], shift * TWO_PI, float(np.float32(3.1415925)), ALU.add, ALU.min))
                ve.tensor_scalar(out[:], out[:], -float(np.float32(3.1415925)), None, ALU.max).then_inc(trig, 1)
                dve.wait_ge(trig, 1 if out is s2 else 2)
            link(ve.tensor_scalar(s1[:], z[:, 0], float(1.0 / np.log(2.0)), MAGIC, ALU.mult, ALU.add))
            link(ve.tensor_scalar(s1[:], s1[:], -MAGIC, None, ALU.add))
            link(ve.tensor_scalar(s1[:], s1[:], -126.0, 127.0, ALU.max, ALU.min))
            src = z[:, 0]
            for part in split(float(np.log(2.0)), 3):
                link(ve.scalar_tensor_tensor(s4[:], s1[:], -part, src, ALU.mult, ALU.add))
                src = s4[:]
            link(ve.tensor_scalar(ki[:], s1[:], 127.0, None, ALU.add))
            link(ve.tensor_scalar(ki[:], ki[:], 23, None, ALU.logical_shift_left))
            fact = [1.0]
            for i in range(1, 10):
                fact.append(fact[-1] * i)
            link(ve.tensor_scalar(s1[:], s4[:], 1.0 / fact[9], None, ALU.mult))
            for i in range(8, 0, -1):
                link(ve.scalar_tensor_tensor(s1[:], s1[:], 1.0 / fact[i], s4[:], ALU.add, ALU.mult))
            link(ve.tensor_scalar(s1[:], s1[:], 1.0, None, ALU.add))
            link(ve.tensor_mul(s1[:], s1[:], ki[:].bitcast(F32)))
            link(ve.memset(pw[:, 0, 0], 1.0))
            link(ve.memset(pw[:, 1, 0], 0.0))
            dve.wait_ge(cos_sem, 2)
            link(ve.tensor_mul(pw[:, 0, 1], s1[:], s3[:]))
            link(ve.tensor_mul(pw[:, 1, 1], s1[:], s2[:]))

            def power(out, x, y):
                w = out.shape[-1]
                link(ve.tensor_mul(s1[:, 0:w], x[:, 0], y[:, 0]))
                link(ve.tensor_mul(s4[:, 0:w], x[:, 1], y[:, 1]))
                link(ve.tensor_sub(out[:, 0], s1[:, 0:w], s4[:, 0:w]))
                link(ve.tensor_mul(s1[:, 0:w], x[:, 0], y[:, 1]))
                link(ve.tensor_mul(s4[:, 0:w], x[:, 1], y[:, 0]))
                link(ve.tensor_add(out[:, 1], s1[:, 0:w], s4[:, 0:w]))
            for e in range(2, L + 1):
                power(pw[:, :, e], pw[:, :, e - 1], pw[:, :, 1])
            x, y = al[:, 0, 0:G], al[:, 1, 0:G]
            n1, n2, den, t = s1[:, 0:G], s2[:, 0:G], s3[:, 0:G], s4[:, 0:G]
            link(ve.tensor_mul(den, x, x))
            link(ve.tensor_mul(t, y, y))
            link(ve.tensor_add(den, den, t))
            link(ve.reciprocal(den, den))
            link(ve.tensor_scalar(n1, pw[:, 0, 1, 0:G], -1.0, None, ALU.add))
            link(ve.tensor_mul(n2, n1, x))
            link(ve.tensor_mul(t, pw[:, 1, 1, 0:G], y))
            link(ve.tensor_add(n2, n2, t))
            link(ve.tensor_mul(f[:, 0], n2, den))
            link(ve.tensor_mul(n2, pw[:, 1, 1, 0:G], x))
            link(ve.tensor_mul(t, n1, y))
            link(ve.tensor_sub(n2, n2, t))
            link(ve.tensor_mul(f[:, 1], n2, den))
            dve.sem_inc(pw_ready, 1)

        def pool_part(pool):
            link = Chain(c, pool, "sd_pool_link")
            ve = nc.gpsimd
            link(ve.memset(c.bbx, 0.0))
            pool.wait_ge(b_loaded, 64)
            link(ve.tensor_scalar(by[:], by[:], c.sign[:, 0:1], -1.0, ALU.mult, ALU.mult))
            pool.wait_ge(pw_ready, 1)
            link(ve.tensor_mul(tmp_p[:], by[:], wide(f[:, 1])))
            link(ve.tensor_mul(c.bbx[:, :, 0:CH], bx[:], wide(f[:, 0])))
            link(ve.tensor_add(c.bbx[:, :, 0:CH], c.bbx[:, :, 0:CH], tmp_p[:]))
            link(ve.tensor_mul(tmp_p[:], bx[:], wide(f[:, 1])))
            link(ve.tensor_mul(c.bby, by[:], wide(f[:, 0])))
            link(ve.tensor_sub(c.bby, c.bby, tmp_p[:]))
            pair = slice(G, A_COLS)
            link(ve.tensor_copy(c.a1p[:, 0:2], pw[:, :, 1, pair]))
            link(ve.tensor_copy(c.a8p[:, 0:2, 0], pw[:, :, L, pair]))
            for j in range(1, SUP):
                x, y, out = c.a8p[:, 0:2, j - 1], c.a8p[:, 0:2, 0], c.a8p[:, 0:2, j]
                link(ve.tensor_mul(q1[:], x[:, 0], y[:, 0]))
                link(ve.tensor_mul(q2[:], x[:, 1], y[:, 1]))
                link(ve.tensor_sub(out[:, 0], q1[:], q2[:]))
                link(ve.tensor_mul(q1[:], x[:, 0], y[:, 1]))
                link(ve.tensor_mul(q2[:], x[:, 1], y[:, 0]))
                link(ve.tensor_add(out[:, 1], q1[:], q2[:]))
            link(ve.tensor_scalar(c.a1p[:, 2], c.a1p[:, 1], -1.0, None, ALU.mult))
            link(ve.tensor_scalar(c.a8p[:, 2], c.a8p[:, 1], -1.0, None, ALU.mult))
            for k in range(KD):
                gs, slot = slice(k * 8, k * 8 + 8), v[:, k % 2]
                if k >= 2:
                    pool.wait_ge(v_out[k % 2], 16 * (k // 2))
                link(ve.tensor_copy(slot[:, :, 0, :], c.bbx[:, gs, 0:CH]))
                for e in range(1, L):
                    link(ve.tensor_mul(slot[:, :, e, :], c.bbx[:, gs, 0:CH], wide(pw[:, 0, e, gs], 8)))
                    link(ve.tensor_mul(tmp_p[:, 0:8], c.bby[:, gs], wide(pw[:, 1, e, gs], 8)))
                    link(ve.tensor_add(slot[:, :, e, :], slot[:, :, e, :], tmp_p[:, 0:8]))
                pool.dma_start(c.scratch_v[:, k], slot.rearrange("p g e c -> p (g e c)")).then_inc(v_out[k % 2], 16)
            for i in range(2):
                pool.wait_ge(v_out[i], 16 * KD // 2)

        return act_part, dve_part, pool_part
    return parts


def stage_ssm_tables(c, norm):
    nc, ps = c.nc, c.psum
    dram = c.dram
    loaded, c_turned, c_kept = c.sem("st_loaded"), c.sem("st_c_turned"), c.sem("st_c_kept")
    v_kept = c.sem("st_v_kept")
    m_ready, k_done, k_kept, k_written = c.sem("st_m_ready"), c.sem("st_k_done"), c.sem("st_k_kept"), c.sem("st_k_written")
    cleared, laid, sent = c.sem("st_x_cleared"), c.sem("st_x_laid"), c.sem("st_x_sent")
    v_in, v_turned, zeroed = [c.sem(f"st_v_in{k}") for k in range(KD)], c.sem("st_v_turned"), c.sem("st_zeroed")
    with ExitStack() as mine:
        def buf(name, shape):
            return c.buf("st_" + name, shape, ctx=mine)
        crow = buf("c_rows", [P, KD, 2, 2, NS])
        cx, cy = buf("cx", [P, G, CH]), buf("cy", [P, G, CH])
        bbx, pw = c.bbx, c.pw
        tmp = buf("tmp", [P, G, CH])
        xc = buf("xc", [P, L, KD, COLS])
        kz = buf("kz", [P, G // 4, (2 * L - 1) * CH])
        tmp_p = c.y[:, 5:7].rearrange("p k t -> p (k t)")[:, 0:G * CH].rearrange("p (g c) -> p g c", c=CH)

        def wide(x, n=G):
            return x.unsqueeze(2).to_broadcast([P, n, CH])

        with nc.Block() as block:
            @block.sync
            def _(sp):
                for i, name in enumerate(("s5_c_re", "s5_c_im")):
                    cc = dram[name][0].rearrange("(k g) c n -> (g c) k n", k=KD)
                    sp.dma_start(crow[:, :, 0, i], cc).then_inc(loaded, 16)
                    sp.dma_start(crow[:, :, 1, 1 - i], cc).then_inc(loaded, 16)
                for k in range(KD):
                    sp.dma_start(c.wb[:, k * 8:(k + 1) * 8].rearrange("p g x -> p (g x)"), c.scratch_v[:, k]).then_inc(v_in[k], 16)
                for e in range(L):
                    sp.wait_ge(laid, e + 3)
                    sp.dma_start(c.scratch_u[:, e], xc[:, e].rearrange("p k x -> p (k x)")).then_inc(sent, 16)
                sp.wait_ge(sent, 16 * L)
                sp.wait_ge(k_kept, 4)
                for q in range(4):
                    sp.dma_start(c.scratch_k.rearrange("(j q) c x -> q c j x", q=4)[q], kz[32 * q:32 * q + CH]).then_inc(k_written, 16)
                sp.wait_ge(k_written, 64)

            @block.scalar
            def _(act):
                norm[0](act)
                act.wait_ge(norm[3], KD)
                act.wait_ge(cleared, 1)
                nc.scalar.copy(xc[:, L - 1, :, NCH:NCH + NB], c.xT[:, :, SEQ:T]).then_inc(laid, 1)
                nc.scalar.copy(xc[:, 0, :, NCH + NB:], c.xT[:, :, SEQ:T]).then_inc(laid, 1)
                for e in range(L):
                    nc.scalar.copy(xc[:, e, :, 0:NCH], c.xT[:, :, 0:SEQ].rearrange("p k (n t) -> p t k n", t=L)[:, L - 1 - e]).then_inc(laid, 1)
                for n in range(2 * KD):
                    act.wait_ge(v_turned, n + 1)
                    nc.scalar.copy(c.wb[:, n * 4:n * 4 + 4, :], ps[:, 5 + n % 2, :].rearrange("p (g x) -> p g x", g=4)).then_inc(v_kept, 1)

            def make_m(ve, link, g0, g1, t):
                gs, n = slice(g0, g1), g1 - g0
                link(ve.tensor_copy(c.mx[:, gs, 0, :], cx[:, gs]))
                for e in range(1, L + 1):
                    link(ve.tensor_mul(c.mx[:, gs, e, :], cx[:, gs], wide(pw[:, 0, e, gs], n)))
                    link(ve.tensor_mul(t[:, gs], cy[:, gs], wide(pw[:, 1, e, gs], n)))
                    link(ve.tensor_add(c.mx[:, gs, e, :], c.mx[:, gs, e, :], t[:, gs]))

            @block.gpsimd
            def _(pool):
                link = Chain(c, pool, "st_pool_link")
                nc.gpsimd.memset(xc[:, :, :, NCH:], 0.0).then_inc(cleared, 1)
                nc.gpsimd.memset(kz[:], 0.0).then_inc(zeroed, 1)
                pool.wait_ge(norm[3], KD)
                pool.wait_ge(c_kept, 4)
                make_m(nc.gpsimd, link, DVE_GROUPS, G, tmp_p)
                pool.sem_inc(m_ready, 1)

            @block.tensor
            def _(pe):
                pe.wait_ge(loaded, 16 * 4)
                for w in range(2):
                    for k in range(KD):
                        mm = nc.tensor.transpose(ps[:, C_BANKS[w * 2 + k // 4], k % 4 * P:(k % 4 + 1) * P],
                                                 crow[:, k, w].rearrange("p i n -> p (i n)"), c.ident[:])
                    mm.then_inc(c_turned, 1)
                norm[1](pe)
                for n in range(2 * KD):
                    if n % 2 == 0:
                        pe.wait_ge(v_in[n // 2], 16)
                    if n >= 2:
                        pe.wait_ge(v_kept, n - 1)
                    for j in range(4):
                        mm = nc.tensor.transpose(ps[:, 5 + n % 2, j * P:(j + 1) * P], c.wb[:, n * 4 + j, :], c.ident[:])
                    mm.then_inc(v_turned, 1)
                pe.wait_ge(norm[3], KD)
                pe.wait_ge(m_ready, 2)
                pe.wait_ge(c_kept, 4)
                for g in range(G):
                    q, j = g % 4, g // 4
                    mm = nc.tensor.matmul(ps[32 * q:32 * q + 32, j // 4, j % 4 * P:(j % 4 + 1) * P], bbx[:, g],
                                          c.mx[:, g, 0:L].rearrange("p e c -> p (e c)"), start=True, stop=True)
                    if g % 16 == 15:
                        mm.then_inc(k_done, 1)

            @block.vector
            def _(dve):
                link = Chain(c, dve, "st_link")
                ve = nc.vector
                norm[2](dve)
                for w in range(2):
                    dve.wait_ge(c_turned, w + 1)
                    for h in range(2):
                        dst, bank = (cx, cy)[w][:, h * 32:(h + 1) * 32], ps[:, C_BANKS[w * 2 + h], :].rearrange("p (g c) -> p g c", c=CH)
                        if w == 0:
                            ve.tensor_scalar(dst, bank, c.sign[:, 0:1], None, ALU.mult).then_inc(c_kept, 1)
                        else:
                            ve.tensor_scalar(dst, bank, -1.0, None, ALU.mult).then_inc(c_kept, 1)
                dve.wait_ge(c_kept, 4)
                make_m(ve, link, 0, DVE_GROUPS, tmp)
                dve.sem_inc(m_ready, 1)
                dve.wait_ge(zeroed, 1)
                for j in range(4):
                    dve.wait_ge(k_done, j + 1)
                    for q in range(4):
                        ins = ve.tensor_copy(kz[32 * q:32 * q + CH, 4 * j:4 * j + 4, (L - 1) * CH:],
                                             ps[32 * q:32 * q + CH, j, :].rearrange("p (g x) -> p g x", g=4))
                    ins.then_inc(k_kept, 1)


def stage_ssm(c):
    nc, ps = c.nc, c.psum
    dram = c.dram
    back, im_kept = c.sem("ss_u_back"), c.sem("ss_x_im_kept")
    xd, xk = c.sem("ss_x_done"), c.sem("ss_x_kept")
    t_in = c.sem("ss_t_in")
    s_in, s_turned, s_kept = c.sem("ss_state_in"), c.sem("ss_state_turned"), c.sem("ss_state_kept")
    with ExitStack() as mine:
        def buf(name, shape, ctx=mine):
            return c.buf("ss_" + name, shape, ctx=ctx)
        ut = c.ut
        x = buf("x", [P, 2, GP, COLS])
        h0 = buf("h0", [P, 2, GP, NB])
        with ExitStack() as here:
            srow = buf("state_rows", [GP, 2 * NB, P], here)
            with nc.Block() as block:
                @block.vector
                def _(dve):
                    dve.wait_ge(s_turned, 1)
                    nc.vector.tensor_copy(h0[:], ps[:, 7, :].rearrange("p (b i q) -> p i q b", i=2, q=GP)).then_inc(s_kept, 1)
                    for k in range(KD):
                        for par in range(2):
                            dve.wait_ge(xd, k + 1)
                            src = ps[0:NS, k % 3 * 2:k % 3 * 2 + 2, 0:4 * COLS].rearrange("p b (q w x) -> p b q w x", q=2, w=2)
                            for b in range(2):
                                ins = nc.vector.tensor_copy(x[par * NS:(par + 1) * NS, 0, k * 4 + b * 2:k * 4 + b * 2 + 2, :], src[:, b, :, par, :])
                        ins.then_inc(xk, 1)

                @block.scalar
                def _(act):
                    for k in range(KD):
                        for par in range(2):
                            act.wait_ge(xk, k + 1)
                            src = ps[NS:P, k % 3 * 2:k % 3 * 2 + 2, 0:4 * COLS].rearrange("p b (q w x) -> p b q w x", q=2, w=2)
                            for b in range(2):
                                ins = nc.scalar.copy(x[par * NS:(par + 1) * NS, 1, k * 4 + b * 2:k * 4 + b * 2 + 2, :], src[:, b, :, par, :])
                        ins.then_inc(im_kept, 1)

                @block.sync
                def _(sp):
                    sp.dma_start(srow[:], dram["state_ssm"][0].rearrange("b i (q w) n -> q (b i) (w n)", w=2)).then_inc(s_in, 16)
                    for e in range(L):
                        sp.dma_start(ut[e * CH:(e + 1) * CH].rearrange("p (g k) x -> p g (k x)", k=KD),
                                     c.scratch_u.rearrange("(g c) e x -> e c g x", c=CH)[e]).then_inc(back, 16)

                @block.tensor
                def _(pe):
                    pe.wait_ge(s_in, 16)
                    for i in range(2 * NB):
                        mm = nc.tensor.transpose(ps[:, 7, i * GP:(i + 1) * GP], srow[:, i, :], c.ident[0:GP, 0:GP])
                    mm.then_inc(s_turned, 1)
                    pe.wait_ge(back, 16 * L)
                    for k in range(KD):
                        if k >= 3:
                            pe.wait_ge(im_kept, k - 2)
                        for g in range(8):
                            mm = nc.tensor.matmul(ps[:, k % 3 * 2 + g // 4, g % 4 * COLS:(g % 4 + 1) * COLS],
                                                  c.wb[:, k * 8 + g, :], ut[:, g * KD + k, :], start=True, stop=True)
                        mm.then_inc(xd, 1)

        with ExitStack() as here:
            ta, tb = buf("ta", [P, 2, GP, SUP], here), buf("tb", [P, 2, GP, SUP], here)
            with nc.Block() as block:
                def carry(eng, ve, link, q0, q1):
                    qs = slice(q0, q1)
                    xs = x[:, :, qs, 0:NCH].rearrange("p i q (s j) -> p i q s j", j=SUP)

                    def axpy(out, src, table, w):
                        complex_axpy(ve, link, out, src, table, ta[:, :, qs, 0:w], tb[:, :, qs, 0:w])
                    for j in range(1, SUP):
                        axpy(xs[:, :, :, :, j], xs[:, :, :, :, j - 1], c.a8p[:, :, 0, qs], SUP)
                    for s in range(1, SUP):
                        axpy(xs[:, :, :, s:s + 1, SUP - 1], xs[:, :, :, s - 1:s, SUP - 1], c.a8p[:, :, SUP - 1, qs], 1)
                    for j in range(SUP - 1):
                        axpy(xs[:, :, :, 1:, j], xs[:, :, :, 0:SUP - 1, SUP - 1], c.a8p[:, :, j, qs], SUP - 1)
                    axpy(x[:, :, qs, NCH + NB:], h0[:, :, qs], c.a1p[:, :, qs], NB)

                @block.vector
                def _(dve):
                    carry(dve, nc.vector, Chain(c, dve, "ss_link"), 0, DVE_PAIRS)

                @block.gpsimd
                def _(pool):
                    carry(pool, nc.gpsimd, Chain(c, pool, "ss_pool_link"), DVE_PAIRS, GP)

                @block.sync
                def _(sp):
                    for e in range(L):
                        sp.dma_start(c.wb[e * CH:(e + 1) * CH], c.scratch_k[:, :, e * CH:e * CH + P].rearrange("g c x -> c g x")).then_inc(t_in, 16)

        hx_done, y_done, y_kept, y_sent = c.sem("ss_hx_done"), c.sem("ss_y_done"), c.sem("ss_y_kept"), c.sem("ss_y_sent")
        y_back, skipped, st_done = [c.sem(f"ss_y_back{i}") for i in range(2)], c.sem("ss_skipped"), c.sem("ss_st_done")
        st_kept, st_out, zeroed, hi_done = c.sem("ss_st_kept"), c.sem("ss_st_out"), c.sem("ss_zeroed"), c.sem("ss_hx_im_done")
        with ExitStack() as here:
            hx = buf("hx", [P, 2, 8, HCOLS], here)
            yt = buf("yt", [P, 2, 8, 2, HCOLS], here)
            yc = buf("yc", [P, 2, L, 2, HCOLS], here)
            orow = buf("out_rows", [GP, 2 * NB + 2, P], here)
            with nc.Block() as block:
                @block.sync
                def _(sp):
                    for j in range(KD // 2):
                        sp.wait_ge(y_kept, 4 * (j + 1))
                        for t in range(L):
                            sp.dma_start(c.scratch_y[j].rearrange("g c t x -> t c g x")[t],
                                         yt[t * CH:(t + 1) * CH, j % 2].rearrange("p g k x -> p g (k x)")).then_inc(y_sent, 16)
                        sp.wait_ge(y_sent, 16 * L * (j + 1))
                        if j >= 2:
                            sp.wait_ge(skipped, 2 * (j - 1))
                        sp.dma_start(yc[:, j % 2].rearrange("p t k x -> p t (k x)"),
                                     c.scratch_y[j].rearrange("g c t x -> (g c) t x")).then_inc(y_back[j % 2], 16)
                    sp.wait_ge(st_kept, 5)
                    sp.dma_start(dram["ssm_sample"][0].rearrange("b i (q w) n -> q (b i) (w n)", w=2), orow[:, 0:2 * NB]).then_inc(st_out, 16)
                    sp.dma_start(dram["ssm_prompt"][0, 0].rearrange("i (q w) n -> q i (w n)", w=2), orow[:, 2 * NB:]).then_inc(st_out, 16)
                    sp.wait_ge(st_out, 32)

                @block.vector
                def _(dve):
                    nc.vector.memset(hx[:], 0.0).then_inc(zeroed, 1)
                    dve.wait_ge(zeroed, 1)

                    def skip(k):
                        dve.wait_ge(y_back[k // 2 % 2], 16 * (k // 4 + 1))
                        col = c.cols[:, k:k + 1]
                        nc.vector.scalar_tensor_tensor(c.y[:, k, 0:SEQ].rearrange("p (n t) -> p t n", t=L),
                                                       c.xT[:, k, 0:SEQ].rearrange("p (n t) -> p t n", t=L), col,
                                                       yc[:, k // 2 % 2, :, k % 2, 0:NCH], ALU.mult, ALU.add)
                        nc.vector.scalar_tensor_tensor(c.y[:, k, SEQ:T], c.xT[:, k, SEQ:T], col, yc[:, k // 2 % 2, 0, k % 2, NCH:],
                                                       ALU.mult, ALU.add).then_inc(skipped, 1)

                    for k in range(KD):
                        if k >= 2:
                            dve.wait_ge(y_done, 2 * (k - 1))
                        for i in range(2):
                            for par in range(2):
                                rows = slice(par * NS, (par + 1) * NS)
                                dst = hx[i * NS:(i + 1) * NS, k % 2].rearrange("p (q w) x -> p w q x", w=2)[:, par]
                                nc.vector.tensor_copy(dst[:, :, 1:NCH], x[rows, i, k * 4:k * 4 + 4, 0:NCH - 1])
                                ins = nc.vector.tensor_copy(dst[:, :, NCH:], h0[rows, i, k * 4:k * 4 + 4, :])
                        ins.then_inc(hx_done, 1)
                        if k >= 4:
                            skip(k - 4)
                    for k in range(KD - 4, KD):
                        skip(k)
                    for n in range(5):
                        dve.wait_ge(st_done, n + 1)
                        w = 4 if n < 4 else 2
                        nc.vector.tensor_copy(orow[:, 4 * n:4 * n + w, :], ps[0:GP, 4 + n % 2, 0:w * P].rearrange("p (j x) -> p j x", x=P)).then_inc(st_kept, 1)

                @block.scalar
                def _(act):
                    for k in range(KD):
                        if k >= 4:
                            act.wait_ge(y_sent, 16 * L * (k // 2 - 1))
                        for h in range(2):
                            act.wait_ge(y_done, 2 * k + h + 1)
                            nc.scalar.copy(yt[:, k // 2 % 2, h * 4:h * 4 + 4, k % 2, :],
                                           ps[:, k % 2 * 2 + h, 0:4 * HCOLS].rearrange("p (g x) -> p g x", g=4)).then_inc(y_kept, 1)

                @block.tensor
                def _(pe):
                    for k in range(KD):
                        if k == 0:
                            pe.wait_ge(t_in, 16 * L)
                        pe.wait_ge(hx_done, k + 1)
                        if k >= 2:
                            pe.wait_ge(y_kept, 2 * (k - 1))
                        for g in range(8):
                            out = ps[:, k % 2 * 2 + g // 4, g % 4 * HCOLS:(g % 4 + 1) * HCOLS]
                            nc.tensor.matmul(out, c.wb[:, k * 8 + g, :], ut[:, g * KD + k, 0:HCOLS], start=True, stop=False)
                            mm = nc.tensor.matmul(out, c.mx[:, k * 8 + g, 1:].rearrange("p e c -> p (e c)"), hx[:, k % 2, g, :],
                                                  start=False, stop=True)
                            if g % 4 == 3:
                                mm.then_inc(y_done, 1)
                    for n in range(5):
                        if n >= 2:
                            pe.wait_ge(st_kept, n - 1)
                        for j in range(4 if n < 4 else 2):
                            if n < 4:
                                b, i = divmod(n * 4 + j, 2)
                                src = x[:, i, :, NCH + NB + b]
                            else:
                                src = x[:, j, :, NCH - 1]
                            mm = nc.tensor.transpose(ps[0:GP, 4 + n % 2, j * P:(j + 1) * P], src, c.ident[:])
                        mm.then_inc(st_done, 1)


def gelu_parts(c, y):
    nc = c.nc
    done = c.sem("gelu_done")

    def act_part(act):
        for k in range(KD):
            nc.scalar.activation(y[:, k, :], y[:, k, :], ACT.Gelu_apprx_tanh).then_inc(done, 1)

    def nothing(eng):
        pass
    return act_part, nothing, nothing, done


def evac_glu(dst, y, bias):
    def make(c, name, filled, freed, per, iters, mine):
        nc, ps = c.nc, c.psum
        gated = c.sem(f"{name}_gated")
        tmp = c.buf(f"{name}_sig", [P, 4, HALF], ctx=mine)

        def act_prog(act):
            act.sem_inc(gated, 4)
            with act.Fori(0, iters) as it:
                for b in range(8 * per):
                    act.wait_ge(filled, it * (8 * per) + b + 1)
                    act.wait_ge(gated, it * (8 * per) + b + 1)
                    nc.scalar.activation(tmp[:, b % 4, :], ps[:, b % 8, 0:HALF], ACT.Sigmoid,
                                         bias=bias[:, bass.ds(it * (4 * per) + b // 2, 1)]).then_inc(freed[b % 2], 1)

        def dve_prog(dve):
            with dve.Fori(0, iters) as it:
                for b in range(8 * per):
                    m, h = b // 2, b % 2
                    dve.wait_ge(freed[h], it * (4 * per) + m + 5)
                    tile, cols = bass.ds(it * (4 * per) + m, 1), slice(h * HALF, (h + 1) * HALF)
                    nc.vector.tensor_mul(dst[:, tile, cols], y[:, tile, cols], tmp[:, b % 4:b % 4 + 1, :]).then_inc(gated, 1)
        return act_prog, dve_prog, [gated]
    return make


def stage_s5(c):
    nc = c.nc
    c.scratch_k = nc.dram_tensor("scratch_k", (G, CH, (2 * L - 1) * CH), F32, kind="Internal").ap()
    c.scratch_u = nc.dram_tensor("scratch_u", (P, L, KD * COLS), F32, kind="Internal").ap()
    c.scratch_y = nc.dram_tensor("scratch_y", (KD // 2, 8, CH, L, 2 * HCOLS), F32, kind="Internal").ap()
    with ExitStack() as tables:
        c.wb = c.buf("wb", [P, G, P], ctx=tables)
        c.mx = c.buf("mx", [P, G, L + 1, CH], ctx=tables)
        stage_ssm_tables(c, norm_parts(c, "ssm_in", c.hT, c.xT, 1, 0, c.y[:, 0:4], c.y[:, 4]))
        stage_ssm(c)


def program(nc, dram):
    with ExitStack() as ctx:
        c = Core(nc, ctx, dram)
        c.ident = c.buf("ident", [P, P])
        c.causal = c.buf("causal", [P, SEQ])
        c.cmask = c.buf("cmask", [P, 2 * GRP * QT * NCP])
        c.own = c.buf("own", [P, NB])
        c.group = c.buf("group", [P, P])
        c.over = c.buf("over", [P, NSEL])
        c.blk = c.buf("blk", [P, NSEL])
        c.sign = c.buf("sign", [P, 1])
        c.al = c.buf("al", [P, 2, G + GP])
        c.cols = c.buf("cols", [P, 2 * KD])
        c.g_cols = c.buf("g_cols", [P, 8 * KD])
        c.ones = c.buf("ones", [P, P])
        c.eps = c.buf("eps", [P, 1])
        c.hT = c.buf("hT", [P, KD, T])
        c.xT = c.buf("xT", [P, KD, T])
        c.pages = c.buf("pages", [1, NB * NPAGE], I32)
        with c.part():
            stage_inputs(c)
        with c.part():
            stage_nsa(c)
        keep = ctx.enter_context(ExitStack())
        with c.part():
            side = ssm_side(c, keep)
            with ExitStack() as mine:
                c.w = c.buf("w0", [P, 2, CK, NG], ctx=mine)
                out = Linear(c, "nsa_o", columns(c.dram["nsa_w_o"][0]), KD, D // NG, 2)
                up = mlp_up(c, 0)
                with ExitStack() as here:
                    y = c.buf("nsa_y", [P, KD, T], ctx=here)
                    stage_mix_out(c, out, c.oT, evac_copy(y), y, 0, up)
                stage_mlp(c, 0, up, side)
        c.y = c.buf("ssm_y", [P, KD, T], ctx=keep)
        with c.part():
            stage_s5(c)
        with c.part(), ExitStack() as mine:
            c.w = c.buf("w1", [P, 2, CK, NG], ctx=mine)
            glu = Linear(c, "glu", columns(c.dram["s5_w_glu"][0]), KD, D // NG, 2)
            up = mlp_up(c, 1)
            stage_mix_out(c, glu, c.y, evac_glu(c.xT, c.y, c.cols[:, KD:]), c.xT, 1, up, gelu_parts(c, c.y))
            stage_mlp(c, 1, up)
            stage_outputs(c)


OUTPUTS = [
    ("y_prompt", (1, SEQ, D)), ("y_sample", (NB, 1, D)),
    ("kv_cmp_prompt", (1, 1, SEQ, 2, NKV, HD)), ("kv_cmp_sample", (1, NB, 1, 2, NKV, HD)),
    ("kv_sel_prompt", (1, 1, SEQ, 2, NKV, HD)), ("kv_sel_sample", (1, NB, 1, 2, NKV, HD)),
    ("kv_win_prompt", (1, 1, WIN, 2, NKV, HD)), ("kv_win_sample", (1, NB, WIN, 2, NKV, HD)),
    ("ssm_prompt", (1, 1, 2, G, NS)), ("ssm_sample", (1, NB, 2, G, NS)),
]


def kernel(**inputs):
    import concourse.bacc as bacc
    from concourse.bass_utils import run_bass_kernel_spmd

    nc = bacc.Bacc("TRN2", target_bir_lowering=False, num_devices=1)
    arrays, dram = {}, {}
    for name, value in [*inputs.items(), *constants().items()]:
        a = np.ascontiguousarray(value)
        arrays[f"in_{name}"] = a
        dram[name] = nc.dram_tensor(f"in_{name}", a.shape, mybir.dt.from_np(a.dtype), kind="ExternalInput").ap()
    for name, shape in OUTPUTS:
        dram[name] = nc.dram_tensor(f"out_{name}", shape, F32, kind="ExternalOutput").ap()
    program(nc, dram)
    r = run_bass_kernel_spmd(nc, [arrays], core_ids=[0])
    return tuple(r.results[0][f"out_{name}"] for name, _ in OUTPUTS)
```
